# Optimizing a Trainium2 kernel written in Bass

```python
import jax
import jax.numpy as jnp
from jax import lax
import numpy as np

D_MODEL = 1024
BATCH = 1
SEQ = 256
DEPTH = 2

ROPE_THETA = 10000.0

MLA_HEADS = 8
MLA_NOPE_DIM = 64
MLA_ROPE_DIM = 32
MLA_V_DIM = 64
MLA_Q_RANK = 768
MLA_KV_RANK = 256
Q_BLOCK = 128

NSA_HEADS = 8
NSA_GROUPS = 2
NSA_HEADS_PER_GROUP = NSA_HEADS // NSA_GROUPS
NSA_HEAD_DIM = 64
CMP_BLOCK = 32
CMP_STRIDE = 16
CMP_HIDDEN = 2 * NSA_HEAD_DIM
SEL_BLOCK = 64
SEL_TOPN = 16
WINDOW = 512
NSA_Q_CHUNK = 64
FORCE_SCORE = 1e9

PEER_HEADS = 8
PEER_KEY_DIM = 128
PEER_N_KEYS = 128
PEER_N_EXPERTS = PEER_N_KEYS * PEER_N_KEYS
PEER_TOPK = 16
PEER_TOKEN_CHUNK = 128

DEEPNORM_ALPHA = (2 * DEPTH) ** 0.25
DEEPNORM_BETA = (8 * DEPTH) ** -0.25
LN_EPS = 1e-5
RMS_EPS = 1e-6
NEG_BIG = -1e30

MLA_MIX = MLA_HEADS * MLA_V_DIM
NSA_MIX = NSA_HEADS * NSA_HEAD_DIM
IN_WIDTHS = (MLA_Q_RANK, MLA_KV_RANK, MLA_ROPE_DIM, NSA_MIX,
             6 * NSA_GROUPS * NSA_HEAD_DIM, 3 * NSA_HEADS, 2 * D_MODEL)
IN_WIDTH = sum(IN_WIDTHS)

kernel_name = "hybrid_mla_nsa_peer_deepnorm"

def layer_norm(x, g, b):
    xf = x.astype(jnp.float32)
    mu = jnp.mean(xf, axis=-1, keepdims=True)
    var = jnp.mean(jnp.square(xf - mu), axis=-1, keepdims=True)
    y = (xf - mu) * lax.rsqrt(var + LN_EPS)
    return (y * g.astype(jnp.float32) + b.astype(jnp.float32)).astype(x.dtype)

def rms_norm(x, g):
    xf = x.astype(jnp.float32)
    y = xf * lax.rsqrt(jnp.mean(jnp.square(xf), axis=-1, keepdims=True) + RMS_EPS)
    return (y * g.astype(jnp.float32)).astype(x.dtype)

def rope_angles(positions, dim):
    inv_freq = ROPE_THETA ** (-jnp.arange(0, dim, 2, dtype=jnp.float32) / dim)
    ang = positions.astype(jnp.float32)[..., None] * inv_freq
    return jnp.cos(ang), jnp.sin(ang)

def apply_rope(x, cos, sin):
    half = x.shape[-1] // 2
    c = cos[:, :, None, :].astype(x.dtype)
    s = sin[:, :, None, :].astype(x.dtype)
    x1, x2 = x[..., :half], x[..., half:]
    return jnp.concatenate([x1 * c - x2 * s, x1 * s + x2 * c], axis=-1)

def masked_softmax(s, mask):
    p = jax.nn.softmax(jnp.where(mask, s, NEG_BIG), axis=-1)
    return jnp.where(mask, p, 0.0)

def mla_attention(q_nope, q_rope, k_nope, k_rope, v):
    B, S, H, _ = q_nope.shape
    dv = v.shape[-1]
    scale = (MLA_NOPE_DIM + MLA_ROPE_DIM) ** -0.5
    kpos = jnp.arange(S)

    def block(i):
        q0 = i * Q_BLOCK
        qn = lax.dynamic_slice_in_dim(q_nope, q0, Q_BLOCK, axis=1)
        qr = lax.dynamic_slice_in_dim(q_rope, q0, Q_BLOCK, axis=1)
        s = (jnp.einsum('bqhd,bkhd->bhqk', qn, k_nope).astype(jnp.float32)
             + jnp.einsum('bqhd,bkd->bhqk', qr, k_rope).astype(jnp.float32)) * scale
        qpos = q0 + jnp.arange(Q_BLOCK)
        p = masked_softmax(s, kpos[None, :] <= qpos[:, None])
        return jnp.einsum('bhqk,bkhd->bqhd', p.astype(v.dtype), v)

    out = lax.map(block, jnp.arange(S // Q_BLOCK))
    return jnp.moveaxis(out, 0, 1).reshape(B, S, H * dv)

def compress_blocks(k, pe, w1, w2):
    B, S, G, dk = k.shape
    n_cmp = (S - CMP_BLOCK) // CMP_STRIDE + 1
    idx = jnp.arange(n_cmp)[:, None] * CMP_STRIDE + jnp.arange(CMP_BLOCK)[None, :]
    blocks = k[:, idx] + pe[None, None, :, None, :]
    blocks = blocks.transpose(0, 1, 3, 2, 4).reshape(B, n_cmp, G, CMP_BLOCK * dk)
    hid = jax.nn.gelu(blocks @ w1, approximate=False)
    return hid @ w2

def nsa_attention(q, kc, vc, k_sel, v_sel, k_win, v_win, gates):
    B, S, H, dk = q.shape
    G, R, C = NSA_GROUPS, NSA_HEADS_PER_GROUP, NSA_Q_CHUNK
    scale = dk ** -0.5
    qg = q.reshape(B, S, G, R, dk)
    gg = gates.reshape(B, S, G, R, 3)
    n_cmp = kc.shape[1]
    n_sel = S // SEL_BLOCK
    top_n = min(SEL_TOPN, n_sel)

    cmp_lo = jnp.arange(n_cmp) * CMP_STRIDE
    cmp_end = cmp_lo + CMP_BLOCK - 1
    sel_lo = jnp.arange(n_sel) * SEL_BLOCK
    overlap = ((cmp_lo[:, None] <= sel_lo[None, :] + SEL_BLOCK - 1)
               & (cmp_end[:, None] >= sel_lo[None, :])).astype(jnp.float32)

    kb = k_sel.reshape(B, n_sel, SEL_BLOCK, G, dk).transpose(0, 3, 1, 2, 4)
    vb = v_sel.reshape(B, n_sel, SEL_BLOCK, G, dk).transpose(0, 3, 1, 2, 4)
    kw_pad = jnp.pad(k_win, ((0, 0), (WINDOW, 0), (0, 0), (0, 0)))
    vw_pad = jnp.pad(v_win, ((0, 0), (WINDOW, 0), (0, 0), (0, 0)))
    b_ix = jnp.arange(B)[:, None, None, None]
    g_ix = jnp.arange(G)[None, :, None, None]
    blk = jnp.arange(n_sel)

    def chunk(i):
        q0 = i * C
        qc = lax.dynamic_slice_in_dim(qg, q0, C, axis=1)
        gc = lax.dynamic_slice_in_dim(gg, q0, C, axis=1)
        t = q0 + jnp.arange(C)

        s_c = jnp.einsum('bcgrd,bngd->bgrcn', qc, kc).astype(jnp.float32) * scale
        p_c = masked_softmax(s_c, cmp_end[None, :] <= t[:, None])
        o_c = jnp.einsum('bgrcn,bngd->bcgrd', p_c.astype(qc.dtype), vc)

        imp = jnp.einsum('bgrcn,nj->bgcj', p_c, overlap)
        cur = t // SEL_BLOCK
        forced = (blk[None, :] == 0) | (blk[None, :] == cur[:, None]) | (blk[None, :] == cur[:, None] - 1)
        future = blk[None, :] > cur[:, None]
        imp = jnp.where(forced, FORCE_SCORE, jnp.where(future, -FORCE_SCORE, imp))
        _, idx = lax.top_k(imp, top_n)

        kg = kb[b_ix, g_ix, idx]
        vg = vb[b_ix, g_ix, idx]
        tok = idx[..., None] * SEL_BLOCK + jnp.arange(SEL_BLOCK)
        mask_s = (tok <= t[None, None, :, None, None]).reshape(B, G, 1, C, top_n * SEL_BLOCK)
        s_s = jnp.einsum('bcgrd,bgcnld->bgrcnl', qc, kg).astype(jnp.float32) * scale
        p_s = masked_softmax(s_s.reshape(B, G, R, C, top_n * SEL_BLOCK), mask_s)
        p_s = p_s.reshape(B, G, R, C, top_n, SEL_BLOCK)
        o_s = jnp.einsum('bgrcnl,bgcnld->bcgrd', p_s.astype(qc.dtype), vg)

        kw = lax.dynamic_slice_in_dim(kw_pad, q0, C + WINDOW, axis=1)
        vw = lax.dynamic_slice_in_dim(vw_pad, q0, C + WINDOW, axis=1)
        kpos = q0 - WINDOW + jnp.arange(C + WINDOW)
        mask_w = ((kpos[None, :] <= t[:, None]) & (kpos[None, :] > t[:, None] - WINDOW)
                  & (kpos[None, :] >= 0))
        s_w = jnp.einsum('bcgrd,bkgd->bgrck', qc, kw).astype(jnp.float32) * scale
        p_w = masked_softmax(s_w, mask_w)
        o_w = jnp.einsum('bgrck,bkgd->bcgrd', p_w.astype(qc.dtype), vw)

        return gc[..., 0:1] * o_c + gc[..., 1:2] * o_s + gc[..., 2:3] * o_w

    out = lax.map(chunk, jnp.arange(S // C))
    return jnp.moveaxis(out, 0, 1).reshape(B, S, H * dk)

def peer(x, w_query, sub_keys, expert_u, expert_v):
    B, S, D = x.shape
    T = B * S
    H, K = PEER_HEADS, PEER_TOPK
    xt = x.reshape(T, D)
    q = (xt @ w_query).reshape(T, H, 2, PEER_KEY_DIM // 2)
    s = jnp.einsum('thpd,hpnd->thpn', q, sub_keys).astype(jnp.float32)
    sv, si = lax.top_k(s, K)
    cand = (sv[:, :, 0, :, None] + sv[:, :, 1, None, :]).reshape(T, H, K * K)
    cidx = (si[:, :, 0, :, None] * PEER_N_KEYS + si[:, :, 1, None, :]).reshape(T, H, K * K)
    best, pos = lax.top_k(cand, K)
    eidx = jnp.take_along_axis(cidx, pos, axis=-1)
    gate = jax.nn.softmax(best, axis=-1).astype(x.dtype)
    n_chunks = T // PEER_TOKEN_CHUNK

    def chunk(args):
        xc, ec, gc = args
        a = jnp.einsum('chkd,cd->chk', expert_u[ec], xc)
        w = gc * jax.nn.gelu(a, approximate=False)
        return jnp.einsum('chk,chkd->cd', w, expert_v[ec])

    y = lax.map(chunk, (xt.reshape(n_chunks, PEER_TOKEN_CHUNK, D),
                        eidx.reshape(n_chunks, PEER_TOKEN_CHUNK, H, K),
                        gate.reshape(n_chunks, PEER_TOKEN_CHUNK, H, K)))
    return y.reshape(B, S, D)

def hybrid_layer(x, rope_mla, rope_nsa, w_in, mla_q_norm, mla_w_uq, mla_kv_norm, mla_w_ukv,
                 ck_pe, ck_w1, ck_w2, cv_pe, cv_w1, cv_w2, w_branch_mla, w_branch_nsa, w_out,
                 ln1_g, ln1_b, peer_w_query, peer_sub_keys, peer_u, peer_v, ln2_g, ln2_b):
    B, S, _ = x.shape
    offsets = [int(o) for o in np.cumsum(IN_WIDTHS)[:-1]]
    c_q, c_kv, k_r, n_q, n_kv, n_gate, m_gate = jnp.split(x @ w_in, offsets, axis=-1)

    q = (rms_norm(c_q, mla_q_norm) @ mla_w_uq).reshape(B, S, MLA_HEADS, MLA_NOPE_DIM + MLA_ROPE_DIM)
    q_nope = q[..., :MLA_NOPE_DIM]
    q_rope = apply_rope(q[..., MLA_NOPE_DIM:], *rope_mla)
    kv = (rms_norm(c_kv, mla_kv_norm) @ mla_w_ukv).reshape(B, S, MLA_HEADS, MLA_NOPE_DIM + MLA_V_DIM)
    k_nope, v = kv[..., :MLA_NOPE_DIM], kv[..., MLA_NOPE_DIM:]
    k_rope = apply_rope(k_r[:, :, None, :], *rope_mla)[:, :, 0, :]
    y_mla = mla_attention(q_nope, q_rope, k_nope, k_rope, v) @ w_branch_mla

    qn = apply_rope(n_q.reshape(B, S, NSA_HEADS, NSA_HEAD_DIM), *rope_nsa)
    kvs = n_kv.reshape(B, S, 6, NSA_GROUPS, NSA_HEAD_DIM)
    k_cmp = apply_rope(kvs[:, :, 0], *rope_nsa)
    k_sel = apply_rope(kvs[:, :, 2], *rope_nsa)
    k_win = apply_rope(kvs[:, :, 4], *rope_nsa)
    kc = compress_blocks(k_cmp, ck_pe, ck_w1, ck_w2)
    vc = compress_blocks(kvs[:, :, 1], cv_pe, cv_w1, cv_w2)
    nsa_gates = jax.nn.sigmoid(n_gate.reshape(B, S, NSA_HEADS, 3))
    y_nsa = nsa_attention(qn, kc, vc, k_sel, kvs[:, :, 3], k_win, kvs[:, :, 5], nsa_gates) @ w_branch_nsa

    g_mla, g_nsa = jnp.split(jax.nn.sigmoid(m_gate), 2, axis=-1)
    mixed = (g_mla * y_mla + g_nsa * y_nsa) @ w_out
    x = layer_norm(DEEPNORM_ALPHA * x + mixed, ln1_g, ln1_b)

    x = layer_norm(DEEPNORM_ALPHA * x + peer(x, peer_w_query, peer_sub_keys, peer_u, peer_v), ln2_g, ln2_b)
    return x

def setup_inputs(seed: int = 0) -> dict:
    key = jax.random.key(seed)
    ks = jax.random.split(key, 28)
    L, D = DEPTH, D_MODEL
    f32 = jnp.float32

    def nrm(k, shape, scale):
        return jax.random.normal(k, shape, f32) * scale

    def gain(k, shape):
        return 1.0 + nrm(k, shape, 0.02)

    offsets = jax.random.randint(ks[1], (BATCH, 1), 0, 1024, dtype=jnp.int32)
    cmp_in = CMP_BLOCK * NSA_HEAD_DIM
    return {
        'x': nrm(ks[0], (BATCH, SEQ, D), 1.0),
        'positions': offsets + jnp.arange(SEQ, dtype=jnp.int32)[None, :],
        'ln_in_g': gain(ks[2], (D,)),
        'ln_in_b': nrm(ks[3], (D,), 0.02),
        'w_in': nrm(ks[4], (L, D, IN_WIDTH), D ** -0.5),
        'mla_q_norm': gain(ks[5], (L, MLA_Q_RANK)),
        'mla_w_uq': nrm(ks[6], (L, MLA_Q_RANK, MLA_HEADS * (MLA_NOPE_DIM + MLA_ROPE_DIM)), MLA_Q_RANK ** -0.5),
        'mla_kv_norm': gain(ks[7], (L, MLA_KV_RANK)),
        'mla_w_ukv': nrm(ks[8], (L, MLA_KV_RANK, MLA_HEADS * (MLA_NOPE_DIM + MLA_V_DIM)), MLA_KV_RANK ** -0.5),
        'nsa_cmp_k_pe': nrm(ks[9], (L, CMP_BLOCK, NSA_HEAD_DIM), 0.02),
        'nsa_cmp_k_w1': nrm(ks[10], (L, cmp_in, CMP_HIDDEN), cmp_in ** -0.5),
        'nsa_cmp_k_w2': nrm(ks[11], (L, CMP_HIDDEN, NSA_HEAD_DIM), CMP_HIDDEN ** -0.5),
        'nsa_cmp_v_pe': nrm(ks[12], (L, CMP_BLOCK, NSA_HEAD_DIM), 0.02),
        'nsa_cmp_v_w1': nrm(ks[13], (L, cmp_in, CMP_HIDDEN), cmp_in ** -0.5),
        'nsa_cmp_v_w2': nrm(ks[14], (L, CMP_HIDDEN, NSA_HEAD_DIM), CMP_HIDDEN ** -0.5),
        'w_branch_mla': nrm(ks[15], (L, MLA_MIX, D), DEEPNORM_BETA * MLA_MIX ** -0.5),
        'w_branch_nsa': nrm(ks[16], (L, NSA_MIX, D), DEEPNORM_BETA * NSA_MIX ** -0.5),
        'w_out': nrm(ks[17], (L, D, D), DEEPNORM_BETA * D ** -0.5),
        'ln1_g': gain(ks[18], (L, D)),
        'ln1_b': nrm(ks[19], (L, D), 0.02),
        'peer_w_query': nrm(ks[20], (L, D, PEER_HEADS * PEER_KEY_DIM), D ** -0.5),
        'peer_sub_keys': nrm(ks[21], (L, PEER_HEADS, 2, PEER_N_KEYS, PEER_KEY_DIM // 2), (PEER_KEY_DIM // 2) ** -0.5),
        'peer_u': nrm(ks[22], (L, PEER_N_EXPERTS, D), D ** -0.5),
        'peer_v': nrm(ks[23], (L, PEER_N_EXPERTS, D), DEEPNORM_BETA),
        'ln2_g': gain(ks[24], (L, D)),
        'ln2_b': nrm(ks[25], (L, D), 0.02),
    }

def reference(x, positions, ln_in_g, ln_in_b, w_in, mla_q_norm, mla_w_uq, mla_kv_norm, mla_w_ukv,
              nsa_cmp_k_pe, nsa_cmp_k_w1, nsa_cmp_k_w2, nsa_cmp_v_pe, nsa_cmp_v_w1, nsa_cmp_v_w2,
              w_branch_mla, w_branch_nsa, w_out, ln1_g, ln1_b,
              peer_w_query, peer_sub_keys, peer_u, peer_v, ln2_g, ln2_b):
    rope_mla = rope_angles(positions, MLA_ROPE_DIM)
    rope_nsa = rope_angles(positions, NSA_HEAD_DIM)
    h = layer_norm(x, ln_in_g, ln_in_b)
    for l in range(DEPTH):
        h = hybrid_layer(h, rope_mla, rope_nsa, w_in[l], mla_q_norm[l], mla_w_uq[l], mla_kv_norm[l], mla_w_ukv[l],
                         nsa_cmp_k_pe[l], nsa_cmp_k_w1[l], nsa_cmp_k_w2[l],
                         nsa_cmp_v_pe[l], nsa_cmp_v_w1[l], nsa_cmp_v_w2[l],
                         w_branch_mla[l], w_branch_nsa[l], w_out[l], ln1_g[l], ln1_b[l],
                         peer_w_query[l], peer_sub_keys[l], peer_u[l], peer_v[l], ln2_g[l], ln2_b[l])
    return h


_drawn_inputs = setup_inputs


def setup_inputs(seed=0):
    import zlib

    import numpy as np

    out = dict(_drawn_inputs(seed))
    spreads = {}
    factors = {'mla_q_norm': 7.508, 'mla_kv_norm': 6.104, 'nsa_cmp_k_pe': 25.536, 'nsa_cmp_v_pe': 5.825}
    for name, (base, spread) in spreads.items():
        noise = np.random.default_rng([zlib.crc32(name.encode()), seed]).standard_normal(out[name].shape)
        drawn = base * np.exp(spread * noise) if base else spread * noise
        out[name] = jnp.asarray(drawn.astype(out[name].dtype))
    for name, factor in factors.items():
        out[name] = (out[name] * factor).astype(out[name].dtype)
    return out
```

```python
from contextlib import ExitStack

import numpy as np

import concourse.bass as bass
from concourse import mybir

F32 = mybir.dt.float32
F32R = mybir.dt.float32r
I32 = mybir.dt.int32
U32 = mybir.dt.uint32
ALU = mybir.AluOpType
ACT = mybir.ActivationFunctionType
AX = mybir.AxisListType

P = 128
SEQ, D, DEPTH = 256, 1024, 2
TT = SEQ // P
DK = D // P
HEADS = 8
NOPE, ROPE, VDIM = 64, 32, 64
QKD = NOPE + ROPE
Q_RANK, KV_RANK = 768, 256
HD = 64
GROUPS = 2
CMP_BLOCK, CMP_STRIDE = 32, 16
NCMP = (SEQ - CMP_BLOCK) // CMP_STRIDE + 1
NKEYS, TOPK = 128, 16
ALPHA = (2 * DEPTH) ** 0.25
LN_EPS, RMS_EPS, NEG = 1e-5, 1e-6, -1e30
MLA_SCALE, NSA_SCALE = QKD ** -0.5, HD ** -0.5
LOWEST = -3.0e38
TWO_PI = 2 * np.pi
PI_A = 6.28125
PI_B = np.round((TWO_PI - PI_A) * 2.0 ** 20) / 2.0 ** 20
PI_C = float(np.float32(TWO_PI - PI_A - PI_B))
ROUND = 12582912.0

C_KR = Q_RANK + KV_RANK
C_NQ = C_KR + ROPE
C_KV = C_NQ + HEADS * HD
C_NG = C_KV + 6 * GROUPS * HD
C_MG = C_NG + 3 * HEADS
GW = GROUPS * HD
COLS_A = [(C_NQ, 512), (C_KV, GW), (C_KV + 2 * GW, GW), (C_KV + 4 * GW, GW), (C_KV + 5 * GW, GW)]
ROT = HEADS + 3 * GROUPS
COLS_B = [(C_KV + GW, GW), (C_KV + 3 * GW, GW), (C_KR, ROPE), (C_NG, 3 * HEADS)]
WB = 2 * GW + ROPE + 3 * HEADS

SLOTS = 4
N_LAT, N_UQ, N_UKV, N_B, N_A, N_MG, N_BR, N_OUT, N_PQ = 8, 6, 2, 4, 8, 16, 8, 8, 8
T_LAT = 0
T_UQ = T_LAT + N_LAT
T_UKV = T_UQ + N_UQ
T_B = T_UKV + N_UKV
T_A = T_B + N_B
T_MG = T_A + N_A
T_BR = T_MG + N_MG
T_OUT = T_BR + N_BR
T_PQ = T_OUT + N_OUT
FRONT = T_PQ + N_PQ
T_U = FRONT
T_V = T_U + NKEYS
NT = T_V + NKEYS
TURNS = NT // SLOTS
AHEAD = 3
assert NT % SLOTS == 0 and FRONT % SLOTS == 0

A_LAT, A_RMS, A_B, A_HID, A_KCVC, A_CS, A_O, A_MG, A_BR, A_PQ, A_SCR, A_U, A_G = (
    0, 8, 10, 12, 13, 14, 16, 24, 40, 48, 56, 64, 192)
NACC = 256
R_RMS, R_HID, R_KCVC, R_CS, R_O, R_SCR, R_G = 0, 2, 3, 4, 6, 14, 22
NREADY = R_G + 64
X_XT, X_Q, X_K, X_NQ, X_KT, X_CD, X_PC, X_AT, X_OT, X_XT2, X_PK = 0, 4, 8, 12, 16, 18, 20, 24, 42, 46, 50
NTR = 52
W_UQ, W_UKV, W_A, W_AT, W_OUT, W_V = 0, 1, 2, 3, 9, 10
NWIDE = 11
OPEN = 1
UNITS = [("mla", 0), ("mla", 1), ("sel", 0), ("win", 0), ("sel", 1), ("win", 1)]
NU = len(UNITS) * TT
O_OF = [0, 1, 2, 2, 3, 3]


def unit(u):
    tt, i = divmod(u, len(UNITS))
    kind, hg = UNITS[i]
    tr = [X_AT + u] if tt == 0 else [X_AT + 6 + 2 * (u - 6), X_AT + 7 + 2 * (u - 6)]
    return kind, hg, tt, tt * 4 + O_OF[i], tr


class Steps:

    def __init__(self, eng, sem, base, per_pass, apart=None):
        self.eng, self.sem, self.base, self.per_pass, self.n = eng, sem, base, per_pass, 0
        self.apart = apart

    def link(self, ins):
        ins.then_inc(self.sem, 1)
        self.n += 1
        self.eng.wait_ge(self.sem, self.base + self.n)
        if self.apart is not None:
            self.eng.sem_inc(self.apart, 1)

    def end(self):
        assert self.n == self.per_pass, (self.n, self.per_pass)


def build(nc, t, out):
    with ExitStack() as ctx:
        def sem(name):
            return ctx.enter_context(nc.semaphore(name))

        base = 16512

        def at(name, shape, dt, offset):
            return nc.alloc_sbuf_tensor_at(name, shape, dt, offset=base + offset)

        K = 1024
        big = at("big", [P, NKEYS, SEQ], F32, 0)
        cq_hi = at("cq_hi", [P, 8, SEQ], F32R, 0)
        cq_lo = at("cq_lo", [P, 8, SEQ], F32R, 8 * K)
        oT_hi = at("oT_hi", [P, 2, 4, SEQ], F32R, 0)
        oT_lo = at("oT_lo", [P, 2, 4, SEQ], F32R, 8 * K)
        pqT = at("pqT", [P, HEADS, SEQ], F32, 0)
        q_tok = at("q_tok", [P, TT, HEADS, QKD], F32, 16 * K)
        k_tok = at("k_tok", [P, TT, HEADS, QKD], F32, 22 * K)
        v_mla = at("v_mla", [P, TT, HEADS, VDIM], F32, 28 * K)
        o_tok = at("o_tok", [P, TT, 2, 512], F32, 16 * K)
        keys = at("keys", [P, HEADS, NKEYS], F32, 24 * K)
        qT = at("qT", [P, HEADS, SEQ], F32, 32 * K)
        kT = at("kT", [P, HEADS, SEQ], F32, 40 * K)
        ln_par = at("ln_par", [P, 2, D], F32, 40 * K)
        rot = at("rot", [P, TT, ROT, HD], F32, 48 * K)
        mix_a = at("mix_a", [P, 512], F32, 48 * K)
        mix_b = at("mix_b", [P, 512], F32, 50 * K)
        v_win = at("v_win", [P, TT, GW], F32, 55 * K)
        v_sel = at("v_sel", [P, TT, GW], F32, 56 * K)
        cmp_tok = at("cmp_tok", [P, TT, 2, GROUPS, 2, HD], F32, 57 * K)
        rope_a = at("rope_a", [P, ROT * HD], F32, 61 * K)
        rope_b = at("rope_b", [P, ROT * HD], F32, 61 * K + 3584)
        lat = at("lat", [P, SEQ], F32, 61 * K)
        nqT = at("nqT", [HD, HEADS, SEQ], F32, 68 * K)
        nkT = at("nkT", [HD, 4, SEQ], F32, 76 * K)
        cmpT = at("cmpT", [P, 4, SEQ], F32, 80 * K)
        blk = at("blk", [P, 2, 16, GROUPS * NCMP], F32, 84 * K)
        w1 = at("w1", [P, 2, 16, P], F32, 88 * K)
        gates = at("gates", [P, 16, SEQ], F32, 88 * K)
        sq = at("sq", [P, 8, SEQ], F32, 104 * K)
        sc = at("sc", [P, 2, 4, SEQ], F32, 104 * K)
        pT = at("pT", [P, 2, 2, 512], F32, 112 * K)
        pcT = at("pcT", [16, HEADS, SEQ], F32, 120 * K)
        S0 = NKEYS - 16
        o = 128 * K
        xs = at("xs", [P, TT, D], F32, o)
        xT_hi = at("xT_hi", [P, DK, SEQ], F32R, o + 8 * K)
        xT_lo = at("xT_lo", [P, DK, SEQ], F32R, o + 16 * K)
        hot_i = at("hot_i", [P, 2, 4, P], F32, o + 8 * K)
        hot_j = at("hot_j", [P, 2, 4, P], F32, o + 12 * K)
        w_hi = at("w_hi", [P, SLOTS, SEQ], F32R, o + 16 * K)
        w_lo = at("w_lo", [P, SLOTS, SEQ], F32R, o + 20 * K)
        raw = at("raw", [P, SLOTS, 1024], F32, o + 24 * K)
        lo = at("lo", [P, SLOTS, 1024], F32R, o + 24 * K)
        hi = at("hi", [P, SLOTS, 1024], F32R, o + 40 * K)
        o += 56 * K
        where = [o]

        def small(name, shape, dt=F32):
            size = int(np.prod(shape[1:])) * 4
            got = at(name, shape, dt, where[0])
            where[0] += (size + 31) // 32 * 32
            assert base + where[0] <= 229344
            return got

        ident = small("ident", [P, P])
        iota = small("iota", [P, P])
        causal = small("causal", [P, SEQ])
        cmask = small("cmask", [P, TT, NCMP])
        cmask01 = small("cmask01", [P, TT, NCMP])
        cos_m = small("cos_m", [P, TT, ROPE])
        sin_m = small("sin_m", [P, TT, ROPE])
        cos_n = small("cos_n", [P, TT, HD])
        sin_n = small("sin_n", [P, TT, HD])
        ones = small("ones", [P, 2])
        neg_half = small("neg_half", [P, 4])
        picks = small("picks", [P, 3, TT, P])
        picksT = small("picksT", [P, 3, SEQ])
        r_s = small("r_s", [P, 2, NKEYS])
        r_s2 = small("r_s2", [P, 2, NKEYS])
        r_v = small("r_v", [P, 2, TOPK])
        r_i = small("r_i", [P, 2, TOPK], U32)
        r_if = small("r_if", [P, 2, TOPK])
        r_c = small("r_c", [P, TOPK * TOPK])
        r_c2 = small("r_c2", [P, TOPK * TOPK])
        r_best = small("r_best", [P, TOPK])
        r_pos = small("r_pos", [P, TOPK], U32)
        r_ab = small("r_ab", [P, 2, TOPK], U32)
        r_abf = small("r_abf", [P, 2, TOPK])
        r_eq = small("r_eq", [P, 2, TOPK, TOPK])
        gsum = small("gsum", [P, TT * HEADS])
        stats = small("stats", [P, TT, 2, 6])
        mv = small("mv", [P, TT, 2])
        var = small("var", [P, 4])
        rstd = small("rstd", [P, 4])
        ngate = small("ngate", [P, TT, 3 * HEADS])
        kr = small("kr", [P, 3, ROPE])
        negmax = small("negmax", [P, 2, 4])
        sums = small("sums", [P, 2, 4])
        recip = small("recip", [P, 2, 4])
        cs = small("cs", [P, TT, HEADS, 16])
        cst = small("cst", [P, TT, 3, HEADS])
        lat_g = small("lat_g", [P, 8])
        pe = small("pe", [P, 2, 16])
        w2 = small("w2", [P, 2, HD])
        hid = small("hid", [P, 2, GROUPS * NCMP])
        kc = small("kc", [HD, GROUPS * NCMP])
        vc = small("vc", [16, GROUPS, HD])
        pos_i = small("pos_i", [P, TT], I32)
        pos_f = small("pos_f", [P, TT])
        freq = small("freq", [P, 48])
        ang = at("ang", [P, 4, TT, 48], F32, 0)
        warm = small("warm", [P, 2])

        acc = ctx.enter_context(nc.psum_tensor("acc", [P, 2, 512], F32))
        tr = ctx.enter_context(nc.psum_tensor("tr", [P, 2, 512], F32))
        wide = ctx.enter_context(nc.psum_tensor("wide", [P, TT, 1024], F32))

        loaded = [sem(f"loaded{s}") for s in range(SLOTS)]
        hi_done = sem("hi_done")
        lo_done = sem("lo_done")
        slot_free = [sem(f"slot_free{s}") for s in range(SLOTS)]
        acc_ready = sem("acc_ready")
        acc_read = [sem("acc_read0"), sem("acc_read1")]
        tr_ready = sem("tr_ready")
        tr_read = [sem("tr_read0"), sem("tr_read1")]
        wide_ready = sem("wide_ready")
        wide_read = [sem("wide_read0"), sem("wide_read1")]
        in_loaded = sem("in_loaded")
        consts_ready = sem("consts_ready")
        tables_step = sem("tables_step")
        angles_ready = sem("angles_ready")
        sines_ready = sem("sines_ready")
        small_loaded = sem("small_loaded")
        keys_loaded = sem("keys_loaded")
        ln_loaded = sem("ln_loaded")
        x_ready = sem("x_ready")
        tr_hi = sem("tr_hi")
        var_ready = sem("var_ready")
        rstd_ready = sem("rstd_ready")
        sq_done = sem("sq_done")
        lat_ready = sem("lat_ready")
        ngate_ready = sem("ngate_ready")
        tok_ready = sem("tok_ready")
        blk_ready = sem("blk_ready")
        cmp_shifted = sem("cmp_shifted")
        cmp_exp = sem("cmp_exp")
        cmp_ready = sem("cmp_ready")
        max_ready = sem("max_ready")
        exp_ready = sem("exp_ready")
        p_ready = sem("p_ready")
        mixed_ready = sem("mixed_ready")
        best_ready = sem("best_ready")
        gate_exp = sem("gate_exp")
        picks_ready = sem("picks_ready")
        hot_ready = sem("hot_ready")
        w_hi_done = sem("w_hi_done")
        w_lo_done = sem("w_lo_done")
        dve_step = sem("dve_step")
        route_step = sem("route_step")
        ln_step = sem("ln_step")
        pool_step = sem("pool_step")
        warm_step = sem("warm_step")
        stored = sem("stored")
        apart = sem("apart")

        block = ctx.enter_context(nc.Block())

        @block.sync
        def _(sp):
            for free in slot_free:
                sp.sem_inc(free, OPEN)
            sp.dma_start(xs[:], t["x"]).then_inc(in_loaded, 16)
            sp.dma_start(pos_i[:], t["positions"]).then_inc(in_loaded, 16)
            sp.dma_start(freq[:], t["freq"].partition_broadcast(P)).then_inc(in_loaded, 16)

            def load(l, src, first, turns):
                with sp.Fori(0, turns) as q:
                    for s in range(SLOTS):
                        turn = l * TURNS + (q + first // SLOTS)
                        sp.wait_ge(slot_free[s], OPEN + turn)
                        sp.dma_start(raw[:, s], src[l, q * SLOTS + s]).then_inc(loaded[s], 16)

            with sp.Fori(0, DEPTH) as l:
                load(l, t["front"], 0, FRONT // SLOTS)
                load(l, t["peer_u"], T_U, NKEYS // SLOTS)
                load(l, t["peer_v"], T_V, NKEYS // SLOTS)
            sp.wait_ge(x_ready, TT * (1 + 2 * DEPTH))
            sp.dma_start(out, xs[:]).then_inc(stored, 16)
            sp.wait_ge(stored, 16)

        @block.gpsimd
        def _(pool):
            pst = Steps(pool, pool_step, 0, 10)

            def ln_load(i):
                for r in range(2):
                    pool.dma_start(ln_par[:, r], t["ln"][i, r].partition_broadcast(P)).then_inc(ln_loaded, 16)

            ln_load(0)
            pst.link(nc.gpsimd.memset(ident[:], 0.0))
            pst.link(nc.gpsimd.affine_select(ident[:], ident[:], [[-1, P]], ALU.not_equal, 1.0, 0, 1))
            pst.link(nc.gpsimd.iota(iota[:], [[1, P]], 0, 0, allow_small_or_imprecise_dtypes=True))
            pst.link(nc.gpsimd.memset(causal[:], 0.0))
            pst.link(nc.gpsimd.affine_select(causal[:, P:], causal[:, P:], [[-1, P]], ALU.is_ge, NEG, 0, 1))
            pst.link(nc.gpsimd.memset(cmask[:], 0.0))
            pst.link(nc.gpsimd.memset(cmask01[:], 1.0))
            pat = [[P, TT], [-CMP_STRIDE, NCMP]]
            pst.link(nc.gpsimd.affine_select(cmask[:], cmask[:], pat, ALU.is_ge, NEG, 1 - CMP_BLOCK, 1))
            pst.link(nc.gpsimd.affine_select(cmask01[:], cmask01[:], pat, ALU.is_ge, 0.0, 1 - CMP_BLOCK, 1))
            nc.gpsimd.memset(ones[:], 1.0)
            pst.link(nc.gpsimd.memset(neg_half[:], -0.5))
            pst.end()
            nc.gpsimd.memset(warm[:], 0.0).then_inc(consts_ready, 1)

            def rsqrt(n, width):
                pool.wait_ge(var_ready, n + 1)
                nc.gpsimd.tensor_tensor(rstd[:, :width], var[:, :width], neg_half[:, :width],
                                        ALU.pow).then_inc(rstd_ready, 1)

            rsqrt(0, TT)
            with pool.Fori(0, DEPTH) as l:
                pool.wait_ge(slot_free[SLOTS - 1], OPEN + l * TURNS)
                pool.dma_start(lat_g[:], t["lat_g"][l]).then_inc(small_loaded, 16)
                pool.dma_start(pe[:], t["cmp_pe"][l]).then_inc(small_loaded, 16)
                pool.dma_start(w2[:], t["cmp_w2"][l]).then_inc(small_loaded, 16)
                pool.dma_start(w1[:], t["cmp_w1"][l]).then_inc(small_loaded, 16)
                rsqrt(3 * l + 1, 4)
                pool.wait_ge(tr_ready, l * NTR + X_NQ)
                pool.dma_start(keys[:], t["sub_keys"][l]).then_inc(keys_loaded, 16)
                pool.wait_ge(acc_ready, l * NREADY + R_SCR)
                for r in range(2):
                    pool.dma_start(ln_par[:, r], t["ln"][l * 2 + 1, r].partition_broadcast(P)).then_inc(ln_loaded, 16)
                rsqrt(3 * l + 2, TT)
                pool.wait_ge(w_lo_done, l * NKEYS + 48)
                for r in range(2):
                    pool.dma_start(ln_par[:, r], t["ln"][l * 2 + 2, r].partition_broadcast(P)).then_inc(ln_loaded, 16)
                rsqrt(3 * l + 3, TT)

        @block.scalar
        def _(act):
            def split_hi(l, q, s):
                act.wait_ge(loaded[s], (l * TURNS + q + 1) * 16)
                nc.scalar.activation(hi[:, s], raw[:, s], ACT.Identity).then_inc(hi_done, 1)

            def tile_step(l, n):
                split_hi(l, (n + AHEAD) // SLOTS, (n + AHEAD) % SLOTS)

            def tile_used(l, q, s):
                act.wait_ge(slot_free[s], OPEN + l * TURNS + q + 1)

            def tr_copy(l, i, dst, src):
                act.wait_ge(tr_ready, l * NTR + i + 1)
                nc.scalar.activation(dst, src, ACT.Identity).then_inc(tr_read[i % 2], 1)

            def warm_up(func, n):
                nc.scalar.activation(warm[:, 1:2], warm[:, 0:1], func).then_inc(warm_step, 1)
                act.wait_ge(warm_step, n)

            act.wait_ge(consts_ready, 1)
            act.wait_ge(angles_ready, 1)
            nc.scalar.activation(ang[:, 2], ang[:, 0], ACT.Sin).then_inc(sines_ready, 1)
            nc.scalar.activation(ang[:, 3], ang[:, 1], ACT.Sin).then_inc(sines_ready, 1)

            with act.Fori(0, DEPTH) as l:
                warm_up(ACT.Gelu, l * 3 + 1)
                for n in range(AHEAD):
                    split_hi(l, 0, n)

                def transposed_hi(first, hi_first, dst):
                    for g in range(4):
                        act.wait_ge(tr_ready, l * NTR + first + g + 1)
                        nc.scalar.activation(dst(g), tr[:, (first + g) % 2].rearrange("p (c t) -> p c t", c=4),
                                             ACT.Identity).then_inc(tr_hi, 1)

                def xT_part(g):
                    tt, cg = divmod(g, 2)
                    return xT_hi[:, 4 * cg:4 * cg + 4, tt * P:(tt + 1) * P]

                transposed_hi(X_XT, 0, xT_part)
                for c in range(N_LAT):
                    tile_step(l, T_LAT + c)
                    tile_used(l, (T_LAT + c) // SLOTS, (T_LAT + c) % SLOTS)
                    nc.scalar.activation(sq[:, c], acc[:, c % 2, :SEQ], ACT.Square).then_inc(sq_done, 1)
                for n in range(T_UQ, T_A):
                    tile_step(l, n)
                n = T_A - 1
                tile_used(l, n // SLOTS, n % SLOTS)
                for tt in range(TT):
                    nc.scalar.activation(ngate[:, tt], acc[:, tt, 2 * GW + ROPE:WB], ACT.Sigmoid).then_inc(ngate_ready, 1)
                for n in range(T_A, T_MG):
                    tile_step(l, n)
                for g in range(0, 4, 2):
                    tt, hg = divmod(g, 2)
                    tr_copy(l, X_Q + g, qT[:QKD, 4 * hg:4 * hg + 4, tt * P:(tt + 1) * P],
                            tr[:QKD, 0].rearrange("p (h t) -> p h t", h=4))
                for g in range(0, 4, 2):
                    tt, hg = divmod(g, 2)
                    tr_copy(l, X_K + g, kT[:QKD, 4 * hg:4 * hg + 4, tt * P:(tt + 1) * P],
                            tr[:QKD, 0].rearrange("p (h t) -> p h t", h=4))
                for g in range(0, 4, 2):
                    tt, hg = divmod(g, 2)
                    tr_copy(l, X_NQ + g, nqT[:, 4 * hg:4 * hg + 4, tt * P:(tt + 1) * P],
                            tr[:HD, 0].rearrange("p (h t) -> p h t", h=4))
                tr_copy(l, X_KT, nkT[:, :, 0:P], tr[:HD, 0].rearrange("p (h t) -> p h t", h=4))
                tr_copy(l, X_CD, cmpT[:, :, 0:P], tr[:, 0].rearrange("p (h t) -> p h t", h=4))
                act.wait_ge(acc_ready, l * NREADY + R_HID + 1)
                nc.scalar.activation(hid[:], acc[:, A_HID % 2, :2 * GROUPS * NCMP].rearrange("p (c n) -> p c n", c=2),
                                     ACT.Gelu).then_inc(acc_read[A_HID % 2], 1)
                for tt in range(TT):
                    act.wait_ge(cmp_shifted, l * TT + tt + 1)
                    nc.scalar.activation(cs[:, tt, :, :NCMP], cs[:, tt, :, :NCMP], ACT.Exp).then_inc(cmp_exp, 1)
                for tt in range(TT):
                    i = X_PC + 2 * tt
                    tr_copy(l, i, pcT[:NCMP, 0:4, tt * P:(tt + 1) * P],
                            tr[:NCMP, 0].rearrange("p (h t) -> p h t", h=4))

                def copy_o(oi):
                    act.wait_ge(acc_ready, l * NREADY + R_O + oi + 1)
                    tt, i = divmod(oi, 4)
                    nc.scalar.activation(o_tok[:, tt, i // 2, 256 * (i % 2):256 * (i % 2) + 256],
                                         acc[:, oi % 2, :256], ACT.Identity).then_inc(acc_read[oi % 2], 1)

                def copy_pT(u):
                    for kb, i in enumerate(unit(u)[4]):
                        if i % 2 == 0:
                            tr_copy(l, i, pT[:, u % 2, kb], tr[:, 0])

                copied = 0
                for u in range(NU + 2):
                    if u < NU:
                        kind, hg, tt, oi, _ = unit(u)
                        act.wait_ge(max_ready, l * NU + u + 1)
                        for h in range(4):
                            ins = nc.scalar.activation(sc[:, u % 2, h, :(tt + 1) * P], sc[:, u % 2, h, :(tt + 1) * P],
                                                       ACT.Exp, bias=negmax[:, u % 2, h:h + 1],
                                                       accum_out=sums[:, u % 2, h:h + 1])
                        ins.then_inc(exp_ready, 1)
                    if 1 <= u <= NU:
                        copy_pT(u - 1)
                    if u >= 2 and (u - 2 == NU - 1 or unit(u - 2)[3] != unit(u - 1)[3]):
                        copy_o(copied)
                        copied += 1
                transposed_hi(X_OT, 4, lambda g: oT_hi[:, g // 2, :, (g % 2) * P:(g % 2 + 1) * P])

                warm_up(ACT.Sigmoid, l * 3 + 2)
                with act.Fori(0, N_MG // SLOTS) as i:
                    for e in range(SLOTS):
                        split_hi(l, (i + (T_MG + e + AHEAD) // SLOTS), (T_MG + e + AHEAD) % SLOTS)
                        tile_used(l, (i + (T_MG + e) // SLOTS), (T_MG + e) % SLOTS)
                        nc.scalar.activation(gates[:, i * SLOTS + e], acc[:, e % 2, :SEQ],
                                             ACT.Sigmoid).then_inc(acc_read[e % 2], 1)
                for n in range(T_BR, T_PQ):
                    tile_step(l, n)
                transposed_hi(X_XT2, 8, xT_part)
                warm_up(ACT.Gelu, l * 3 + 3)
                with act.Fori(0, N_PQ // SLOTS) as i:
                    for e in range(SLOTS):
                        split_hi(l, (i + (T_PQ + e + AHEAD) // SLOTS), (T_PQ + e + AHEAD) % SLOTS)
                        tile_used(l, (i + (T_PQ + e) // SLOTS), (T_PQ + e) % SLOTS)
                        nc.scalar.activation(pqT[:, i * SLOTS + e], acc[:, e % 2, :SEQ],
                                             ACT.Identity).then_inc(acc_read[e % 2], 1)
                for i in range(8):
                    c, p = divmod(i, 2)
                    act.wait_ge(acc_ready, l * NREADY + R_SCR + i + 1)
                    nc.scalar.activation(big[:, S0 + 4 * c:S0 + 4 * c + 4, p * P:(p + 1) * P],
                                         acc[:, p].rearrange("p (u n) -> p u n", u=4),
                                         ACT.Identity).then_inc(acc_read[p], 1)
                with act.Fori(0, NKEYS // 8) as i:
                    for e in range(8):
                        n = T_U + e
                        split_hi(l, (i * 2 + (n + AHEAD) // SLOTS), (n + AHEAD) % SLOTS)
                        tile_used(l, (i * 2 + n // SLOTS), n % SLOTS)
                        nc.scalar.activation(big[:, i * 8 + e], acc[:, e % 2, :SEQ],
                                             ACT.Gelu).then_inc(acc_read[e % 2], 1)
                act.wait_ge(best_ready, l + 1)
                nc.scalar.activation(picks[:, 2], picks[:, 2], ACT.Exp).then_inc(gate_exp, 1)
                tr_copy(l, X_PK, picksT[:, 0:2], tr[:, 0].rearrange("p (k t) -> p k t", k=2))

                def split_w_hi(j, s):
                    nc.scalar.activation(w_hi[:, s], big[:, j], ACT.Identity).then_inc(w_hi_done, 1)

                for b in range(2):
                    act.wait_ge(acc_read[b], OPEN + l * (NACC // 2) + NACC // 2)
                for j in range(AHEAD):
                    split_w_hi(j, j)
                with act.Fori(0, NKEYS // SLOTS - 1) as i:
                    for e in range(SLOTS):
                        n = T_V + e + AHEAD
                        split_hi(l, (i + n // SLOTS), n % SLOTS)
                        split_w_hi(i * SLOTS + (e + AHEAD), n % SLOTS)
                split_hi(l, TURNS - 1, SLOTS - 1)
                split_w_hi(NKEYS - 1, SLOTS - 1)

        @block.vector
        def _(dve):
            def split_lo(l, q, s):
                dve.wait_ge(hi_done, l * NT + q * SLOTS + s + 1)
                nc.vector.tensor_tensor(lo[:, s], raw[:, s], hi[:, s].bitcast(F32), ALU.subtract).then_inc(lo_done, 1)

            def tile_step(l, n):
                split_lo(l, (n + AHEAD) // SLOTS, (n + AHEAD) % SLOTS)

            def tile_used(l, q, s):
                dve.wait_ge(slot_free[s], OPEN + l * TURNS + q + 1)

            def tr_copy(l, i, dst, src):
                dve.wait_ge(tr_ready, l * NTR + i + 1)
                nc.vector.tensor_copy(dst, src).then_inc(tr_read[i % 2], 1)

            def layer_norm(nth, add, rs_nth, loads, chain):
                for tt in range(TT):
                    if add is not None:
                        add(tt)
                    for c in range(2):
                        chain.link(nc.vector.bn_stats(stats[:, tt, c], xs[:, tt, 512 * c:512 * c + 512]))
                    dve.sem_inc(apart, 1)
                    chain.link(nc.vector.bn_aggr(mv[:, tt], stats[:, tt].rearrange("p c s -> p (c s)")))
                nc.vector.tensor_scalar(var[:, :TT], mv[:, :, 1], LN_EPS, None, ALU.add).then_inc(var_ready, 1)
                dve.wait_ge(rstd_ready, rs_nth + 1)
                dve.wait_ge(ln_loaded, loads)
                for tt in range(TT):
                    chain.link(nc.vector.tensor_scalar(xs[:, tt], xs[:, tt], mv[:, tt, 0:1], rstd[:, tt:tt + 1],
                                                       ALU.subtract, ALU.mult))
                    chain.link(nc.vector.tensor_tensor(xs[:, tt], xs[:, tt], ln_par[:, 0], ALU.mult))
                    nc.vector.tensor_tensor(xs[:, tt], xs[:, tt], ln_par[:, 1], ALU.add).then_inc(x_ready, 1)

            for done in (lat_ready, mixed_ready):
                dve.sem_inc(done, OPEN)

            tab = Steps(dve, tables_step, 0, 15)
            dve.wait_ge(in_loaded, 48)
            tab.link(nc.vector.tensor_copy(pos_f[:], pos_i[:]))
            for tt in range(TT):
                tab.link(nc.vector.tensor_scalar(ang[:, 0, tt], freq[:], pos_f[:, tt:tt + 1], None, ALU.mult))
            tab.link(nc.vector.tensor_scalar(ang[:, 1], ang[:, 0], 1.0 / TWO_PI, None, ALU.mult))
            tab.link(nc.vector.tensor_scalar(ang[:, 1], ang[:, 1], ROUND, None, ALU.add))
            tab.link(nc.vector.tensor_scalar(ang[:, 1], ang[:, 1], ROUND, None, ALU.subtract))
            for part in (PI_A, PI_B, PI_C):
                tab.link(nc.vector.scalar_tensor_tensor(out=ang[:, 0], in0=ang[:, 1], scalar=-part, in1=ang[:, 0],
                                                        op0=ALU.mult, op1=ALU.add))
            tab.link(nc.vector.tensor_scalar(ang[:, 0], ang[:, 0], float(np.float32(np.pi)),
                                             -float(np.float32(np.pi)), ALU.min, ALU.max))
            tab.link(nc.vector.scalar_tensor_tensor(out=ang[:, 1], in0=ang[:, 0], scalar=-1.0, in1=ang[:, 0],
                                                    op0=ALU.mult, op1=ALU.max))
            nc.vector.tensor_scalar(ang[:, 1], ang[:, 1], -1.0, float(np.pi / 2), ALU.mult, ALU.add).then_inc(angles_ready, 1)
            dve.wait_ge(sines_ready, 2)
            R2, H2 = ROPE // 2, HD // 2
            tab.link(nc.vector.tensor_copy(cos_m[:, :, :R2], ang[:, 3, :, :R2]))
            tab.link(nc.vector.tensor_copy(cos_m[:, :, R2:], ang[:, 3, :, :R2]))
            tab.link(nc.vector.tensor_copy(sin_m[:, :, R2:], ang[:, 2, :, :R2]))
            tab.link(nc.vector.tensor_scalar(sin_m[:, :, :R2], ang[:, 2, :, :R2], -1.0, None, ALU.mult))
            tab.end()
            tab = Steps(dve, tables_step, 15, 4)
            tab.link(nc.vector.tensor_copy(cos_n[:, :, :H2], ang[:, 3, :, R2:]))
            tab.link(nc.vector.tensor_copy(cos_n[:, :, H2:], ang[:, 3, :, R2:]))
            tab.link(nc.vector.tensor_copy(sin_n[:, :, H2:], ang[:, 2, :, R2:]))
            tab.link(nc.vector.tensor_scalar(sin_n[:, :, :H2], ang[:, 2, :, R2:], -1.0, None, ALU.mult))
            tab.end()
            LN_STEPS = TT * 5
            chain = Steps(dve, ln_step, 0, LN_STEPS)
            layer_norm(0, None, 0, 32, chain)
            chain.end()
            dve.wait_ge(consts_ready, 1)

            with dve.Fori(0, DEPTH) as l:
                st = Steps(dve, dve_step, l * DVE_STEPS, DVE_STEPS)
                for n in range(AHEAD):
                    split_lo(l, 0, n)

                def transposed_lo(first, hi_first, dst_hi, dst_lo):
                    for g in range(4):
                        dve.wait_ge(tr_hi, l * 12 + hi_first + g + 1)
                        nc.vector.tensor_tensor(dst_lo(g), tr[:, (first + g) % 2].rearrange("p (c t) -> p c t", c=4),
                                                dst_hi(g).bitcast(F32), ALU.subtract).then_inc(tr_read[(first + g) % 2], 1)

                def x_part(part):
                    def f(g):
                        tt, cg = divmod(g, 2)
                        return part[:, 4 * cg:4 * cg + 4, tt * P:(tt + 1) * P]
                    return f

                def o_part(part):
                    return lambda g: part[:, g // 2, :, (g % 2) * P:(g % 2 + 1) * P]

                def rotate(dst, src, cos, sin, heads, width, tmp_a, tmp_b, release=None):
                    h = width // 2
                    a = tmp_a[:, :heads * width].rearrange("p (h d) -> p h d", d=width)
                    b = tmp_b[:, :heads * width].rearrange("p (h d) -> p h d", d=width)
                    full = [P, heads, width]
                    half = [P, heads, h]
                    st.link(nc.vector.tensor_tensor(a, src, cos.unsqueeze(1).broadcast_to(full), ALU.mult))
                    st.link(nc.vector.tensor_tensor(b[:, :, :h], src[:, :, h:], sin[:, :h].unsqueeze(1).broadcast_to(half), ALU.mult))
                    st.link(nc.vector.tensor_tensor(b[:, :, h:], src[:, :, :h], sin[:, h:].unsqueeze(1).broadcast_to(half), ALU.mult))
                    if release is not None:
                        release()
                    return nc.vector.tensor_tensor(dst, a, b, ALU.add)

                transposed_lo(X_XT, 0, x_part(xT_hi), x_part(xT_lo))
                dve.wait_ge(small_loaded, l * 64 + 64)
                for c in range(N_LAT):
                    n = T_LAT + c
                    tile_step(l, n)
                    dve.wait_ge(sq_done, l * N_LAT + c + 1)
                    dve.wait_ge(lat_ready, OPEN + l * N_LAT + c)
                    nc.vector.tensor_scalar(lat[:], acc[:, c % 2, :SEQ], lat_g[:, c:c + 1], None,
                                            ALU.mult).then_inc(acc_read[c % 2], 1)
                    dve.wait_ge(acc_read[c % 2], OPEN + l * (NACC // 2) + (A_LAT + c) // 2 + 1)
                    st.link(nc.vector.tensor_copy(cq_hi[:, c], lat[:]))
                    nc.vector.tensor_tensor(cq_lo[:, c], lat[:], cq_hi[:, c].bitcast(F32), ALU.subtract).then_inc(lat_ready, 1)
                dve.wait_ge(acc_ready, l * NREADY + R_RMS + 1)
                nc.vector.tensor_scalar(var[:, 0:TT], acc[:, 0, 0:TT], 1.0 / Q_RANK, RMS_EPS, ALU.mult,
                                        ALU.add).then_inc(acc_read[0], 1)
                dve.wait_ge(acc_ready, l * NREADY + R_RMS + 2)
                st.link(nc.vector.tensor_scalar(var[:, TT:2 * TT], acc[:, 1, 0:TT], 1.0 / KV_RANK, RMS_EPS, ALU.mult, ALU.add))
                nc.vector.tensor_copy(gsum[:, 0:TT], acc[:, 1, 0:TT]).then_inc(acc_read[1], 1)
                nc.vector.tensor_copy(gsum[:, TT:2 * TT], var[:, 0:TT]).then_inc(var_ready, 1)
                for n in range(T_UQ, T_UKV):
                    tile_step(l, n)
                dve.wait_ge(rstd_ready, 3 * l + 2)
                n = T_UKV - 1
                tile_used(l, n // SLOTS, n % SLOTS)
                for tt in range(TT):
                    nc.vector.tensor_scalar(q_tok[:, tt].rearrange("p (a h) d -> p a (h d)", a=2),
                                            wide[:, tt].rearrange("p (a c) -> p a c", a=2)[:, :, :384],
                                            rstd[:, tt:tt + 1], None, ALU.mult).then_inc(wide_read[tt], 1)
                for n in range(T_UKV, T_B):
                    tile_step(l, n)
                for tt in range(TT):
                    dve.wait_ge(wide_read[tt], OPEN + l * NWIDE + W_UQ + 1)
                    part = q_tok[:, tt, :, NOPE:]
                    st.link(rotate(part, part, cos_m[:, tt], sin_m[:, tt], HEADS, ROPE, rope_a, rope_b))
                n = T_B - 1
                tile_used(l, n // SLOTS, n % SLOTS)
                for tt in range(TT):
                    kv = wide[:, tt].rearrange("p (h d) -> p h d", d=NOPE + VDIM)
                    nc.vector.tensor_scalar(k_tok[:, tt, :, :NOPE], kv[:, :, :NOPE], rstd[:, TT + tt:TT + tt + 1], None, ALU.mult)
                    nc.vector.tensor_scalar(v_mla[:, tt], kv[:, :, NOPE:], rstd[:, TT + tt:TT + tt + 1], None,
                                            ALU.mult).then_inc(wide_read[tt], 1)
                for n in range(T_B, T_A):
                    tile_step(l, n)
                n = T_A - 1
                tile_used(l, n // SLOTS, n % SLOTS)
                for tt in range(TT):
                    dve.wait_ge(ngate_ready, l * TT + tt + 1)
                    pair = acc[:, tt, :GW].rearrange("p (g d) -> p g d", g=GROUPS)
                    nc.vector.tensor_copy(cmp_tok[:, tt, 1], pair.unsqueeze(2).broadcast_to([P, GROUPS, 2, HD]))
                    nc.vector.tensor_copy(v_sel[:, tt], acc[:, tt, GW:2 * GW])
                    st.link(nc.vector.tensor_copy(kr[:, 0], acc[:, tt, 2 * GW:2 * GW + ROPE]))
                    nc.vector.tensor_copy(kr[:, 1], acc[:, tt, 2 * GW:2 * GW + ROPE]).then_inc(acc_read[tt], 1)
                    dve.wait_ge(acc_read[tt], OPEN + l * (NACC // 2) + (A_B + tt) // 2 + 1)
                    st.link(rotate(kr[:, 1:2], kr[:, 0:1], cos_m[:, tt], sin_m[:, tt], 1, ROPE, rope_a, rope_b))
                    nc.vector.tensor_copy(k_tok[:, tt, :, NOPE:], kr[:, 1:2].broadcast_to([P, HEADS, ROPE]))
                for n in range(T_A, T_MG):
                    tile_step(l, n)
                n = T_MG - 1
                tile_used(l, n // SLOTS, n % SLOTS)
                for tt in range(TT):
                    def release():
                        nc.vector.tensor_copy(v_win[:, tt], wide[:, tt, ROT * HD:]).then_inc(wide_read[tt], 1)

                    st.link(rotate(rot[:, tt], wide[:, tt, :ROT * HD].rearrange("p (h d) -> p h d", d=HD),
                                   cos_n[:, tt], sin_n[:, tt], ROT, HD, rope_a, rope_b, release))
                    nc.vector.tensor_copy(cmp_tok[:, tt, 0], rot[:, tt, HEADS:HEADS + GROUPS].unsqueeze(2).broadcast_to(
                        [P, GROUPS, 2, HD])).then_inc(tok_ready, 1)
                for g in range(1, 4, 2):
                    tt, hg = divmod(g, 2)
                    tr_copy(l, X_Q + g, qT[:QKD, 4 * hg:4 * hg + 4, tt * P:(tt + 1) * P],
                            tr[:QKD, 1].rearrange("p (h t) -> p h t", h=4))
                for g in range(1, 4, 2):
                    tt, hg = divmod(g, 2)
                    tr_copy(l, X_K + g, kT[:QKD, 4 * hg:4 * hg + 4, tt * P:(tt + 1) * P],
                            tr[:QKD, 1].rearrange("p (h t) -> p h t", h=4))
                for g in range(1, 4, 2):
                    tt, hg = divmod(g, 2)
                    tr_copy(l, X_NQ + g, nqT[:, 4 * hg:4 * hg + 4, tt * P:(tt + 1) * P],
                            tr[:HD, 1].rearrange("p (h t) -> p h t", h=4))
                tr_copy(l, X_KT + 1, nkT[:, :, P:], tr[:HD, 1].rearrange("p (h t) -> p h t", h=4))
                tr_copy(l, X_CD + 1, cmpT[:, :, P:], tr[:, 1].rearrange("p (h t) -> p h t", h=4))
                for b in range(2):
                    dve.wait_ge(tr_read[b], OPEN + l * (NTR // 2) + (X_CD + 1) // 2 + 1)
                for c in range(2):
                    for par in range(2):
                        rows = slice(par * HD, par * HD + HD)
                        for g in range(GROUPS):
                            src = bass.AP(cmpT[rows, 2 * c + g].tensor, cmpT[rows, 2 * c + g].offset + par,
                                          [cmpT[rows, 2 * c + g].ap[0], [2, 16], [CMP_STRIDE, NCMP]])
                            ins = nc.vector.tensor_tensor(
                                blk[rows, c, :, g * NCMP:(g + 1) * NCMP], src,
                                pe[rows, c].unsqueeze(2).broadcast_to([HD, 16, NCMP]), ALU.add)
                            ins.then_inc(blk_ready, 1)
                dve.wait_ge(acc_ready, l * NREADY + R_KCVC + 1)
                b = A_KCVC % 2
                st.link(nc.vector.tensor_copy(kc[:], acc[:HD, b, 0:GROUPS * NCMP]))
                nc.vector.tensor_copy(vc[:NCMP], acc[:NCMP, b, 64:64 + GROUPS * HD].rearrange(
                    "p (g d) -> p g d", g=GROUPS)).then_inc(acc_read[b], 1)
                m3 = [P, HEADS, NCMP]
                for tt in range(TT):
                    b = (A_CS + tt) % 2
                    dve.wait_ge(acc_ready, l * NREADY + R_CS + tt + 1)
                    e = cs[:, tt, :, :NCMP]
                    nc.vector.scalar_tensor_tensor(
                        out=e, in0=acc[:, b, :HEADS * 16].rearrange("p (h n) -> p h n", n=16)[:, :, :NCMP],
                        scalar=NSA_SCALE, in1=cmask[:, tt].unsqueeze(1).broadcast_to(m3),
                        op0=ALU.mult, op1=ALU.add).then_inc(acc_read[b], 1)
                    dve.wait_ge(acc_read[b], OPEN + l * (NACC // 2) + (A_CS + tt) // 2 + 1)
                    st.link(nc.vector.tensor_reduce(cst[:, tt, 0], e, AX.X, ALU.max))
                    nc.vector.tensor_tensor(e, e, cst[:, tt, 0].unsqueeze(2).broadcast_to(m3),
                                            ALU.subtract).then_inc(cmp_shifted, 1)
                for tt in range(TT):
                    e = cs[:, tt, :, :NCMP]
                    dve.wait_ge(cmp_exp, l * TT + tt + 1)
                    st.link(nc.vector.tensor_reduce(cst[:, tt, 1], e, AX.X, ALU.add))
                    st.link(nc.vector.reciprocal(cst[:, tt, 2], cst[:, tt, 1]))
                    g0 = ngate[:, tt].rearrange("p (h b) -> p h b", b=3)[:, :, 0]
                    st.link(nc.vector.tensor_tensor(cst[:, tt, 2], cst[:, tt, 2], g0, ALU.mult))
                    st.link(nc.vector.tensor_tensor(e, e, cmask01[:, tt].unsqueeze(1).broadcast_to(m3), ALU.mult))
                    nc.vector.tensor_tensor(e, e, cst[:, tt, 2].unsqueeze(2).broadcast_to(m3),
                                            ALU.mult).then_inc(cmp_ready, 1)
                for tt in range(TT):
                    tr_copy(l, X_PC + 2 * tt + 1, pcT[:NCMP, 4:8, tt * P:(tt + 1) * P],
                            tr[:NCMP, 1].rearrange("p (h t) -> p h t", h=4))

                def scores_in(u):
                    kind, hg, tt, oi, trs = unit(u)
                    keys_n = (tt + 1) * P
                    dve.wait_ge(wide_ready, l * NU + u + 1)
                    if u >= 2:
                        dve.wait_ge(tr_ready, l * NTR + unit(u - 2)[4][-1] + 1)
                    s = sc[:, u % 2, :, :keys_n]
                    nc.vector.scalar_tensor_tensor(
                        out=s, in0=wide[:, u % 2].rearrange("p (h k) -> p h k", h=4)[:, :, :keys_n],
                        scalar=MLA_SCALE if kind == "mla" else NSA_SCALE,
                        in1=causal[:, SEQ - keys_n:].unsqueeze(1).broadcast_to([P, 4, keys_n]),
                        op0=ALU.mult, op1=ALU.add).then_inc(wide_read[u % 2], 1)
                    dve.wait_ge(wide_read[u % 2], OPEN + l * NWIDE + W_AT + u // 2 + 1)
                    nc.vector.tensor_reduce(negmax[:, u % 2], s, AX.X, ALU.max, negate=True).then_inc(max_ready, 1)

                def weights_out(u):
                    kind, hg, tt, oi, trs = unit(u)
                    dve.wait_ge(exp_ready, l * NU + u + 1)
                    st.link(nc.vector.reciprocal(recip[:, u % 2], sums[:, u % 2]))
                    if kind != "mla":
                        g = ngate[:, tt].rearrange("p (h b) -> p h b", b=3)[:, 4 * hg:4 * hg + 4, 1 if kind == "sel" else 2]
                        st.link(nc.vector.tensor_tensor(recip[:, u % 2], recip[:, u % 2], g, ALU.mult))
                    for h in range(4):
                        s = sc[:, u % 2, h, :(tt + 1) * P]
                        ins = nc.vector.tensor_scalar(s, s, recip[:, u % 2, h:h + 1], None, ALU.mult)
                    ins.then_inc(p_ready, 1)

                def copy_pT(u):
                    for kb, i in enumerate(unit(u)[4]):
                        if i % 2 == 1:
                            tr_copy(l, i, pT[:, u % 2, kb], tr[:, 1])

                scores_in(0)
                for u in range(NU):
                    if u + 1 < NU:
                        scores_in(u + 1)
                    if u >= 1:
                        copy_pT(u - 1)
                    weights_out(u)
                copy_pT(NU - 1)
                transposed_lo(X_OT, 4, o_part(oT_hi), o_part(oT_lo))

                with dve.Fori(0, N_MG // SLOTS) as i:
                    for e in range(SLOTS):
                        split_lo(l, (i + (T_MG + e + AHEAD) // SLOTS), (T_MG + e + AHEAD) % SLOTS)
                for q in range(4):
                    for e in range(2):
                        n = T_BR + 2 * q + e
                        tile_step(l, n)
                        tile_used(l, n // SLOTS, n % SLOTS)
                        if q == 0:
                            dve.wait_ge(acc_read[e], OPEN + l * (NACC // 2) + A_BR // 2)
                        if e == 0:
                            dve.wait_ge(mixed_ready, OPEN + l * 4 + q)
                        nc.vector.tensor_tensor((mix_a if e == 0 else mix_b)[:].rearrange("p (f t) -> p f t", f=2),
                                                acc[:, e].rearrange("p (f t) -> p f t", f=2),
                                                gates[:, 8 * e + 2 * q:8 * e + 2 * q + 2], ALU.mult).then_inc(acc_read[e], 1)
                    for e in range(2):
                        dve.wait_ge(acc_read[e], OPEN + l * (NACC // 2) + A_BR // 2 + q + 1)
                    st.link(nc.vector.tensor_tensor(mix_a[:], mix_a[:], mix_b[:], ALU.add))
                    m = mix_a[:].rearrange("p (f t) -> p f t", f=2)
                    st.link(nc.vector.tensor_copy(xT_hi[:, 2 * q:2 * q + 2], m))
                    nc.vector.tensor_tensor(xT_lo[:, 2 * q:2 * q + 2], m, xT_hi[:, 2 * q:2 * q + 2].bitcast(F32),
                                            ALU.subtract).then_inc(mixed_ready, 1)
                for n in range(T_OUT, T_PQ):
                    tile_step(l, n)

                def add_branch(last_tile, use):
                    def f(tt):
                        if tt == 0:
                            tile_used(l, last_tile // SLOTS, last_tile % SLOTS)
                        nc.vector.scalar_tensor_tensor(out=xs[:, tt], in0=xs[:, tt], scalar=ALPHA, in1=wide[:, tt],
                                                       op0=ALU.mult, op1=ALU.add).then_inc(wide_read[tt], 1)
                        dve.wait_ge(wide_read[tt], OPEN + l * NWIDE + use + 1)
                    return f

                layer_norm(None, add_branch(T_PQ - 1, W_OUT), 3 * l + 2, l * 64 + 64, st)
                transposed_lo(X_XT2, 8, x_part(xT_hi), x_part(xT_lo))
                with dve.Fori(0, N_PQ // SLOTS) as i:
                    for e in range(SLOTS):
                        split_lo(l, (i + (T_PQ + e + AHEAD) // SLOTS), (T_PQ + e + AHEAD) % SLOTS)
                for b in range(2):
                    dve.wait_ge(acc_read[b], OPEN + l * (NACC // 2) + A_U // 2)
                dve.sem_inc(apart, 1)

                with dve.Fori(0, NKEYS // 8) as i:
                    rt = Steps(dve, route_step, (l * 16 + i) * ROUTE_STEPS, ROUTE_STEPS, apart)

                    def top16(vals, spare, best, index, part=None):
                        return [
                            lambda: rt.link(nc.vector.max(best[:, 0:8], vals)),
                            lambda: rt.link(nc.vector.match_replace(spare, best[:, 0:8], vals, LOWEST)),
                            lambda: rt.link(nc.vector.max_index(index[:, 0:8], best[:, 0:8], vals)),
                            lambda: rt.link(nc.vector.max(best[:, 8:16], spare)),
                            lambda: rt.link(nc.vector.max_index(index[:, 8:16], best[:, 8:16], spare)),
                        ]

                    kk = [P, TOPK, TOPK]
                    k2 = [P, 2, TOPK, TOPK]
                    steps = [lambda: rt.link(nc.vector.tensor_copy(
                        r_s[:].rearrange("p a n -> p (a n)"), big[:, i + S0]))]
                    for p in range(2):
                        steps += top16(r_s[:, p], r_s2[:, p], r_v[:, p], r_i[:, p])
                    steps += [
                        lambda: rt.link(nc.vector.tensor_copy(r_if[:], r_i[:])),
                        lambda: rt.link(nc.vector.tensor_tensor(
                            r_c[:].rearrange("p (a b) -> p a b", a=TOPK), r_v[:, 0].unsqueeze(2).broadcast_to(kk),
                            r_v[:, 1].unsqueeze(1).broadcast_to(kk), ALU.add)),
                    ]
                    steps += top16(r_c[:], r_c2[:], r_best[:], r_pos[:])
                    steps += [
                        lambda: rt.link(nc.vector.tensor_scalar(r_ab[:, 0], r_pos[:], 4, None, ALU.logical_shift_right)),
                        lambda: rt.link(nc.vector.tensor_scalar(r_ab[:, 1], r_pos[:], 15, None, ALU.bitwise_and)),
                        lambda: rt.link(nc.vector.tensor_copy(r_abf[:], r_ab[:])),
                        lambda: rt.link(nc.vector.tensor_tensor(
                            r_eq[:], r_abf[:].unsqueeze(3).broadcast_to(k2),
                            iota[:, :TOPK].unsqueeze(1).unsqueeze(1).broadcast_to(k2), ALU.is_equal)),
                        lambda: rt.link(nc.vector.tensor_tensor(
                            r_eq[:], r_eq[:], r_if[:].unsqueeze(2).broadcast_to(k2), ALU.mult)),
                        lambda: rt.link(nc.vector.tensor_reduce(
                            picks[:, 0:2].rearrange("p a t (h k) -> p a (t h) k", k=TOPK)[:, :, i], r_eq[:], AX.X, ALU.add)),
                        lambda: rt.link(nc.vector.tensor_scalar(
                            picks[:, 2].rearrange("p t (h k) -> p (t h) k", k=TOPK)[:, i], r_best[:],
                            r_best[:, 0:1], None, ALU.subtract)),
                    ]
                    cuts = [round(len(steps) * e / 8) for e in range(9)]
                    for e in range(8):
                        n = T_U + e + AHEAD
                        split_lo(l, (i * 2 + n // SLOTS), n % SLOTS)
                        for s in steps[cuts[e]:cuts[e + 1]]:
                            s()
                    rt.end()

                nc.vector.tensor_copy(gsum[:, 0:1], gsum[:, 0:1]).then_inc(best_ready, 1)
                dve.wait_ge(gate_exp, l + 1)
                g = picks[:, 2].rearrange("p t (h k) -> p (t h) k", k=TOPK)
                st.link(nc.vector.tensor_reduce(gsum[:], g, AX.X, ALU.add))
                st.link(nc.vector.reciprocal(gsum[:], gsum[:]))
                nc.vector.tensor_tensor(g, g, gsum[:].unsqueeze(2).broadcast_to([P, TT * HEADS, TOPK]),
                                        ALU.mult).then_inc(picks_ready, 1)
                tr_copy(l, X_PK + 1, picksT[:, 2], tr[:, 1, :SEQ])
                for b in range(2):
                    dve.wait_ge(tr_read[b], OPEN + l * (NTR // 2) + NTR // 2)
                dve.sem_inc(apart, 1)

                with dve.Fori(0, SEQ // 8) as i:
                    for e in range(2):
                        dve.wait_ge(acc_ready, l * NREADY + R_G - 1 + (i * 2 + e))
                        for r in range(4):
                            tok = i * 8 + (4 * e + r)
                            nc.vector.tensor_scalar(hot_i[:, e, r], iota[:], picksT[:, 0, bass.ds(tok, 1)], None, ALU.is_equal)
                            ins = nc.vector.tensor_scalar(hot_j[:, e, r], iota[:], picksT[:, 1, bass.ds(tok, 1)],
                                                          picksT[:, 2, bass.ds(tok, 1)], ALU.is_equal, ALU.mult)
                        ins.then_inc(hot_ready, 1)
                    for e in range(2):
                        dve.wait_ge(acc_ready, l * NREADY + R_G + 1 + (i * 2 + e))
                        part = big[:, :, bass.ds(i * 8 + 4 * e, 4)].rearrange("p j t -> p t j")
                        nc.vector.tensor_tensor(part, acc[:, e].rearrange("p (t j) -> p t j", t=4), part,
                                                ALU.mult).then_inc(acc_read[e], 1)

                def split_w_lo(nth, j, s):
                    dve.wait_ge(w_hi_done, l * NKEYS + nth + 1)
                    nc.vector.tensor_tensor(w_lo[:, s], big[:, j], w_hi[:, s].bitcast(F32), ALU.subtract).then_inc(w_lo_done, 1)

                for b in range(2):
                    dve.wait_ge(acc_read[b], OPEN + l * (NACC // 2) + NACC // 2)
                for j in range(AHEAD):
                    split_w_lo(j, j, j)
                with dve.Fori(0, NKEYS // SLOTS - 1) as i:
                    for e in range(SLOTS):
                        n = T_V + e + AHEAD
                        split_lo(l, (i + n // SLOTS), n % SLOTS)
                        j = i * SLOTS + (e + AHEAD)
                        split_w_lo(j, j, n % SLOTS)
                split_lo(l, TURNS - 1, SLOTS - 1)
                split_w_lo(NKEYS - 1, NKEYS - 1, SLOTS - 1)
                layer_norm(None, add_branch(NT - 1, W_V), 3 * l + 3, l * 64 + 96, st)
                st.end()

        @block.tensor
        def _(pe_):
            mm = nc.tensor.matmul

            def tile_ready(l, q, s):
                pe_.wait_ge(lo_done, l * NT + q * SLOTS + s + 1)

            def acc_free(l, use):
                pe_.wait_ge(acc_read[use % 2], OPEN + l * (NACC // 2) + use // 2)

            def tr_free(l, use):
                pe_.wait_ge(tr_read[use % 2], OPEN + l * (NTR // 2) + use // 2)

            def wide_free(l, use):
                for tt in range(TT):
                    pe_.wait_ge(wide_read[tt], OPEN + l * NWIDE + use)

            def columns_tile(s, xh, xl, bank):
                for k in range(DK):
                    c = slice(k * P, (k + 1) * P)
                    dst = acc[:, bank, :SEQ]
                    mm(dst, lo[:, s, c], xh[:, k], start=k == 0, stop=False)
                    mm(dst, hi[:, s, c], xl[:, k], start=False, stop=False)
                    ins = mm(dst, hi[:, s, c], xh[:, k], start=False, stop=k == DK - 1)
                ins.then_inc(slot_free[s], 1)

            def rows_tile(s, ah, al, first, last, width, offsets, wide_at=0, rows=slice(0, 1024), release=True):
                for tt in range(TT):
                    tok = slice(tt * P, (tt + 1) * P)
                    for k, (a, w) in enumerate(((al, hi), (ah, lo), (ah, hi))):
                        for h, off in enumerate(offsets):
                            ins = mm(wide[:, tt, 512 * h:512 * h + width], a[:, tok], w[:, s, off:off + width],
                                     start=first and k == 0, stop=last and k == 2)
                ins.then_inc(slot_free[s], 1)

            for free in (*acc_read, *tr_read, *wide_read):
                pe_.sem_inc(free, OPEN)
            pe_.wait_ge(consts_ready, 1)
            with pe_.Fori(0, DEPTH) as l:
                def transpose_x(first, nth):
                    for g in range(4):
                        tt, cg = divmod(g, 2)
                        pe_.wait_ge(x_ready, nth + tt + 1)
                        tr_free(l, first + g)
                        for c in range(4):
                            ins = nc.tensor.transpose(tr[:, (first + g) % 2, c * P:(c + 1) * P],
                                                      xs[:, tt, (4 * cg + c) * P:(4 * cg + c + 1) * P], ident[:])
                        ins.then_inc(tr_ready, 1)

                def xT_written(first):
                    for b in range(2):
                        pe_.wait_ge(tr_read[b], OPEN + l * (NTR // 2) + first // 2 + 2)

                transpose_x(X_XT, l * 4)
                xT_written(X_XT)
                for c in range(N_LAT):
                    n = T_LAT + c
                    acc_free(l, A_LAT + c)
                    tile_ready(l, n // SLOTS, n % SLOTS)
                    columns_tile(n % SLOTS, xT_hi, xT_lo, c % 2)
                pe_.wait_ge(sq_done, l * N_LAT + N_LAT)
                for b, chunks in enumerate((range(0, 6), range(6, 8))):
                    acc_free(l, A_RMS + b)
                    for tt in range(TT):
                        for c in chunks:
                            ins = mm(acc[:, b, tt:tt + 1], sq[:, c, tt * P:(tt + 1) * P], ones[:, 0:1],
                                     start=c == chunks[0], stop=c == chunks[-1])
                    ins.then_inc(acc_ready, 1)
                wide_free(l, W_UQ)
                for c in range(N_UQ):
                    n = T_UQ + c
                    pe_.wait_ge(lat_ready, OPEN + l * N_LAT + c + 1)
                    tile_ready(l, n // SLOTS, n % SLOTS)
                    rows_tile(n % SLOTS, cq_hi[:, c], cq_lo[:, c], c == 0, c == N_UQ - 1, 384, (0, 384))
                wide_free(l, W_UKV)
                for c in range(N_UKV):
                    n = T_UKV + c
                    pe_.wait_ge(lat_ready, OPEN + l * N_LAT + N_UQ + c + 1)
                    tile_ready(l, n // SLOTS, n % SLOTS)
                    rows_tile(n % SLOTS, cq_hi[:, 6 + c], cq_lo[:, 6 + c], c == 0, c == 1, 512, (0, 512))
                for b in range(2):
                    acc_free(l, A_B + b)
                for q in range(N_B):
                    n = T_B + q
                    tile_ready(l, n // SLOTS, n % SLOTS)
                    s = n % SLOTS
                    for kk in range(2):
                        k = 2 * q + kk
                        c = slice(kk * WB, (kk + 1) * WB)
                        for tt in range(TT):
                            tok = slice(tt * P, (tt + 1) * P)
                            dst = acc[:, tt, :WB]
                            mm(dst, xT_lo[:, k, tok], hi[:, s, c], start=k == 0, stop=False)
                            mm(dst, xT_hi[:, k, tok], lo[:, s, c], start=False, stop=False)
                            ins = mm(dst, xT_hi[:, k, tok], hi[:, s, c], start=False, stop=k == DK - 1)
                    ins.then_inc(slot_free[s], 1)
                wide_free(l, W_A)
                for k in range(N_A):
                    n = T_A + k
                    tile_ready(l, n // SLOTS, n % SLOTS)
                    rows_tile(n % SLOTS, xT_hi[:, k], xT_lo[:, k], k == 0, k == N_A - 1, 512, (0, 512))

                def transpose_heads(use, sources, rows):
                    tr_free(l, use)
                    pe_.sem_inc(apart, 1)
                    for j, src in enumerate(sources):
                        ins = nc.tensor.transpose(tr[:rows, use % 2, j * P:(j + 1) * P], src, ident[:])
                    ins.then_inc(tr_ready, 1)

                pe_.wait_ge(tok_ready, l * TT + TT)
                for use, src in ((X_Q, q_tok), (X_K, k_tok)):
                    for g in range(4):
                        tt, hg = divmod(g, 2)
                        transpose_heads(use + g, [src[:, tt, 4 * hg + j] for j in range(4)], QKD)
                for g in range(4):
                    tt, hg = divmod(g, 2)
                    transpose_heads(X_NQ + g, [rot[:, tt, 4 * hg + j] for j in range(4)], HD)
                for tt in range(TT):
                    transpose_heads(X_KT + tt, [rot[:, tt, HEADS + GROUPS + j] for j in range(4)], HD)
                for tt in range(TT):
                    transpose_heads(X_CD + tt, [cmp_tok[:, tt, c, g].rearrange("p a d -> p (a d)")
                                                for c in range(2) for g in range(GROUPS)], P)
                pe_.wait_ge(blk_ready, l * 8 + 8)
                acc_free(l, A_HID)
                nb = GROUPS * NCMP
                for c in range(2):
                    for r in range(16):
                        ins = mm(acc[:, A_HID % 2, c * nb:(c + 1) * nb], w1[:, c, r], blk[:, c, r], start=r == 0, stop=r == 15)
                ins.then_inc(acc_ready, 1)
                pe_.wait_ge(acc_read[A_HID % 2], OPEN + l * (NACC // 2) + A_HID // 2 + 1)
                acc_free(l, A_KCVC)
                b = A_KCVC % 2
                mm(acc[:HD, b, 0:nb], w2[:, 0], hid[:, 0], start=True, stop=True)
                for g in range(GROUPS):
                    ins = mm(acc[:NCMP, b, 64 + g * HD:64 + (g + 1) * HD], hid[:, 1, g * NCMP:(g + 1) * NCMP], w2[:, 1],
                             start=True, stop=True)
                ins.then_inc(acc_ready, 1)
                pe_.wait_ge(acc_read[b], OPEN + l * (NACC // 2) + A_KCVC // 2 + 1)
                for tt in range(TT):
                    acc_free(l, A_CS + tt)
                    for h in range(HEADS):
                        g = h // 4
                        ins = mm(acc[:, (A_CS + tt) % 2, h * 16:h * 16 + NCMP], nqT[:, h, tt * P:(tt + 1) * P],
                                 kc[:, g * NCMP:(g + 1) * NCMP], start=True, stop=True)
                    ins.then_inc(acc_ready, 1)
                for tt in range(TT):
                    pe_.wait_ge(cmp_ready, l * TT + tt + 1)
                    for hg in range(2):
                        transpose_heads(X_PC + 2 * tt + hg, [cs[:, tt, 4 * hg + j, :NCMP] for j in range(4)], NCMP)

                def scores(u):
                    kind, hg, tt, oi, trs = unit(u)
                    keys_n = (tt + 1) * P
                    pe_.wait_ge(wide_read[u % 2], OPEN + l * NWIDE + W_AT + u // 2)
                    for h in range(4):
                        dst = wide[:, u % 2, 256 * h:256 * h + keys_n]
                        tok = slice(tt * P, (tt + 1) * P)
                        if kind == "mla":
                            ins = mm(dst, qT[:QKD, 4 * hg + h, tok], kT[:QKD, 4 * hg + h, :keys_n], start=True, stop=True)
                        else:
                            kk = nkT[:, (0 if kind == "sel" else GROUPS) + hg, :keys_n]
                            ins = mm(dst, nqT[:, 4 * hg + h, tok], kk, start=True, stop=True)
                    ins.then_inc(wide_ready, 1)

                def transpose_p(u):
                    kind, hg, tt, oi, trs = unit(u)
                    pe_.wait_ge(p_ready, l * NU + u + 1)
                    for kb, use in enumerate(trs):
                        transpose_heads(use, [sc[:, u % 2, h, kb * P:(kb + 1) * P] for h in range(4)], P)

                def outputs(u):
                    kind, hg, tt, oi, trs = unit(u)
                    bank = oi % 2
                    first = kind != "win"
                    if first:
                        acc_free(l, A_O + oi)
                    if kind == "sel":
                        if hg == 0:
                            for b in range(2):
                                pe_.wait_ge(tr_read[b], OPEN + l * (NTR // 2) + X_PC // 2 + tt + 1)
                        for h in range(4):
                            mm(acc[:, bank, h * HD:(h + 1) * HD], pcT[:NCMP, 4 * hg + h, tt * P:(tt + 1) * P], vc[:NCMP, hg],
                               start=first, stop=False, skip_group_check=True)
                            first = False
                    for kb, use in enumerate(trs):
                        pe_.wait_ge(tr_read[use % 2], OPEN + l * (NTR // 2) + use // 2 + 1)
                    for h in range(4):
                        for kb in range(tt + 1):
                            if kind == "mla":
                                v = v_mla[:, kb, 4 * hg + h]
                            else:
                                v = (v_sel if kind == "sel" else v_win)[:, kb, hg * HD:(hg + 1) * HD]
                            ins = mm(acc[:, bank, h * HD:(h + 1) * HD], pT[:, u % 2, kb, h * P:(h + 1) * P], v,
                                     start=first, stop=kind != "sel" and h == 3 and kb == tt, skip_group_check=True)
                            first = False
                    if kind != "sel":
                        ins.then_inc(acc_ready, 1)

                scores(0)
                for u in range(NU):
                    if u + 1 < NU:
                        scores(u + 1)
                    transpose_p(u)
                    if u >= 1:
                        outputs(u - 1)
                outputs(NU - 1)
                for b in range(2):
                    pe_.wait_ge(acc_read[b], OPEN + l * (NACC // 2) + A_MG // 2)
                for g in range(4):
                    kind, tt = divmod(g, 2)
                    transpose_heads(X_OT + g, [o_tok[:, tt, kind, c * P:(c + 1) * P] for c in range(4)], P)
                with pe_.Fori(0, N_MG // SLOTS) as i:
                    for e in range(SLOTS):
                        s, q = (T_MG + e) % SLOTS, (T_MG + e) // SLOTS
                        pe_.wait_ge(acc_read[e % 2], OPEN + l * (NACC // 2) + (i * 2 + (A_MG + e) // 2))
                        tile_ready(l, (i + q), s)
                        columns_tile(s, xT_hi, xT_lo, e % 2)
                for b in range(2):
                    pe_.wait_ge(tr_read[b], OPEN + l * (NTR // 2) + X_OT // 2 + 2)
                for c in range(N_BR):
                    n = T_BR + c
                    s = n % SLOTS
                    acc_free(l, A_BR + c)
                    tile_ready(l, n // SLOTS, s)
                    for f in range(2):
                        for k in range(4):
                            w = slice(k * 256 + f * P, k * 256 + f * P + P)
                            dst = acc[:, c % 2, f * SEQ:(f + 1) * SEQ]
                            mm(dst, lo[:, s, w], oT_hi[:, c % 2, k], start=k == 0, stop=False)
                            mm(dst, hi[:, s, w], oT_lo[:, c % 2, k], start=False, stop=False)
                            ins = mm(dst, hi[:, s, w], oT_hi[:, c % 2, k], start=False, stop=k == 3)
                    ins.then_inc(slot_free[s], 1)
                wide_free(l, W_OUT)
                for k in range(N_OUT):
                    n = T_OUT + k
                    pe_.wait_ge(mixed_ready, OPEN + l * 4 + k // 2 + 1)
                    tile_ready(l, n // SLOTS, n % SLOTS)
                    rows_tile(n % SLOTS, xT_hi[:, k], xT_lo[:, k], k == 0, k == N_OUT - 1, 512, (0, 512))
                transpose_x(X_XT2, l * 4 + 2)
                xT_written(X_XT2)
                pe_.sem_inc(apart, 1)
                with pe_.Fori(0, N_PQ // SLOTS) as i:
                    for e in range(SLOTS):
                        s, q = (T_PQ + e) % SLOTS, (T_PQ + e) // SLOTS
                        pe_.wait_ge(acc_read[e % 2], OPEN + l * (NACC // 2) + (i * 2 + (A_PQ + e) // 2))
                        tile_ready(l, (i + q), s)
                        columns_tile(s, xT_hi, xT_lo, e % 2)
                pe_.wait_ge(keys_loaded, l * 16 + 16)
                for b in range(2):
                    pe_.wait_ge(acc_read[b], OPEN + l * (NACC // 2) + A_SCR // 2)
                for c in range(4):
                    for p in range(2):
                        acc_free(l, A_SCR + 2 * c + p)
                        rows = slice(p * HD, (p + 1) * HD)
                        for r in range(4):
                            tt, h = divmod(4 * c + r, HEADS)
                            ins = mm(acc[:, p, r * P:(r + 1) * P], pqT[rows, h, tt * P:(tt + 1) * P], keys[rows, h],
                                     start=True, stop=True)
                        ins.then_inc(acc_ready, 1)
                with pe_.Fori(0, NKEYS // 8) as i:
                    for e in range(8):
                        s, q = (T_U + e) % SLOTS, (T_U + e) // SLOTS
                        pe_.wait_ge(acc_read[e % 2], OPEN + l * (NACC // 2) + (i * 4 + (A_U + e) // 2))
                        tile_ready(l, (i * 2 + q), s)
                        columns_tile(s, xT_hi, xT_lo, e % 2)
                pe_.wait_ge(picks_ready, l + 1)
                transpose_heads(X_PK, [picks[:, a, tt] for a in range(2) for tt in range(TT)], P)
                transpose_heads(X_PK + 1, [picks[:, 2, tt] for tt in range(TT)], P)
                with pe_.Fori(0, SEQ // 8) as i:
                    for e in range(2):
                        pe_.wait_ge(acc_read[e], OPEN + l * (NACC // 2) + (i + A_G // 2))
                        pe_.wait_ge(hot_ready, l * 64 + (i * 2 + (e + 1)))
                        for r in range(4):
                            ins = mm(acc[:, e, r * P:(r + 1) * P], hot_i[:, e, r], hot_j[:, e, r], start=True, stop=True)
                        ins.then_inc(acc_ready, 1)
                wide_free(l, W_V)
                pe_.sem_inc(apart, 1)

                def v_tile(i, e, first, last):
                    s, q = (T_V + e) % SLOTS, (T_V + e) // SLOTS
                    pe_.wait_ge(w_lo_done, l * NKEYS + (i * SLOTS + (e + 1)))
                    tile_ready(l, (i + q), s)
                    rows_tile(s, w_hi[:, s], w_lo[:, s], first, last, 512, (0, 512))

                for e in range(SLOTS):
                    v_tile(0, e, e == 0, False)
                with pe_.Fori(1, NKEYS // SLOTS - 1) as i:
                    for e in range(SLOTS):
                        v_tile(i, e, False, False)
                for e in range(SLOTS):
                    v_tile(NKEYS // SLOTS - 1, e, False, e == SLOTS - 1)


DVE_STEPS = 8 + 1 + 8 + 10 + 8 + 1 + 2 + 8 + 12 + 8 + 8 + 10 + 2 + 10
ROUTE_STEPS = 1 + 10 + 2 + 5 + 7


def lay_out(a):
    L = DEPTH
    w_in = a["w_in"]

    def columns(w, first, width=P):
        part = w[:, first:first + width]
        return part.reshape(-1, P, width).transpose(1, 0, 2).reshape(P, -1)

    front = np.zeros((L, FRONT, P, 1024), np.float32)
    for l in range(L):
        w = w_in[l]
        wa = np.concatenate([w[:, c:c + n] for c, n in COLS_A], axis=1)
        wb = np.concatenate([w[:, c:c + n] for c, n in COLS_B], axis=1)
        for c in range(N_LAT):
            front[l, T_LAT + c] = columns(w, c * P)
        for c in range(N_UQ):
            front[l, T_UQ + c, :, :HEADS * QKD] = a["mla_w_uq"][l, c * P:(c + 1) * P]
        for c in range(N_UKV):
            front[l, T_UKV + c] = a["mla_w_ukv"][l, c * P:(c + 1) * P]
        for q in range(N_B):
            front[l, T_B + q, :, :2 * WB] = columns(wb[q * 2 * P:(q + 1) * 2 * P], 0, WB)
        for k in range(N_A):
            front[l, T_A + k] = wa[k * P:(k + 1) * P]
        for c in range(N_MG):
            front[l, T_MG + c] = columns(w, C_MG + c * P)
        for q in range(4):
            front[l, T_BR + 2 * q] = columns(a["w_branch_mla"][l], q * 256, 256)
            front[l, T_BR + 2 * q + 1] = columns(a["w_branch_nsa"][l], q * 256, 256)
        for k in range(N_OUT):
            front[l, T_OUT + k] = a["w_out"][l, k * P:(k + 1) * P]
        for h in range(N_PQ):
            front[l, T_PQ + h] = columns(a["peer_w_query"][l], h * P)

    def odd_even(x, width):
        return x.reshape(L, 16, 2, HD, width).transpose(0, 2, 3, 1, 4).reshape(L, P, 16, width)

    got = {
        "x": a["x"].reshape(TT, P, D).transpose(1, 0, 2),
        "positions": a["positions"].reshape(TT, P).T,
        "freq": np.concatenate([10000.0 ** (-np.arange(0, d, 2, dtype=np.float64) / d) for d in (ROPE, HD)]).astype(np.float32),
        "ln": np.stack([np.stack([a["ln_in_g"], a["ln_in_b"]])] + [
            np.stack([a[f"ln{i}_g"][l], a[f"ln{i}_b"][l]]) for l in range(L) for i in (1, 2)]),
        "front": front,
        "lat_g": np.concatenate([a["mla_q_norm"], a["mla_kv_norm"]], axis=1).reshape(L, 8, P).transpose(0, 2, 1),
        "cmp_pe": np.stack([odd_even(a["nsa_cmp_k_pe"], 1)[..., 0], odd_even(a["nsa_cmp_v_pe"], 1)[..., 0]], axis=2),
        "cmp_w1": np.stack([odd_even(a["nsa_cmp_k_w1"], P), odd_even(a["nsa_cmp_v_w1"], P)], axis=2),
        "cmp_w2": np.stack([a["nsa_cmp_k_w2"], a["nsa_cmp_v_w2"]], axis=2),
        "sub_keys": a["peer_sub_keys"].transpose(0, 2, 4, 1, 3).reshape(L, P, HEADS, NKEYS),
        "peer_u": a["peer_u"].reshape(L, P, NKEYS, DK, P).transpose(0, 2, 4, 3, 1).reshape(L, NKEYS, P, 1024),
        "peer_v": a["peer_v"].reshape(L, P, NKEYS, D).transpose(0, 2, 1, 3),
    }
    got["positions"] = got["positions"].astype(np.int32)
    return {k: np.ascontiguousarray(v) for k, v in got.items()}


def kernel(**inputs):
    import concourse.bacc as bacc
    from concourse.bass_utils import run_bass_kernel_spmd

    arrays = lay_out({k: np.asarray(v) for k, v in inputs.items()})
    nc = bacc.Bacc("TRN2", target_bir_lowering=False, num_devices=1)
    t = {k: nc.dram_tensor(f"in_{k}", v.shape, mybir.dt.from_np(v.dtype), kind="ExternalInput").ap()
         for k, v in arrays.items()}
    out = nc.dram_tensor("out_0", (P, TT, D), F32, kind="ExternalOutput").ap()
    build(nc, t, out)
    r = run_bass_kernel_spmd(nc, [{f"in_{k}": v for k, v in arrays.items()}], core_ids=[0])
    return r.results[0]["out_0"].transpose(1, 0, 2).reshape(1, SEQ, D)
```

```python
from contextlib import ExitStack

import numpy as np

import concourse.bass as bass
from concourse import mybir

F32 = mybir.dt.float32
F32R = mybir.dt.float32r
I32 = mybir.dt.int32
U32 = mybir.dt.uint32
ALU = mybir.AluOpType
ACT = mybir.ActivationFunctionType
AX = mybir.AxisListType

P = 128
SEQ, D, DEPTH = 256, 1024, 2
TT = SEQ // P
DK = D // P
HEADS = 8
NOPE, ROPE, VDIM = 64, 32, 64
QKD = NOPE + ROPE
Q_RANK, KV_RANK = 768, 256
HD = 64
GROUPS = 2
CMP_BLOCK, CMP_STRIDE = 32, 16
NCMP = (SEQ - CMP_BLOCK) // CMP_STRIDE + 1
NKEYS, TOPK = 128, 16
ALPHA = (2 * DEPTH) ** 0.25
LN_EPS, RMS_EPS, NEG = 1e-5, 1e-6, -1e30
MLA_SCALE, NSA_SCALE = QKD ** -0.5, HD ** -0.5
LOWEST = -3.0e38
TWO_PI = 2 * np.pi
PI_A = 6.28125
PI_B = np.round((TWO_PI - PI_A) * 2.0 ** 20) / 2.0 ** 20
PI_C = float(np.float32(TWO_PI - PI_A - PI_B))
ROUND = 12582912.0

C_KR = Q_RANK + KV_RANK
C_NQ = C_KR + ROPE
C_KV = C_NQ + HEADS * HD
C_NG = C_KV + 6 * GROUPS * HD
C_MG = C_NG + 3 * HEADS
GW = GROUPS * HD
COLS_A = [(C_NQ, 512), (C_KV, GW), (C_KV + 2 * GW, GW), (C_KV + 4 * GW, GW), (C_KV + 5 * GW, GW)]
ROT = HEADS + 3 * GROUPS
COLS_B = [(C_KV + GW, GW), (C_KV + 3 * GW, GW), (C_KR, ROPE), (C_NG, 3 * HEADS)]
WB = 2 * GW + ROPE + 3 * HEADS

SLOTS = 4
N_LAT, N_UQ, N_UKV, N_B, N_A, N_MG, N_BR, N_OUT, N_PQ = 8, 6, 2, 4, 8, 16, 8, 8, 8
MG_EARLY = 2
T_LAT = 0
T_UQ = T_LAT + N_LAT
T_B = T_UQ + N_UQ
T_UKV = T_B + N_B
T_MG = T_UKV + N_UKV
T_A = T_MG + MG_EARLY
T_MG2 = T_A + N_A
T_BR = T_MG2 + N_MG - MG_EARLY
MG_TILE = [T_MG + c for c in range(MG_EARLY)] + [T_MG2 + c for c in range(N_MG - MG_EARLY)]
T_OUT = T_BR + N_BR
T_PQ = T_OUT + N_OUT
FRONT = T_PQ + N_PQ
T_U = FRONT
T_V = T_U + NKEYS
NT = T_V + NKEYS
TURNS = NT // SLOTS
AHEAD = 3
assert NT % SLOTS == 0 and FRONT % SLOTS == 0

A_LAT, A_RMS, A_B, A_HID, A_KCVC, A_CS, A_ATT, A_BR, A_PQ, A_SCR, A_U, A_G = (
    0, 8, 10, 16, 18, 20, 24, 40, 48, 56, 64, 192)
ATT_ORDER = "F0 F1 O0 F2 O1 F3 O2 F4 F5 O3 F6 F7 O4 O5 O6 O7".split()
O_USE = [A_ATT + ATT_ORDER.index(f"O{k}") for k in range(8)]
MG_USE = [12, 13, 14, 15, 17, 19, 22, 23] + [A_ATT + ATT_ORDER.index(f"F{k}") for k in range(8)]
NACC = 256
R_RMS, R_HID, R_KCVC, R_CS, R_O, R_SCR, R_G = 0, 2, 3, 4, 6, 14, 22
NREADY = R_G + SEQ // 4
NG = SEQ // 4
HOTS = 4
X_XT, X_Q, X_K, X_NQ, X_KT, X_CD, X_PC, X_AT, X_OT, X_XT2, X_PK = 0, 4, 8, 12, 16, 18, 20, 24, 42, 46, 50
NTR = 52
W_UQ, W_UKV, W_A, W_OUT, W_V = range(5)
NWIDE = 5
OPEN = 1
UNITS = [("mla", 0), ("mla", 1), ("sel", 0), ("win", 0), ("sel", 1), ("win", 1)]
NU = len(UNITS) * TT
O_OF = [0, 1, 2, 2, 3, 3]


def unit(u):
    tt, i = divmod(u, len(UNITS))
    kind, hg = UNITS[i]
    tr = [X_AT + u] if tt == 0 else [X_AT + 6 + 2 * (u - 6), X_AT + 7 + 2 * (u - 6)]
    return kind, hg, tt, tt * 4 + O_OF[i], tr


class Steps:

    def __init__(self, eng, sem, base, per_pass, apart=None):
        self.eng, self.sem, self.base, self.per_pass, self.n = eng, sem, base, per_pass, 0
        self.apart = apart

    def link(self, ins):
        ins.then_inc(self.sem, 1)
        self.n += 1
        self.eng.wait_ge(self.sem, self.base + self.n)
        if self.apart is not None:
            self.eng.sem_inc(self.apart, 1)

    def mark(self, ins):
        ins.then_inc(self.sem, 1)
        self.n += 1

    def settle(self):
        self.eng.wait_ge(self.sem, self.base + self.n)
        if self.apart is not None:
            self.eng.sem_inc(self.apart, 1)

    def end(self):
        assert self.n == self.per_pass, (self.n, self.per_pass)


def build(nc, t, out):
    with ExitStack() as ctx:
        def sem(name):
            return ctx.enter_context(nc.semaphore(name))

        base = 16512

        def at(name, shape, dt, offset):
            return nc.alloc_sbuf_tensor_at(name, shape, dt, offset=base + offset)

        K = 1024
        big = at("big", [P, NKEYS, SEQ], F32, 0)
        cq_hi = at("cq_hi", [P, 8, SEQ], F32R, 0)
        cq_lo = at("cq_lo", [P, 8, SEQ], F32R, 8 * K)
        oT_hi = at("oT_hi", [P, 2, 4, SEQ], F32R, 0)
        oT_lo = at("oT_lo", [P, 2, 4, SEQ], F32R, 8 * K)
        pqT = at("pqT", [P, HEADS, SEQ], F32, 0)
        q_tok = at("q_tok", [P, TT, HEADS, QKD], F32, 16 * K)
        k_tok = at("k_tok", [P, TT, HEADS, QKD], F32, 22 * K)
        v_mla = at("v_mla", [P, TT, HEADS, VDIM], F32, 28 * K)
        o_tok = at("o_tok", [P, TT, 2, 512], F32, 16 * K)
        keys = at("keys", [P, HEADS, NKEYS], F32, 24 * K)
        qT = at("qT", [P, HEADS, SEQ], F32, 32 * K)
        kT = at("kT", [P, HEADS, SEQ], F32, 40 * K)
        ln_par = at("ln_par", [P, 2, D], F32, 40 * K)
        rot = at("rot", [P, TT, ROT, HD], F32, 48 * K)
        mix_a = at("mix_a", [P, 512], F32, 48 * K)
        mix_b = at("mix_b", [P, 512], F32, 50 * K)
        v_win = at("v_win", [P, TT, GW], F32, 55 * K)
        v_sel = at("v_sel", [P, TT, GW], F32, 56 * K)
        cmp_tok = at("cmp_tok", [P, TT, 2, GROUPS, 2, HD], F32, 57 * K)
        rope_a = at("rope_a", [P, ROT * HD], F32, 61 * K)
        rope_b = at("rope_b", [P, ROT * HD], F32, 61 * K + 3584)
        lat = at("lat", [P, SEQ], F32, 61 * K)
        nqT = at("nqT", [HD, HEADS, SEQ], F32, 68 * K)
        nkT = at("nkT", [HD, 4, SEQ], F32, 76 * K)
        cmpT = at("cmpT", [P, 4, SEQ], F32, 80 * K)
        blk = at("blk", [P, 2, 16, GROUPS * NCMP], F32, 84 * K)
        w1 = at("w1", [P, 2, 16, P], F32, 0)
        gates = at("gates", [P, 16, SEQ], F32, 88 * K)
        sq = at("sq", [P, 8, SEQ], F32, 104 * K)
        sc = at("sc", [P, 2, 4, SEQ], F32, 104 * K)
        pT = at("pT", [P, 2, 2, 512], F32, 112 * K)
        pcT = at("pcT", [16, HEADS, SEQ], F32, 120 * K)
        S0 = NKEYS - 16
        o = 128 * K
        xs = at("xs", [P, TT, D], F32, o)
        xT_hi = at("xT_hi", [P, DK, SEQ], F32R, o + 8 * K)
        xT_lo = at("xT_lo", [P, DK, SEQ], F32R, o + 16 * K)
        hot_i = at("hot_i", [P, HOTS, 4, P], F32, o + 8 * K)
        hot_j = at("hot_j", [P, HOTS, 4, P], F32, o + 16 * K)
        w_hi = at("w_hi", [P, SLOTS, SEQ], F32R, o + 16 * K)
        w_lo = at("w_lo", [P, SLOTS, SEQ], F32R, o + 20 * K)
        raw = at("raw", [P, SLOTS, 1024], F32, o + 24 * K)
        lo = at("lo", [P, SLOTS, 1024], F32R, o + 24 * K)
        hi = at("hi", [P, SLOTS, 1024], F32R, o + 40 * K)
        o += 56 * K
        where = [o]

        def small(name, shape, dt=F32):
            size = int(np.prod(shape[1:])) * 4
            got = at(name, shape, dt, where[0])
            where[0] += (size + 31) // 32 * 32
            assert base + where[0] <= 229344
            return got

        ident = small("ident", [P, P])
        iota = small("iota", [P, P])
        causal = small("causal", [P, P])
        ident_r = small("ident_r", [P, P], F32R)
        causal_r = small("causal_r", [P, P], F32R)
        cmask = small("cmask", [P, TT, NCMP])
        cmask01 = small("cmask01", [P, TT, NCMP])
        cos_m = small("cos_m", [P, TT, ROPE])
        sin_m = small("sin_m", [P, TT, ROPE])
        cos_n = small("cos_n", [P, TT, HD])
        sin_n = small("sin_n", [P, TT, HD])
        ones = small("ones", [P, 2])
        neg_half = small("neg_half", [P, 4])
        picks = small("picks", [P, 3, TT, P])
        picksT = small("picksT", [P, 3, SEQ])
        r_s = small("r_s", [P, 2, NKEYS])
        r_s2 = small("r_s2", [P, 2, NKEYS])
        r_v = small("r_v", [P, 2, TOPK])
        r_i = small("r_i", [P, 2, TOPK], U32)
        r_if = small("r_if", [P, 2, TOPK])
        r_c = small("r_c", [P, TOPK * TOPK])
        r_c2 = small("r_c2", [P, TOPK * TOPK])
        r_best = small("r_best", [P, TOPK])
        r_pos = small("r_pos", [P, TOPK], U32)
        r_ab = small("r_ab", [P, 2, TOPK], U32)
        r_abf = small("r_abf", [P, 2, TOPK])
        r_eq = small("r_eq", [P, 2, TOPK, TOPK])
        gsum = small("gsum", [P, TT * HEADS])
        stats = small("stats", [P, TT, 2, 6])
        mv = small("mv", [P, TT, 2])
        var = small("var", [P, 4])
        rstd = small("rstd", [P, 4])
        ngate = small("ngate", [P, TT, 3 * HEADS])
        kr = small("kr", [P, 3, ROPE])
        negmax = small("negmax", [P, 2, 4])
        sums = small("sums", [P, 2, 4])
        recip = small("recip", [P, 2, 4])
        cs = small("cs", [P, TT, HEADS, 16])
        cst = small("cst", [P, TT, 3, HEADS])
        lat_g = small("lat_g", [P, 8])
        pe = small("pe", [P, 2, 16])
        w2 = small("w2", [P, 2, HD])
        hid = small("hid", [P, 2, GROUPS * NCMP])
        kc = small("kc", [HD, GROUPS * NCMP])
        vc = small("vc", [16, GROUPS, HD])
        pos_i = small("pos_i", [P, TT], I32)
        pos_f = small("pos_f", [P, TT])
        freq = small("freq", [P, 48])
        ang = at("ang", [P, 4, TT, 48], F32, 0)
        warm = small("warm", [P, 2])

        acc = ctx.enter_context(nc.psum_tensor("acc", [P, 2, 512], F32))
        tr = ctx.enter_context(nc.psum_tensor("tr", [P, 2, 512], F32))
        wide = ctx.enter_context(nc.psum_tensor("wide", [P, TT, 1024], F32))

        loaded = [sem(f"loaded{s}") for s in range(SLOTS)]
        hi_done = sem("hi_done")
        lo_done = sem("lo_done")
        slot_free = [sem(f"slot_free{s}") for s in range(SLOTS)]
        acc_ready = sem("acc_ready")
        acc_read = [sem("acc_read0"), sem("acc_read1")]
        tr_ready = sem("tr_ready")
        tr_read = [sem("tr_read0"), sem("tr_read1")]
        wide_ready = sem("wide_ready")
        wide_read = [sem("wide_read0"), sem("wide_read1")]
        pos_loaded = sem("pos_loaded")
        x_loaded = [sem("x_loaded0"), sem("x_loaded1")]
        masks_ready = sem("masks_ready")
        consts_ready = sem("consts_ready")
        tables_step = sem("tables_step")
        angles_ready = sem("angles_ready")
        sines_ready = sem("sines_ready")
        small_loaded = sem("small_loaded")
        keys_loaded = sem("keys_loaded")
        w1_loaded = sem("w1_loaded")
        half_ready = sem("half_ready")
        qk_ready = sem("qk_ready")
        raw_gates = sem("raw_gates")
        gates_ready = sem("gates_ready")
        ln_loaded = sem("ln_loaded")
        x_ready = sem("x_ready")
        tr_hi = sem("tr_hi")
        var_ready = sem("var_ready")
        rstd_ready = sem("rstd_ready")
        sq_done = sem("sq_done")
        lat_ready = sem("lat_ready")
        ngate_ready = sem("ngate_ready")
        tok_ready = sem("tok_ready")
        blk_ready = sem("blk_ready")
        cmp_shifted = sem("cmp_shifted")
        cmp_exp = sem("cmp_exp")
        cmp_ready = sem("cmp_ready")
        max_ready = sem("max_ready")
        exp_ready = sem("exp_ready")
        p_ready = sem("p_ready")
        mixed_ready = sem("mixed_ready")
        best_ready = sem("best_ready")
        gate_exp = sem("gate_exp")
        picks_ready = sem("picks_ready")
        distance_done = sem("distance_done")
        hot_i_ready = sem("hot_i_ready")
        hot_j_ready = sem("hot_j_ready")
        w_hi_done = sem("w_hi_done")
        w_lo_done = sem("w_lo_done")
        dve_step = sem("dve_step")
        route_step = sem("route_step")
        ln_step = sem("ln_step")
        pool_step = sem("pool_step")
        warm_step = sem("warm_step")
        stored = sem("stored")
        apart = sem("apart")

        block = ctx.enter_context(nc.Block())

        @block.sync
        def _(sp):
            for free in slot_free:
                sp.sem_inc(free, OPEN)
            sp.dma_start(pos_i[:], t["positions"]).then_inc(pos_loaded, 16)
            sp.dma_start(freq[:], t["freq"].partition_broadcast(P)).then_inc(pos_loaded, 16)
            for tt in range(TT):
                sp.dma_start(xs[:, tt], t["x"][:, tt]).then_inc(x_loaded[tt], 16)

            def load(l, src, first, turns):
                with sp.Fori(0, turns) as q:
                    for s in range(SLOTS):
                        turn = l * TURNS + (q + first // SLOTS)
                        sp.wait_ge(slot_free[s], OPEN + turn)
                        sp.dma_start(raw[:, s], src[l, q * SLOTS + s]).then_inc(loaded[s], 16)

            with sp.Fori(0, DEPTH) as l:
                load(l, t["front"], 0, FRONT // SLOTS)
                load(l, t["peer_u"], T_U, NKEYS // SLOTS)
                load(l, t["peer_v"], T_V, NKEYS // SLOTS)
            sp.wait_ge(x_ready, TT * (1 + 2 * DEPTH))
            sp.dma_start(out, xs[:]).then_inc(stored, 16)
            sp.wait_ge(stored, 16)

        @block.gpsimd
        def _(pool):
            pst = Steps(pool, pool_step, 0, 10)

            def ln_load(i):
                for r in range(2):
                    pool.dma_start(ln_par[:, r], t["ln"][i, r].partition_broadcast(P)).then_inc(ln_loaded, 16)

            ln_load(0)
            pst.link(nc.gpsimd.memset(ident[:], 0.0))
            pst.link(nc.gpsimd.affine_select(ident[:], ident[:], [[-1, P]], ALU.not_equal, 1.0, 0, 1))
            pst.link(nc.gpsimd.iota(iota[:], [[1, P]], 0, 0, allow_small_or_imprecise_dtypes=True))
            pst.link(nc.gpsimd.memset(causal[:], 0.0))
            pst.link(nc.gpsimd.affine_select(causal[:], causal[:], [[-1, P]], ALU.is_ge, NEG, 0, 1))
            pst.link(nc.gpsimd.memset(cmask[:], 0.0))
            pst.link(nc.gpsimd.memset(cmask01[:], 1.0))
            pat = [[P, TT], [-CMP_STRIDE, NCMP]]
            pst.link(nc.gpsimd.affine_select(cmask[:], cmask[:], pat, ALU.is_ge, NEG, 1 - CMP_BLOCK, 1))
            pst.link(nc.gpsimd.affine_select(cmask01[:], cmask01[:], pat, ALU.is_ge, 0.0, 1 - CMP_BLOCK, 1))
            nc.gpsimd.memset(ones[:], 1.0)
            pst.link(nc.gpsimd.memset(neg_half[:], -0.5))
            pst.end()
            nc.gpsimd.memset(warm[:], 0.0).then_inc(consts_ready, 1)

            def rsqrt(n, width):
                pool.wait_ge(var_ready, n + 1)
                nc.gpsimd.tensor_tensor(rstd[:, :width], var[:, :width], neg_half[:, :width],
                                        ALU.pow).then_inc(rstd_ready, 1)

            rsqrt(0, TT)
            with pool.Fori(0, DEPTH) as l:
                pool.wait_ge(slot_free[SLOTS - 1], OPEN + l * TURNS)
                pool.dma_start(lat_g[:], t["lat_g"][l]).then_inc(small_loaded, 16)
                pool.dma_start(pe[:], t["cmp_pe"][l]).then_inc(small_loaded, 16)
                pool.dma_start(w2[:], t["cmp_w2"][l]).then_inc(small_loaded, 16)
                rsqrt(3 * l + 1, 4)
                pool.wait_ge(slot_free[(T_MG - 1) % SLOTS], OPEN + l * TURNS + (T_MG - 1) // SLOTS + 1)
                pool.dma_start(w1[:], t["cmp_w1"][l]).then_inc(w1_loaded, 16)
                pool.wait_ge(tr_ready, l * NTR + X_NQ)
                pool.dma_start(keys[:], t["sub_keys"][l]).then_inc(keys_loaded, 16)
                pool.wait_ge(acc_ready, l * NREADY + R_SCR)
                for r in range(2):
                    pool.dma_start(ln_par[:, r], t["ln"][l * 2 + 1, r].partition_broadcast(P)).then_inc(ln_loaded, 16)
                rsqrt(3 * l + 2, TT)
                pool.wait_ge(w_lo_done, l * NKEYS + 48)
                for r in range(2):
                    pool.dma_start(ln_par[:, r], t["ln"][l * 2 + 2, r].partition_broadcast(P)).then_inc(ln_loaded, 16)
                rsqrt(3 * l + 3, TT)

        @block.scalar
        def _(act):
            def split_hi(l, q, s):
                act.wait_ge(loaded[s], (l * TURNS + q + 1) * 16)
                nc.scalar.activation(hi[:, s], raw[:, s], ACT.Identity).then_inc(hi_done, 1)

            def tile_step(l, n):
                split_hi(l, (n + AHEAD) // SLOTS, (n + AHEAD) % SLOTS)

            def tile_used(l, q, s):
                act.wait_ge(slot_free[s], OPEN + l * TURNS + q + 1)

            def tr_copy(l, i, dst, src):
                act.wait_ge(tr_ready, l * NTR + i + 1)
                nc.scalar.activation(dst, src, ACT.Identity).then_inc(tr_read[i % 2], 1)

            def warm_up(func, n):
                nc.scalar.activation(warm[:, 1:2], warm[:, 0:1], func).then_inc(warm_step, 1)
                act.wait_ge(warm_step, n)

            act.wait_ge(consts_ready, 1)
            nc.scalar.activation(ident_r[:], ident[:], ACT.Identity).then_inc(masks_ready, 1)
            nc.scalar.activation(causal_r[:], causal[:], ACT.Identity).then_inc(masks_ready, 1)
            act.wait_ge(angles_ready, 1)
            nc.scalar.activation(ang[:, 2], ang[:, 0], ACT.Sin).then_inc(sines_ready, 1)
            nc.scalar.activation(ang[:, 3], ang[:, 1], ACT.Sin).then_inc(sines_ready, 1)

            with act.Fori(0, DEPTH) as l:
                warm_up(ACT.Gelu, l * 2 + 1)
                for n in range(AHEAD):
                    split_hi(l, 0, n)

                def transposed_hi(first, hi_first, dst):
                    for g in range(4):
                        act.wait_ge(tr_ready, l * NTR + first + g + 1)
                        nc.scalar.activation(dst(g), tr[:, (first + g) % 2].rearrange("p (c t) -> p c t", c=4),
                                             ACT.Identity).then_inc(tr_hi, 1)

                def xT_part(g):
                    tt, cg = divmod(g, 2)
                    return xT_hi[:, 4 * cg:4 * cg + 4, tt * P:(tt + 1) * P]

                transposed_hi(X_XT, 0, xT_part)
                for c in range(N_LAT):
                    tile_step(l, T_LAT + c)
                    tile_used(l, (T_LAT + c) // SLOTS, (T_LAT + c) % SLOTS)
                    nc.scalar.activation(sq[:, c], acc[:, c % 2, :SEQ], ACT.Square).then_inc(sq_done, 1)
                for n in range(T_UQ, T_UKV):
                    tile_step(l, n)
                n = T_UKV - 1
                tile_used(l, n // SLOTS, n % SLOTS)
                for tt in range(TT):
                    nc.scalar.activation(ngate[:, tt], acc[:, tt, 2 * GW + ROPE:WB], ACT.Sigmoid).then_inc(ngate_ready, 1)
                for n in range(T_UKV, T_MG):
                    tile_step(l, n)

                def gate_copy(c):
                    n, use = MG_TILE[c], MG_USE[c]
                    tile_step(l, n)
                    tile_used(l, n // SLOTS, n % SLOTS)
                    nc.scalar.activation(gates[:, c], acc[:, use % 2, :SEQ], ACT.Identity).then_inc(acc_read[use % 2], 1)

                for c in range(MG_EARLY):
                    gate_copy(c)
                for n in range(T_A, T_MG2):
                    tile_step(l, n)
                for c in range(MG_EARLY, 4):
                    gate_copy(c)

                def heads_copy(i, part, width, bank, scale=1.0):
                    act.wait_ge(tr_ready, l * NTR + i + 1)
                    nc.scalar.activation(part, tr[:width, bank].rearrange("p (h t) -> p h t", h=4), ACT.Identity,
                                         scale=scale).then_inc(tr_read[bank], 1)

                for first, dst in ((X_Q, qT), (X_K, kT)):
                    for g in range(4):
                        tt, hg = divmod(g, 2)
                        heads_copy(first + g, dst[:QKD, 4 * hg:4 * hg + 4, tt * P:(tt + 1) * P], QKD, g % 2)
                for g in range(0, 4, 2):
                    tt, hg = divmod(g, 2)
                    heads_copy(X_NQ + g, nqT[:, 4 * hg:4 * hg + 4, tt * P:(tt + 1) * P], HD, 0, NSA_SCALE)
                heads_copy(X_KT, nkT[:, :, 0:P], HD, 0)
                heads_copy(X_CD, cmpT[:, :, 0:P], P, 0)
                act.wait_ge(acc_ready, l * NREADY + R_HID + 1)
                nc.scalar.activation(hid[:], acc[:, A_HID % 2, :2 * GROUPS * NCMP].rearrange("p (c n) -> p c n", c=2),
                                     ACT.Gelu).then_inc(acc_read[A_HID % 2], 1)
                gate_copy(4)
                gate_copy(5)
                for tt in range(TT):
                    act.wait_ge(cmp_shifted, l * TT + tt + 1)
                    nc.scalar.activation(cs[:, tt, :, :NCMP], cs[:, tt, :, :NCMP], ACT.Exp).then_inc(cmp_exp, 1)
                gate_copy(6)
                gate_copy(7)
                for tt in range(TT):
                    i = X_PC + 2 * tt
                    tr_copy(l, i, pcT[:NCMP, 0:4, tt * P:(tt + 1) * P],
                            tr[:NCMP, 0].rearrange("p (h t) -> p h t", h=4))

                def copy_o(oi):
                    act.wait_ge(acc_ready, l * NREADY + R_O + oi + 1)
                    tt, i = divmod(oi, 4)
                    bank = O_USE[oi] % 2
                    nc.scalar.activation(o_tok[:, tt, i // 2, 256 * (i % 2):256 * (i % 2) + 256],
                                         acc[:, bank, :256], ACT.Identity).then_inc(acc_read[bank], 1)

                def copy_pT(u):
                    for kb, i in enumerate(unit(u)[4]):
                        if i % 2 == 0:
                            tr_copy(l, i, pT[:, u % 2, kb], tr[:, 0])

                def exp_scores(u):
                    tt = unit(u)[2]
                    if u >= 2:
                        act.wait_ge(tr_ready, l * NTR + unit(u - 2)[4][-1] + 1)
                    act.wait_ge(max_ready, l * NU + u + 1)
                    for h in range(4):
                        ins = nc.scalar.activation(sc[:, u % 2, h, :(tt + 1) * P],
                                                   wide[:, u % 2, 256 * h:256 * h + (tt + 1) * P],
                                                   ACT.Exp, bias=negmax[:, u % 2, h:h + 1],
                                                   accum_out=sums[:, u % 2, h:h + 1])
                    ins.then_inc(exp_ready, 1)

                exp_scores(0)
                for u in range(NU + 1):
                    if u + 1 < NU:
                        exp_scores(u + 1)
                    if u + 8 < N_MG:
                        gate_copy(u + 8)
                    if u < NU:
                        copy_pT(u)
                    if u >= 1 and (u == NU or unit(u - 1)[3] != unit(u)[3]):
                        copy_o(unit(u - 1)[3])
                transposed_hi(X_OT, 4, lambda g: oT_hi[:, g // 2, :, (g % 2) * P:(g % 2 + 1) * P])

                for b in range(2):
                    act.wait_ge(acc_read[b], OPEN + l * (NACC // 2) + A_BR // 2)
                g2 = gates[:].rearrange("p (b c) t -> p b c t", b=2)
                for q in range(4):
                    nc.scalar.activation(g2[:, :, 2 * q:2 * q + 2], g2[:, :, 2 * q:2 * q + 2],
                                         ACT.Sigmoid).then_inc(gates_ready, 1)
                for n in range(T_BR, T_PQ):
                    tile_step(l, n)
                transposed_hi(X_XT2, 8, xT_part)
                warm_up(ACT.Gelu, l * 2 + 2)
                with act.Fori(0, N_PQ // SLOTS) as i:
                    for e in range(SLOTS):
                        split_hi(l, (i + (T_PQ + e + AHEAD) // SLOTS), (T_PQ + e + AHEAD) % SLOTS)
                        tile_used(l, (i + (T_PQ + e) // SLOTS), (T_PQ + e) % SLOTS)
                        nc.scalar.activation(pqT[:, i * SLOTS + e], acc[:, e % 2, :SEQ],
                                             ACT.Identity).then_inc(acc_read[e % 2], 1)
                for i in range(8):
                    c, p = divmod(i, 2)
                    act.wait_ge(acc_ready, l * NREADY + R_SCR + i + 1)
                    nc.scalar.activation(big[:, S0 + 4 * c:S0 + 4 * c + 4, p * P:(p + 1) * P],
                                         acc[:, p].rearrange("p (u n) -> p u n", u=4),
                                         ACT.Identity).then_inc(acc_read[p], 1)
                with act.Fori(0, NKEYS // 8) as i:
                    for e in range(8):
                        n = T_U + e
                        split_hi(l, (i * 2 + (n + AHEAD) // SLOTS), (n + AHEAD) % SLOTS)
                        tile_used(l, (i * 2 + n // SLOTS), n % SLOTS)
                        nc.scalar.activation(big[:, i * 8 + e], acc[:, e % 2, :SEQ],
                                             ACT.Gelu).then_inc(acc_read[e % 2], 1)
                act.wait_ge(best_ready, l + 1)
                nc.scalar.activation(picks[:, 2], picks[:, 2], ACT.Exp).then_inc(gate_exp, 1)
                tr_copy(l, X_PK, picksT[:, 0:2], tr[:, 0].rearrange("p (k t) -> p k t", k=2))

                def distances(i, e):
                    act.wait_ge(acc_ready, l * NREADY + (R_G + 1 - HOTS) + (i * HOTS + e))
                    for r in range(4):
                        tok = i * (4 * HOTS) + (4 * e + r)
                        ins = nc.scalar.activation(hot_i[:, e % HOTS, r], iota[:], ACT.Abs,
                                                   bias=picksT[:, 0, bass.ds(tok, 1)], scale=-1.0)
                    ins.then_inc(distance_done, 1)

                def one_hot(i, e):
                    act.wait_ge(distance_done, l * NG + (i * HOTS + (e + 1)))
                    nc.scalar.activation(hot_i[:, e], hot_i[:, e], ACT.Relu, bias=ones[:, 0:1],
                                         scale=-1.0).then_inc(hot_i_ready, 1)

                act.wait_ge(tr_read[X_PK % 2], OPEN + l * (NTR // 2) + NTR // 2)
                distances(0, 0)
                with act.Fori(0, NG // HOTS - 1) as i:
                    for e in range(HOTS):
                        distances(i, e + 1)
                        one_hot(i, e)
                for e in range(HOTS):
                    if e + 1 < HOTS:
                        distances(NG // HOTS - 1, e + 1)
                    one_hot(NG // HOTS - 1, e)

                def split_w_hi(j, s):
                    nc.scalar.activation(w_hi[:, s], big[:, j], ACT.Identity).then_inc(w_hi_done, 1)

                for b in range(2):
                    act.wait_ge(acc_read[b], OPEN + l * (NACC // 2) + NACC // 2)
                for j in range(AHEAD):
                    split_w_hi(j, j)
                with act.Fori(0, NKEYS // SLOTS - 1) as i:
                    for e in range(SLOTS):
                        n = T_V + e + AHEAD
                        split_hi(l, (i + n // SLOTS), n % SLOTS)
                        split_w_hi(i * SLOTS + (e + AHEAD), n % SLOTS)
                split_hi(l, TURNS - 1, SLOTS - 1)
                split_w_hi(NKEYS - 1, SLOTS - 1)

        @block.vector
        def _(dve):
            def split_lo(l, q, s):
                dve.wait_ge(hi_done, l * NT + q * SLOTS + s + 1)
                nc.vector.tensor_tensor(lo[:, s], raw[:, s], hi[:, s].bitcast(F32), ALU.subtract).then_inc(lo_done, 1)

            def tile_step(l, n):
                split_lo(l, (n + AHEAD) // SLOTS, (n + AHEAD) % SLOTS)

            def tile_used(l, q, s):
                dve.wait_ge(slot_free[s], OPEN + l * TURNS + q + 1)

            def tr_copy(l, i, dst, src):
                dve.wait_ge(tr_ready, l * NTR + i + 1)
                nc.vector.tensor_copy(dst, src).then_inc(tr_read[i % 2], 1)

            def statistics(tt, chain):
                for c in range(2):
                    chain.link(nc.vector.bn_stats(stats[:, tt, c], xs[:, tt, 512 * c:512 * c + 512]))
                dve.sem_inc(apart, 1)
                chain.link(nc.vector.bn_aggr(mv[:, tt], stats[:, tt].rearrange("p c s -> p (c s)")))

            def normalise(rs_nth, loads, chain):
                nc.vector.tensor_scalar(var[:, :TT], mv[:, :, 1], LN_EPS, None, ALU.add).then_inc(var_ready, 1)
                dve.wait_ge(ln_loaded, loads)
                for tt in range(TT):
                    chain.link(nc.vector.scalar_tensor_tensor(out=xs[:, tt], in0=xs[:, tt], scalar=mv[:, tt, 0:1],
                                                              in1=ln_par[:, 0], op0=ALU.subtract, op1=ALU.mult))
                    if tt == 0:
                        dve.wait_ge(rstd_ready, rs_nth + 1)
                    nc.vector.scalar_tensor_tensor(out=xs[:, tt], in0=xs[:, tt], scalar=rstd[:, tt:tt + 1],
                                                   in1=ln_par[:, 1], op0=ALU.mult, op1=ALU.add).then_inc(x_ready, 1)

            for done in (lat_ready, mixed_ready):
                dve.sem_inc(done, OPEN)

            tab = Steps(dve, tables_step, 0, 19)
            dve.wait_ge(pos_loaded, 32)
            tab.link(nc.vector.tensor_copy(pos_f[:], pos_i[:]))
            for tt in range(TT):
                tab.link(nc.vector.tensor_scalar(ang[:, 0, tt], freq[:], pos_f[:, tt:tt + 1], None, ALU.mult))
            tab.link(nc.vector.tensor_scalar(ang[:, 1], ang[:, 0], 1.0 / TWO_PI, None, ALU.mult))
            tab.link(nc.vector.tensor_scalar(ang[:, 1], ang[:, 1], ROUND, None, ALU.add))
            tab.link(nc.vector.tensor_scalar(ang[:, 1], ang[:, 1], ROUND, None, ALU.subtract))
            for part in (PI_A, PI_B, PI_C):
                tab.link(nc.vector.scalar_tensor_tensor(out=ang[:, 0], in0=ang[:, 1], scalar=-part, in1=ang[:, 0],
                                                        op0=ALU.mult, op1=ALU.add))
            tab.link(nc.vector.tensor_scalar(ang[:, 0], ang[:, 0], float(np.float32(np.pi)),
                                             -float(np.float32(np.pi)), ALU.min, ALU.max))
            tab.link(nc.vector.scalar_tensor_tensor(out=ang[:, 1], in0=ang[:, 0], scalar=-1.0, in1=ang[:, 0],
                                                    op0=ALU.mult, op1=ALU.max))
            nc.vector.tensor_scalar(ang[:, 1], ang[:, 1], -1.0, float(np.pi / 2), ALU.mult, ALU.add).then_inc(angles_ready, 1)
            chain = Steps(dve, ln_step, 0, TT * 4)
            for tt in range(TT):
                dve.wait_ge(x_loaded[tt], 16)
                statistics(tt, chain)
            normalise(0, 32, chain)
            chain.end()
            dve.wait_ge(sines_ready, 2)
            R2, H2 = ROPE // 2, HD // 2
            tab.link(nc.vector.tensor_copy(cos_m[:, :, :R2], ang[:, 3, :, :R2]))
            tab.link(nc.vector.tensor_copy(cos_m[:, :, R2:], ang[:, 3, :, :R2]))
            tab.link(nc.vector.tensor_copy(sin_m[:, :, R2:], ang[:, 2, :, :R2]))
            tab.link(nc.vector.tensor_scalar(sin_m[:, :, :R2], ang[:, 2, :, :R2], -1.0, None, ALU.mult))
            tab.link(nc.vector.tensor_copy(cos_n[:, :, :H2], ang[:, 3, :, R2:]))
            tab.link(nc.vector.tensor_copy(cos_n[:, :, H2:], ang[:, 3, :, R2:]))
            tab.link(nc.vector.tensor_copy(sin_n[:, :, H2:], ang[:, 2, :, R2:]))
            tab.link(nc.vector.tensor_scalar(sin_n[:, :, :H2], ang[:, 2, :, R2:], -1.0, None, ALU.mult))
            tab.end()
            dve.wait_ge(consts_ready, 1)

            with dve.Fori(0, DEPTH) as l:
                st = Steps(dve, dve_step, l * DVE_STEPS, DVE_STEPS)
                for n in range(AHEAD):
                    split_lo(l, 0, n)

                def transposed_lo(first, hi_first, dst_hi, dst_lo):
                    for g in range(4):
                        dve.wait_ge(tr_hi, l * 12 + hi_first + g + 1)
                        nc.vector.tensor_tensor(dst_lo(g), tr[:, (first + g) % 2].rearrange("p (c t) -> p c t", c=4),
                                                dst_hi(g).bitcast(F32), ALU.subtract).then_inc(tr_read[(first + g) % 2], 1)

                def x_part(part):
                    def f(g):
                        tt, cg = divmod(g, 2)
                        return part[:, 4 * cg:4 * cg + 4, tt * P:(tt + 1) * P]
                    return f

                def o_part(part):
                    return lambda g: part[:, g // 2, :, (g % 2) * P:(g % 2 + 1) * P]

                def rotate(dst, src, cos, sin, heads, width, tmp_a, tmp_b, release=None):
                    h = width // 2
                    a = tmp_a[:, :heads * width].rearrange("p (h d) -> p h d", d=width)
                    b = tmp_b[:, :heads * width].rearrange("p (h d) -> p h d", d=width)
                    full = [P, heads, width]
                    half = [P, heads, h]
                    st.link(nc.vector.tensor_tensor(a, src, cos.unsqueeze(1).broadcast_to(full), ALU.mult))
                    st.link(nc.vector.tensor_tensor(b[:, :, :h], src[:, :, h:], sin[:, :h].unsqueeze(1).broadcast_to(half), ALU.mult))
                    st.link(nc.vector.tensor_tensor(b[:, :, h:], src[:, :, :h], sin[:, h:].unsqueeze(1).broadcast_to(half), ALU.mult))
                    if release is not None:
                        release()
                    return nc.vector.tensor_tensor(dst, a, b, ALU.add)

                transposed_lo(X_XT, 0, x_part(xT_hi), x_part(xT_lo))
                dve.wait_ge(small_loaded, l * 48 + 48)
                for c in range(N_LAT):
                    n = T_LAT + c
                    tile_step(l, n)
                    dve.wait_ge(sq_done, l * N_LAT + c + 1)
                    dve.wait_ge(lat_ready, OPEN + l * N_LAT + c)
                    nc.vector.tensor_scalar(lat[:], acc[:, c % 2, :SEQ], lat_g[:, c:c + 1], None,
                                            ALU.mult).then_inc(acc_read[c % 2], 1)
                    dve.wait_ge(acc_read[c % 2], OPEN + l * (NACC // 2) + (A_LAT + c) // 2 + 1)
                    st.link(nc.vector.tensor_copy(cq_hi[:, c], lat[:]))
                    nc.vector.tensor_tensor(cq_lo[:, c], lat[:], cq_hi[:, c].bitcast(F32), ALU.subtract).then_inc(lat_ready, 1)
                dve.wait_ge(acc_ready, l * NREADY + R_RMS + 1)
                nc.vector.tensor_scalar(var[:, 0:TT], acc[:, 0, 0:TT], 1.0 / Q_RANK, RMS_EPS, ALU.mult,
                                        ALU.add).then_inc(acc_read[0], 1)
                dve.wait_ge(acc_ready, l * NREADY + R_RMS + 2)
                st.link(nc.vector.tensor_scalar(var[:, TT:2 * TT], acc[:, 1, 0:TT], 1.0 / KV_RANK, RMS_EPS, ALU.mult, ALU.add))
                nc.vector.tensor_copy(gsum[:, 0:TT], acc[:, 1, 0:TT]).then_inc(acc_read[1], 1)
                nc.vector.tensor_copy(gsum[:, TT:2 * TT], var[:, 0:TT]).then_inc(var_ready, 1)
                for n in range(T_UQ, T_B):
                    tile_step(l, n)
                dve.wait_ge(rstd_ready, 3 * l + 2)
                n = T_B - 1
                tile_used(l, n // SLOTS, n % SLOTS)
                for tt in range(TT):
                    nc.vector.tensor_scalar(q_tok[:, tt].rearrange("p (a h) d -> p a (h d)", a=2),
                                            wide[:, tt].rearrange("p (a c) -> p a c", a=2)[:, :, :384],
                                            rstd[:, tt:tt + 1], MLA_SCALE, ALU.mult, ALU.mult).then_inc(wide_read[tt], 1)
                    tile_step(l, T_B + tt)
                for tt in range(TT):
                    dve.wait_ge(wide_read[tt], OPEN + l * NWIDE + W_UQ + 1)
                    part = q_tok[:, tt, :, NOPE:]
                    st.link(rotate(part, part, cos_m[:, tt], sin_m[:, tt], HEADS, ROPE, rope_a, rope_b))
                    tile_step(l, T_B + 2 + tt)
                n = T_UKV - 1
                tile_used(l, n // SLOTS, n % SLOTS)
                for tt in range(TT):
                    dve.wait_ge(ngate_ready, l * TT + tt + 1)
                    pair = acc[:, tt, :GW].rearrange("p (g d) -> p g d", g=GROUPS)
                    nc.vector.tensor_copy(cmp_tok[:, tt, 1], pair.unsqueeze(2).broadcast_to([P, GROUPS, 2, HD]))
                    nc.vector.tensor_copy(v_sel[:, tt], acc[:, tt, GW:2 * GW])
                    st.link(nc.vector.tensor_copy(kr[:, 0], acc[:, tt, 2 * GW:2 * GW + ROPE]))
                    nc.vector.tensor_copy(kr[:, 1], acc[:, tt, 2 * GW:2 * GW + ROPE]).then_inc(acc_read[tt], 1)
                    tile_step(l, T_UKV + tt)
                    dve.wait_ge(acc_read[tt], OPEN + l * (NACC // 2) + (A_B + tt) // 2 + 1)
                    st.link(rotate(kr[:, 1:2], kr[:, 0:1], cos_m[:, tt], sin_m[:, tt], 1, ROPE, rope_a, rope_b))
                    nc.vector.tensor_copy(k_tok[:, tt, :, NOPE:], kr[:, 1:2].broadcast_to([P, HEADS, ROPE]))
                n = T_MG - 1
                tile_used(l, n // SLOTS, n % SLOTS)
                for tt in range(TT):
                    kv = wide[:, tt].rearrange("p (h d) -> p h d", d=NOPE + VDIM)
                    nc.vector.tensor_scalar(k_tok[:, tt, :, :NOPE], kv[:, :, :NOPE], rstd[:, TT + tt:TT + tt + 1], None,
                                            ALU.mult).then_inc(qk_ready, 1)
                    nc.vector.tensor_scalar(v_mla[:, tt], kv[:, :, NOPE:], rstd[:, TT + tt:TT + tt + 1], None,
                                            ALU.mult).then_inc(wide_read[tt], 1)
                    tile_step(l, T_MG + tt)
                for n in range(T_A, T_MG2):
                    tile_step(l, n)
                n = T_MG2 - 1
                tile_used(l, n // SLOTS, n % SLOTS)
                for tt in range(TT):
                    def release():
                        nc.vector.tensor_copy(v_win[:, tt], wide[:, tt, ROT * HD:]).then_inc(wide_read[tt], 1)

                    st.link(rotate(rot[:, tt], wide[:, tt, :ROT * HD].rearrange("p (h d) -> p h d", d=HD),
                                   cos_n[:, tt], sin_n[:, tt], ROT, HD, rope_a, rope_b, release))
                    nc.vector.tensor_copy(cmp_tok[:, tt, 0], rot[:, tt, HEADS:HEADS + GROUPS].unsqueeze(2).broadcast_to(
                        [P, GROUPS, 2, HD])).then_inc(tok_ready, 1)
                for c in range(MG_EARLY, 4):
                    tile_step(l, MG_TILE[c])
                for g in range(1, 4, 2):
                    tt, hg = divmod(g, 2)
                    dve.wait_ge(tr_ready, l * NTR + X_NQ + g + 1)
                    nc.vector.tensor_scalar(nqT[:, 4 * hg:4 * hg + 4, tt * P:(tt + 1) * P],
                                            tr[:HD, 1].rearrange("p (h t) -> p h t", h=4), NSA_SCALE, None,
                                            ALU.mult).then_inc(tr_read[1], 1)
                tr_copy(l, X_KT + 1, nkT[:, :, P:], tr[:HD, 1].rearrange("p (h t) -> p h t", h=4))
                tr_copy(l, X_CD + 1, cmpT[:, :, P:], tr[:, 1].rearrange("p (h t) -> p h t", h=4))
                for b in range(2):
                    dve.wait_ge(tr_read[b], OPEN + l * (NTR // 2) + (X_CD + 1) // 2 + 1)
                for c in range(2):
                    for par in range(2):
                        rows = slice(par * HD, par * HD + HD)
                        for g in range(GROUPS):
                            src = bass.AP(cmpT[rows, 2 * c + g].tensor, cmpT[rows, 2 * c + g].offset + par,
                                          [cmpT[rows, 2 * c + g].ap[0], [2, 16], [CMP_STRIDE, NCMP]])
                            ins = nc.vector.tensor_tensor(
                                blk[rows, c, :, g * NCMP:(g + 1) * NCMP], src,
                                pe[rows, c].unsqueeze(2).broadcast_to([HD, 16, NCMP]), ALU.add)
                            ins.then_inc(blk_ready, 1)
                tile_step(l, MG_TILE[4])
                dve.wait_ge(acc_ready, l * NREADY + R_KCVC + 1)
                b = A_KCVC % 2
                st.link(nc.vector.tensor_copy(kc[:], acc[:HD, b, 0:GROUPS * NCMP]))
                nc.vector.tensor_copy(vc[:NCMP], acc[:NCMP, b, 64:64 + GROUPS * HD].rearrange(
                    "p (g d) -> p g d", g=GROUPS)).then_inc(acc_read[b], 1)
                tile_step(l, MG_TILE[5])
                m3 = [P, HEADS, NCMP]
                for tt in range(TT):
                    b = (A_CS + tt) % 2
                    dve.wait_ge(acc_ready, l * NREADY + R_CS + tt + 1)
                    e = cs[:, tt, :, :NCMP]
                    nc.vector.tensor_tensor(
                        e, acc[:, b, :HEADS * 16].rearrange("p (h n) -> p h n", n=16)[:, :, :NCMP],
                        cmask[:, tt].unsqueeze(1).broadcast_to(m3), ALU.add).then_inc(acc_read[b], 1)
                    dve.wait_ge(acc_read[b], OPEN + l * (NACC // 2) + (A_CS + tt) // 2 + 1)
                    st.link(nc.vector.tensor_reduce(cst[:, tt, 0], e, AX.X, ALU.max))
                    nc.vector.tensor_tensor(e, e, cst[:, tt, 0].unsqueeze(2).broadcast_to(m3),
                                            ALU.subtract).then_inc(cmp_shifted, 1)
                tile_step(l, MG_TILE[6])
                for tt in range(TT):
                    e = cs[:, tt, :, :NCMP]
                    dve.wait_ge(cmp_exp, l * TT + tt + 1)
                    st.link(nc.vector.tensor_reduce(cst[:, tt, 1], e, AX.X, ALU.add))
                    st.link(nc.vector.reciprocal(cst[:, tt, 2], cst[:, tt, 1]))
                    g0 = ngate[:, tt].rearrange("p (h b) -> p h b", b=3)[:, :, 0]
                    st.link(nc.vector.tensor_tensor(cst[:, tt, 2], cst[:, tt, 2], g0, ALU.mult))
                    st.link(nc.vector.tensor_tensor(e, e, cmask01[:, tt].unsqueeze(1).broadcast_to(m3), ALU.mult))
                    nc.vector.tensor_tensor(e, e, cst[:, tt, 2].unsqueeze(2).broadcast_to(m3),
                                            ALU.mult).then_inc(cmp_ready, 1)
                tile_step(l, MG_TILE[7])
                for tt in range(TT):
                    tr_copy(l, X_PC + 2 * tt + 1, pcT[:NCMP, 4:8, tt * P:(tt + 1) * P],
                            tr[:NCMP, 1].rearrange("p (h t) -> p h t", h=4))

                def largest(u):
                    keys_n = (unit(u)[2] + 1) * P
                    dve.wait_ge(wide_ready, l * NU + u + 1)
                    nc.vector.tensor_reduce(negmax[:, u % 2], wide[:, u % 2].rearrange("p (h k) -> p h k", h=4)[:, :, :keys_n],
                                            AX.X, ALU.max, negate=True).then_inc(max_ready, 1)

                def weights_out(u):
                    kind, hg, tt, oi, trs = unit(u)
                    dve.wait_ge(exp_ready, l * NU + u + 1)
                    st.link(nc.vector.reciprocal(recip[:, u % 2], sums[:, u % 2]))
                    if kind != "mla":
                        g = ngate[:, tt].rearrange("p (h b) -> p h b", b=3)[:, 4 * hg:4 * hg + 4, 1 if kind == "sel" else 2]
                        st.link(nc.vector.tensor_tensor(recip[:, u % 2], recip[:, u % 2], g, ALU.mult))
                    for h in range(4):
                        s = sc[:, u % 2, h, :(tt + 1) * P]
                        ins = nc.vector.tensor_scalar(s, s, recip[:, u % 2, h:h + 1], None, ALU.mult)
                    ins.then_inc(p_ready, 1)

                def copy_pT(u):
                    for kb, i in enumerate(unit(u)[4]):
                        if i % 2 == 1:
                            tr_copy(l, i, pT[:, u % 2, kb], tr[:, 1])

                largest(0)
                weights_out(0)
                for u in range(NU):
                    if u + 1 < NU:
                        largest(u + 1)
                    if u + 8 < N_MG:
                        tile_step(l, MG_TILE[u + 8])
                    copy_pT(u)
                    if u + 1 < NU:
                        weights_out(u + 1)
                transposed_lo(X_OT, 4, o_part(oT_hi), o_part(oT_lo))

                for q in range(4):
                    for e in range(2):
                        n = T_BR + 2 * q + e
                        tile_step(l, n)
                        tile_used(l, n // SLOTS, n % SLOTS)
                        dve.wait_ge(gates_ready, l * 4 + q + 1)
                        if e == 0:
                            dve.wait_ge(mixed_ready, OPEN + l * 4 + q)
                        nc.vector.tensor_tensor((mix_a if e == 0 else mix_b)[:].rearrange("p (f t) -> p f t", f=2),
                                                acc[:, e].rearrange("p (f t) -> p f t", f=2),
                                                gates[:, 8 * e + 2 * q:8 * e + 2 * q + 2], ALU.mult).then_inc(acc_read[e], 1)
                    for e in range(2):
                        dve.wait_ge(acc_read[e], OPEN + l * (NACC // 2) + A_BR // 2 + q + 1)
                    st.link(nc.vector.tensor_tensor(mix_a[:], mix_a[:], mix_b[:], ALU.add))
                    m = mix_a[:].rearrange("p (f t) -> p f t", f=2)
                    st.link(nc.vector.tensor_copy(xT_hi[:, 2 * q:2 * q + 2], m))
                    nc.vector.tensor_tensor(xT_lo[:, 2 * q:2 * q + 2], m, xT_hi[:, 2 * q:2 * q + 2].bitcast(F32),
                                            ALU.subtract).then_inc(mixed_ready, 1)
                for n in range(T_OUT, T_PQ - AHEAD):
                    tile_step(l, n)

                def add_branch(nth, last_tile, use):
                    for tt in range(TT):
                        if tt == 0:
                            dve.wait_ge(half_ready, l * 2 + nth + 1)
                        else:
                            tile_used(l, last_tile // SLOTS, last_tile % SLOTS)
                        nc.vector.scalar_tensor_tensor(out=xs[:, tt], in0=xs[:, tt], scalar=ALPHA, in1=wide[:, tt],
                                                       op0=ALU.mult, op1=ALU.add).then_inc(wide_read[tt], 1)
                        dve.wait_ge(wide_read[tt], OPEN + l * NWIDE + use + 1)
                        statistics(tt, st)

                add_branch(0, T_PQ - 1, W_OUT)
                normalise(3 * l + 2, l * 64 + 64, st)
                for n in range(T_PQ - AHEAD, T_PQ):
                    tile_step(l, n)
                transposed_lo(X_XT2, 8, x_part(xT_hi), x_part(xT_lo))
                with dve.Fori(0, N_PQ // SLOTS) as i:
                    for e in range(SLOTS):
                        split_lo(l, (i + (T_PQ + e + AHEAD) // SLOTS), (T_PQ + e + AHEAD) % SLOTS)
                for b in range(2):
                    dve.wait_ge(acc_read[b], OPEN + l * (NACC // 2) + A_U // 2)
                dve.sem_inc(apart, 1)

                with dve.Fori(0, NKEYS // 8) as i:
                    rt = Steps(dve, route_step, (l * 16 + i) * ROUTE_STEPS, ROUTE_STEPS, apart)

                    kk = [P, TOPK, TOPK]
                    k2 = [P, 2, TOPK, TOPK]
                    unit_places = picks[:, 0:2].rearrange("p a t (h k) -> p a (t h) k", k=TOPK)[:, :, i]
                    unit_gates = picks[:, 2].rearrange("p t (h k) -> p (t h) k", k=TOPK)[:, i]
                    stages = [
                        [lambda: nc.vector.tensor_copy(r_s[:].rearrange("p a n -> p (a n)"), big[:, i + S0])],
                        [lambda p=p: nc.vector.max(r_v[:, p, 0:8], r_s[:, p]) for p in range(2)],
                        [lambda p=p: nc.vector.match_replace(r_s2[:, p], r_v[:, p, 0:8], r_s[:, p], LOWEST) for p in range(2)]
                        + [lambda p=p: nc.vector.max_index(r_i[:, p, 0:8], r_v[:, p, 0:8], r_s[:, p]) for p in range(2)],
                        [lambda p=p: nc.vector.max(r_v[:, p, 8:16], r_s2[:, p]) for p in range(2)],
                        [lambda: nc.vector.tensor_tensor(
                            r_c[:].rearrange("p (a b) -> p a b", a=TOPK), r_v[:, 0].unsqueeze(2).broadcast_to(kk),
                            r_v[:, 1].unsqueeze(1).broadcast_to(kk), ALU.add)]
                        + [lambda p=p: nc.vector.max_index(r_i[:, p, 8:16], r_v[:, p, 8:16], r_s2[:, p]) for p in range(2)],
                        [lambda: nc.vector.max(r_best[:, 0:8], r_c[:]), lambda: nc.vector.tensor_copy(r_if[:], r_i[:])],
                        [lambda: nc.vector.match_replace(r_c2[:], r_best[:, 0:8], r_c[:], LOWEST),
                         lambda: nc.vector.max_index(r_pos[:, 0:8], r_best[:, 0:8], r_c[:])],
                        [lambda: nc.vector.max(r_best[:, 8:16], r_c2[:])],
                        [lambda: nc.vector.max_index(r_pos[:, 8:16], r_best[:, 8:16], r_c2[:]),
                         lambda: nc.vector.tensor_scalar(unit_gates, r_best[:], r_best[:, 0:1], None, ALU.subtract)],
                        [lambda: nc.vector.tensor_scalar(r_ab[:, 0], r_pos[:], 4, None, ALU.logical_shift_right),
                         lambda: nc.vector.tensor_scalar(r_ab[:, 1], r_pos[:], 15, None, ALU.bitwise_and)],
                        [lambda: nc.vector.tensor_copy(r_abf[:], r_ab[:])],
                        [lambda: nc.vector.tensor_tensor(
                            r_eq[:], r_abf[:].unsqueeze(3).broadcast_to(k2),
                            iota[:, :TOPK].unsqueeze(1).unsqueeze(1).broadcast_to(k2), ALU.is_equal)],
                        [lambda: nc.vector.tensor_tensor(
                            r_eq[:], r_eq[:], r_if[:].unsqueeze(2).broadcast_to(k2), ALU.mult)],
                        [lambda: nc.vector.tensor_reduce(unit_places, r_eq[:], AX.X, ALU.add)],
                    ]
                    assert sum(map(len, stages)) == ROUTE_STEPS
                    split_after = [round((len(stages) - 1) * (e + 0.5) / 8) for e in range(8)]
                    for g, stage in enumerate(stages):
                        for ins in stage:
                            rt.mark(ins())
                        for e in range(8):
                            if split_after[e] == g:
                                n = T_U + e + AHEAD
                                split_lo(l, (i * 2 + n // SLOTS), n % SLOTS)
                        rt.settle()
                    rt.end()

                nc.vector.tensor_copy(gsum[:, 0:1], gsum[:, 0:1]).then_inc(best_ready, 1)
                dve.wait_ge(gate_exp, l + 1)
                g = picks[:, 2].rearrange("p t (h k) -> p (t h) k", k=TOPK)
                st.link(nc.vector.tensor_reduce(gsum[:], g, AX.X, ALU.add))
                st.link(nc.vector.reciprocal(gsum[:], gsum[:]))
                nc.vector.tensor_tensor(g, g, gsum[:].unsqueeze(2).broadcast_to([P, TT * HEADS, TOPK]),
                                        ALU.mult).then_inc(picks_ready, 1)
                tr_copy(l, X_PK + 1, picksT[:, 2], tr[:, 1, :SEQ])
                for b in range(2):
                    dve.wait_ge(tr_read[b], OPEN + l * (NTR // 2) + NTR // 2)
                dve.sem_inc(apart, 1)

                def gated_rows(i, e):
                    dve.wait_ge(acc_ready, l * NREADY + (R_G + 1 - HOTS) + (i * HOTS + e))
                    for r in range(4):
                        tok = i * (4 * HOTS) + (4 * e + r)
                        ins = nc.vector.tensor_scalar(hot_j[:, e % HOTS, r], iota[:], picksT[:, 1, bass.ds(tok, 1)],
                                                      picksT[:, 2, bass.ds(tok, 1)], ALU.is_equal, ALU.mult)
                    ins.then_inc(hot_j_ready, 1)

                def gate_gelu(i, e):
                    dve.wait_ge(acc_ready, l * NREADY + R_G + 1 + (i * HOTS + e))
                    part = big[:, :, bass.ds(i * (4 * HOTS) + 4 * e, 4)].rearrange("p j t -> p t j")
                    nc.vector.tensor_tensor(part, acc[:, e % 2].rearrange("p (t j) -> p t j", t=4), part,
                                            ALU.mult).then_inc(acc_read[e % 2], 1)

                for e in range(2):
                    gated_rows(0, e)
                with dve.Fori(0, NG // HOTS - 1) as i:
                    for e in range(HOTS):
                        gated_rows(i, e + 2)
                        gate_gelu(i, e)
                for e in range(HOTS):
                    if e + 2 < HOTS:
                        gated_rows(NG // HOTS - 1, e + 2)
                    gate_gelu(NG // HOTS - 1, e)

                def split_w_lo(nth, j, s):
                    dve.wait_ge(w_hi_done, l * NKEYS + nth + 1)
                    nc.vector.tensor_tensor(w_lo[:, s], big[:, j], w_hi[:, s].bitcast(F32), ALU.subtract).then_inc(w_lo_done, 1)

                for b in range(2):
                    dve.wait_ge(acc_read[b], OPEN + l * (NACC // 2) + NACC // 2)
                for j in range(AHEAD):
                    split_w_lo(j, j, j)
                with dve.Fori(0, NKEYS // SLOTS - 1) as i:
                    for e in range(SLOTS):
                        n = T_V + e + AHEAD
                        split_lo(l, (i + n // SLOTS), n % SLOTS)
                        j = i * SLOTS + (e + AHEAD)
                        split_w_lo(j, j, n % SLOTS)
                split_lo(l, TURNS - 1, SLOTS - 1)
                split_w_lo(NKEYS - 1, NKEYS - 1, SLOTS - 1)
                add_branch(1, NT - 1, W_V)
                normalise(3 * l + 3, l * 64 + 96, st)
                st.end()

        @block.tensor
        def _(pe_):
            mm = nc.tensor.matmul

            def tile_ready(l, q, s):
                pe_.wait_ge(lo_done, l * NT + q * SLOTS + s + 1)

            def acc_free(l, use):
                pe_.wait_ge(acc_read[use % 2], OPEN + l * (NACC // 2) + use // 2)

            def tr_free(l, use):
                pe_.wait_ge(tr_read[use % 2], OPEN + l * (NTR // 2) + use // 2)

            def wide_free(l, use):
                for tt in range(TT):
                    pe_.wait_ge(wide_read[tt], OPEN + l * NWIDE + use)

            def columns_tile(s, xh, xl, bank):
                for k in range(DK):
                    c = slice(k * P, (k + 1) * P)
                    dst = acc[:, bank, :SEQ]
                    mm(dst, lo[:, s, c], xh[:, k], start=k == 0, stop=False)
                    mm(dst, hi[:, s, c], xl[:, k], start=False, stop=False)
                    ins = mm(dst, hi[:, s, c], xh[:, k], start=False, stop=k == DK - 1)
                ins.then_inc(slot_free[s], 1)

            def rows_tile(s, ah, al, first, last, width, offsets, tts=range(TT)):
                for tt in tts:
                    tok = slice(tt * P, (tt + 1) * P)
                    for k, (a, w) in enumerate(((al, hi), (ah, lo), (ah, hi))):
                        for h, off in enumerate(offsets):
                            ins = mm(wide[:, tt, 512 * h:512 * h + width], a[:, tok], w[:, s, off:off + width],
                                     start=first and k == 0, stop=last and k == 2)
                if TT - 1 in tts:
                    ins.then_inc(slot_free[s], 1)
                elif last:
                    ins.then_inc(half_ready, 1)

            for free in (*acc_read, *tr_read, *wide_read):
                pe_.sem_inc(free, OPEN)
            pe_.wait_ge(consts_ready, 1)
            pe_.wait_ge(masks_ready, 2)
            with pe_.Fori(0, DEPTH) as l:
                def transpose_x(first, nth):
                    for g in range(4):
                        tt, cg = divmod(g, 2)
                        pe_.wait_ge(x_ready, nth + tt + 1)
                        tr_free(l, first + g)
                        for c in range(4):
                            ins = nc.tensor.transpose(tr[:, (first + g) % 2, c * P:(c + 1) * P],
                                                      xs[:, tt, (4 * cg + c) * P:(4 * cg + c + 1) * P], ident[:])
                        ins.then_inc(tr_ready, 1)

                def xT_written(first):
                    for b in range(2):
                        pe_.wait_ge(tr_read[b], OPEN + l * (NTR // 2) + first // 2 + 2)

                transpose_x(X_XT, l * 4)
                xT_written(X_XT)
                for c in range(N_LAT):
                    n = T_LAT + c
                    acc_free(l, A_LAT + c)
                    tile_ready(l, n // SLOTS, n % SLOTS)
                    columns_tile(n % SLOTS, xT_hi, xT_lo, c % 2)
                pe_.wait_ge(sq_done, l * N_LAT + N_LAT)
                for b, chunks in enumerate((range(0, 6), range(6, 8))):
                    acc_free(l, A_RMS + b)
                    for tt in range(TT):
                        for c in chunks:
                            ins = mm(acc[:, b, tt:tt + 1], sq[:, c, tt * P:(tt + 1) * P], ones[:, 0:1],
                                     start=c == chunks[0], stop=c == chunks[-1])
                    ins.then_inc(acc_ready, 1)
                wide_free(l, W_UQ)
                for c in range(N_UQ):
                    n = T_UQ + c
                    pe_.wait_ge(lat_ready, OPEN + l * N_LAT + c + 1)
                    tile_ready(l, n // SLOTS, n % SLOTS)
                    rows_tile(n % SLOTS, cq_hi[:, c], cq_lo[:, c], c == 0, c == N_UQ - 1, 384, (0, 384))
                for b in range(2):
                    acc_free(l, A_B + b)
                for q in range(N_B):
                    n = T_B + q
                    tile_ready(l, n // SLOTS, n % SLOTS)
                    s = n % SLOTS
                    for kk in range(2):
                        k = 2 * q + kk
                        c = slice(kk * WB, (kk + 1) * WB)
                        for tt in range(TT):
                            tok = slice(tt * P, (tt + 1) * P)
                            dst = acc[:, tt, :WB]
                            mm(dst, xT_lo[:, k, tok], hi[:, s, c], start=k == 0, stop=False)
                            mm(dst, xT_hi[:, k, tok], lo[:, s, c], start=False, stop=False)
                            ins = mm(dst, xT_hi[:, k, tok], hi[:, s, c], start=False, stop=k == DK - 1)
                    ins.then_inc(slot_free[s], 1)
                wide_free(l, W_UKV)
                for c in range(N_UKV):
                    n = T_UKV + c
                    pe_.wait_ge(lat_ready, OPEN + l * N_LAT + N_UQ + c + 1)
                    tile_ready(l, n // SLOTS, n % SLOTS)
                    rows_tile(n % SLOTS, cq_hi[:, 6 + c], cq_lo[:, 6 + c], c == 0, c == 1, 512, (0, 512))

                def gate_tile(c):
                    n = MG_TILE[c]
                    acc_free(l, MG_USE[c])
                    tile_ready(l, n // SLOTS, n % SLOTS)
                    columns_tile(n % SLOTS, xT_hi, xT_lo, MG_USE[c] % 2)

                for c in range(MG_EARLY):
                    gate_tile(c)
                wide_free(l, W_A)
                for k in range(N_A):
                    n = T_A + k
                    tile_ready(l, n // SLOTS, n % SLOTS)
                    rows_tile(n % SLOTS, xT_hi[:, k], xT_lo[:, k], k == 0, k == N_A - 1, 512, (0, 512))

                def transpose_heads(use, sources, rows):
                    tr_free(l, use)
                    pe_.sem_inc(apart, 1)
                    for j, src in enumerate(sources):
                        ins = nc.tensor.transpose(tr[:rows, use % 2, j * P:(j + 1) * P], src, ident[:])
                    ins.then_inc(tr_ready, 1)

                for c in range(MG_EARLY, 4):
                    gate_tile(c)
                pe_.wait_ge(qk_ready, l * TT + TT)
                for use, src in ((X_Q, q_tok), (X_K, k_tok)):
                    for g in range(4):
                        tt, hg = divmod(g, 2)
                        transpose_heads(use + g, [src[:, tt, 4 * hg + j] for j in range(4)], QKD)
                pe_.wait_ge(tok_ready, l * TT + TT)
                for g in range(4):
                    tt, hg = divmod(g, 2)
                    transpose_heads(X_NQ + g, [rot[:, tt, 4 * hg + j] for j in range(4)], HD)
                for tt in range(TT):
                    transpose_heads(X_KT + tt, [rot[:, tt, HEADS + GROUPS + j] for j in range(4)], HD)
                for tt in range(TT):
                    transpose_heads(X_CD + tt, [cmp_tok[:, tt, c, g].rearrange("p a d -> p (a d)")
                                                for c in range(2) for g in range(GROUPS)], P)
                pe_.wait_ge(w1_loaded, l * 16 + 16)
                pe_.wait_ge(blk_ready, l * 8 + 8)
                acc_free(l, A_HID)
                nb = GROUPS * NCMP
                for c in range(2):
                    for r in range(16):
                        ins = mm(acc[:, A_HID % 2, c * nb:(c + 1) * nb], w1[:, c, r], blk[:, c, r], start=r == 0, stop=r == 15)
                ins.then_inc(acc_ready, 1)
                gate_tile(4)
                pe_.wait_ge(acc_read[A_HID % 2], OPEN + l * (NACC // 2) + A_HID // 2 + 1)
                acc_free(l, A_KCVC)
                b = A_KCVC % 2
                mm(acc[:HD, b, 0:nb], w2[:, 0], hid[:, 0], start=True, stop=True)
                for g in range(GROUPS):
                    ins = mm(acc[:NCMP, b, 64 + g * HD:64 + (g + 1) * HD], hid[:, 1, g * NCMP:(g + 1) * NCMP], w2[:, 1],
                             start=True, stop=True)
                ins.then_inc(acc_ready, 1)
                gate_tile(5)
                pe_.wait_ge(acc_read[b], OPEN + l * (NACC // 2) + A_KCVC // 2 + 1)
                for tt in range(TT):
                    acc_free(l, A_CS + tt)
                    for h in range(HEADS):
                        g = h // 4
                        ins = mm(acc[:, (A_CS + tt) % 2, h * 16:h * 16 + NCMP], nqT[:, h, tt * P:(tt + 1) * P],
                                 kc[:, g * NCMP:(g + 1) * NCMP], start=True, stop=True)
                    ins.then_inc(acc_ready, 1)
                gate_tile(6)
                gate_tile(7)
                for tt in range(TT):
                    pe_.wait_ge(cmp_ready, l * TT + tt + 1)
                    for hg in range(2):
                        transpose_heads(X_PC + 2 * tt + hg, [cs[:, tt, 4 * hg + j, :NCMP] for j in range(4)], NCMP)

                def scores(u):
                    kind, hg, tt, oi, trs = unit(u)
                    keys_n = (tt + 1) * P
                    if u < 2:
                        pe_.wait_ge(wide_read[u], OPEN + l * NWIDE + W_OUT)
                    else:
                        pe_.wait_ge(exp_ready, l * NU + u - 1)
                    for h in range(4):
                        dst = wide[:, u % 2, 256 * h:256 * h + keys_n]
                        tok = slice(tt * P, (tt + 1) * P)
                        if kind == "mla":
                            mm(dst, qT[:QKD, 4 * hg + h, tok], kT[:QKD, 4 * hg + h, :keys_n], start=True, stop=False)
                        else:
                            kk = nkT[:, (0 if kind == "sel" else GROUPS) + hg, :keys_n]
                            mm(dst, nqT[:, 4 * hg + h, tok], kk, start=True, stop=False)
                        ins = mm(dst[:, keys_n - P:], ident_r[:], causal_r[:], start=False, stop=True)
                    ins.then_inc(wide_ready, 1)

                def transpose_p(u):
                    kind, hg, tt, oi, trs = unit(u)
                    pe_.wait_ge(p_ready, l * NU + u + 1)
                    for kb, use in enumerate(trs):
                        transpose_heads(use, [sc[:, u % 2, h, kb * P:(kb + 1) * P] for h in range(4)], P)

                def outputs(u):
                    kind, hg, tt, oi, trs = unit(u)
                    bank = O_USE[oi] % 2
                    first = kind != "win"
                    if first:
                        acc_free(l, O_USE[oi])
                    if kind == "sel":
                        if hg == 0:
                            for b in range(2):
                                pe_.wait_ge(tr_read[b], OPEN + l * (NTR // 2) + X_PC // 2 + tt + 1)
                        for h in range(4):
                            mm(acc[:, bank, h * HD:(h + 1) * HD], pcT[:NCMP, 4 * hg + h, tt * P:(tt + 1) * P], vc[:NCMP, hg],
                               start=first, stop=False, skip_group_check=True)
                            first = False
                    for kb, use in enumerate(trs):
                        pe_.wait_ge(tr_read[use % 2], OPEN + l * (NTR // 2) + use // 2 + 1)
                    for h in range(4):
                        for kb in range(tt + 1):
                            if kind == "mla":
                                v = v_mla[:, kb, 4 * hg + h]
                            else:
                                v = (v_sel if kind == "sel" else v_win)[:, kb, hg * HD:(hg + 1) * HD]
                            ins = mm(acc[:, bank, h * HD:(h + 1) * HD], pT[:, u % 2, kb, h * P:(h + 1) * P], v,
                                     start=first, stop=kind != "sel" and h == 3 and kb == tt, skip_group_check=True)
                            first = False
                    if kind != "sel":
                        ins.then_inc(acc_ready, 1)

                scores(0)
                for u in range(NU):
                    if u + 1 < NU:
                        scores(u + 1)
                    if u + 8 < N_MG:
                        gate_tile(u + 8)
                    transpose_p(u)
                    if u >= 1:
                        outputs(u - 1)
                outputs(NU - 1)
                for b in range(2):
                    pe_.wait_ge(acc_read[b], OPEN + l * (NACC // 2) + A_BR // 2)
                for g in range(4):
                    kind, tt = divmod(g, 2)
                    transpose_heads(X_OT + g, [o_tok[:, tt, kind, c * P:(c + 1) * P] for c in range(4)], P)
                for b in range(2):
                    pe_.wait_ge(tr_read[b], OPEN + l * (NTR // 2) + X_OT // 2 + 2)
                for c in range(N_BR):
                    n = T_BR + c
                    s = n % SLOTS
                    acc_free(l, A_BR + c)
                    tile_ready(l, n // SLOTS, s)
                    for f in range(2):
                        for k in range(4):
                            w = slice(k * 256 + f * P, k * 256 + f * P + P)
                            dst = acc[:, c % 2, f * SEQ:(f + 1) * SEQ]
                            mm(dst, lo[:, s, w], oT_hi[:, c % 2, k], start=k == 0, stop=False)
                            mm(dst, hi[:, s, w], oT_lo[:, c % 2, k], start=False, stop=False)
                            ins = mm(dst, hi[:, s, w], oT_hi[:, c % 2, k], start=False, stop=k == 3)
                    ins.then_inc(slot_free[s], 1)
                wide_free(l, W_OUT)
                for k in range(N_OUT - SLOTS):
                    n = T_OUT + k
                    pe_.wait_ge(mixed_ready, OPEN + l * 4 + k // 2 + 1)
                    tile_ready(l, n // SLOTS, n % SLOTS)
                    rows_tile(n % SLOTS, xT_hi[:, k], xT_lo[:, k], k == 0, False, 512, (0, 512))
                for tt in range(TT):
                    for k in range(N_OUT - SLOTS, N_OUT):
                        n = T_OUT + k
                        pe_.wait_ge(mixed_ready, OPEN + l * 4 + k // 2 + 1)
                        tile_ready(l, n // SLOTS, n % SLOTS)
                        rows_tile(n % SLOTS, xT_hi[:, k], xT_lo[:, k], False, k == N_OUT - 1, 512, (0, 512), (tt,))
                transpose_x(X_XT2, l * 4 + 2)
                xT_written(X_XT2)
                pe_.sem_inc(apart, 1)
                with pe_.Fori(0, N_PQ // SLOTS) as i:
                    for e in range(SLOTS):
                        s, q = (T_PQ + e) % SLOTS, (T_PQ + e) // SLOTS
                        pe_.wait_ge(acc_read[e % 2], OPEN + l * (NACC // 2) + (i * 2 + (A_PQ + e) // 2))
                        tile_ready(l, (i + q), s)
                        columns_tile(s, xT_hi, xT_lo, e % 2)
                pe_.wait_ge(keys_loaded, l * 16 + 16)
                for b in range(2):
                    pe_.wait_ge(acc_read[b], OPEN + l * (NACC // 2) + A_SCR // 2)
                for c in range(4):
                    for p in range(2):
                        acc_free(l, A_SCR + 2 * c + p)
                        rows = slice(p * HD, (p + 1) * HD)
                        for r in range(4):
                            tt, h = divmod(4 * c + r, HEADS)
                            ins = mm(acc[:, p, r * P:(r + 1) * P], pqT[rows, h, tt * P:(tt + 1) * P], keys[rows, h],
                                     start=True, stop=True)
                        ins.then_inc(acc_ready, 1)
                with pe_.Fori(0, NKEYS // 8) as i:
                    for e in range(8):
                        s, q = (T_U + e) % SLOTS, (T_U + e) // SLOTS
                        pe_.wait_ge(acc_read[e % 2], OPEN + l * (NACC // 2) + (i * 4 + (A_U + e) // 2))
                        tile_ready(l, (i * 2 + q), s)
                        columns_tile(s, xT_hi, xT_lo, e % 2)
                pe_.wait_ge(picks_ready, l + 1)
                transpose_heads(X_PK, [picks[:, a, tt] for a in range(2) for tt in range(TT)], P)
                transpose_heads(X_PK + 1, [picks[:, 2, tt] for tt in range(TT)], P)
                with pe_.Fori(0, NG // HOTS) as i:
                    for e in range(HOTS):
                        pe_.wait_ge(acc_read[e % 2], OPEN + l * (NACC // 2) + (i * 2 + (A_G + e) // 2))
                        pe_.wait_ge(hot_i_ready, l * NG + (i * HOTS + (e + 1)))
                        pe_.wait_ge(hot_j_ready, l * NG + (i * HOTS + (e + 1)))
                        for r in range(4):
                            ins = mm(acc[:, e % 2, r * P:(r + 1) * P], hot_i[:, e, r], hot_j[:, e, r], start=True, stop=True)
                        ins.then_inc(acc_ready, 1)
                wide_free(l, W_V)
                pe_.sem_inc(apart, 1)

                def v_tile(i, e, first, last, tts=range(TT)):
                    s, q = (T_V + e) % SLOTS, (T_V + e) // SLOTS
                    pe_.wait_ge(w_lo_done, l * NKEYS + (i * SLOTS + (e + 1)))
                    tile_ready(l, (i + q), s)
                    rows_tile(s, w_hi[:, s], w_lo[:, s], first, last, 512, (0, 512), tts)

                for e in range(SLOTS):
                    v_tile(0, e, e == 0, False)
                with pe_.Fori(1, NKEYS // SLOTS - 1) as i:
                    for e in range(SLOTS):
                        v_tile(i, e, False, False)
                for tt in range(TT):
                    for e in range(SLOTS):
                        v_tile(NKEYS // SLOTS - 1, e, False, e == SLOTS - 1, (tt,))


DVE_STEPS = 92
ROUTE_STEPS = 25


def lay_out(a):
    L = DEPTH
    w_in = a["w_in"]

    def columns(w, first, width=P):
        part = w[:, first:first + width]
        return part.reshape(-1, P, width).transpose(1, 0, 2).reshape(P, -1)

    front = np.zeros((L, FRONT, P, 1024), np.float32)
    for l in range(L):
        w = w_in[l]
        wa = np.concatenate([w[:, c:c + n] for c, n in COLS_A], axis=1)
        wb = np.concatenate([w[:, c:c + n] for c, n in COLS_B], axis=1)
        for c in range(N_LAT):
            front[l, T_LAT + c] = columns(w, c * P)
        for c in range(N_UQ):
            front[l, T_UQ + c, :, :HEADS * QKD] = a["mla_w_uq"][l, c * P:(c + 1) * P]
        for c in range(N_UKV):
            front[l, T_UKV + c] = a["mla_w_ukv"][l, c * P:(c + 1) * P]
        for q in range(N_B):
            front[l, T_B + q, :, :2 * WB] = columns(wb[q * 2 * P:(q + 1) * 2 * P], 0, WB)
        for k in range(N_A):
            front[l, T_A + k] = wa[k * P:(k + 1) * P]
        for c in range(N_MG):
            front[l, MG_TILE[c]] = columns(w, C_MG + c * P)
        for q in range(4):
            front[l, T_BR + 2 * q] = columns(a["w_branch_mla"][l], q * 256, 256)
            front[l, T_BR + 2 * q + 1] = columns(a["w_branch_nsa"][l], q * 256, 256)
        for k in range(N_OUT):
            front[l, T_OUT + k] = a["w_out"][l, k * P:(k + 1) * P]
        for h in range(N_PQ):
            front[l, T_PQ + h] = columns(a["peer_w_query"][l], h * P)

    def odd_even(x, width):
        return x.reshape(L, 16, 2, HD, width).transpose(0, 2, 3, 1, 4).reshape(L, P, 16, width)

    got = {
        "x": a["x"].reshape(TT, P, D).transpose(1, 0, 2),
        "positions": a["positions"].reshape(TT, P).T,
        "freq": np.concatenate([10000.0 ** (-np.arange(0, d, 2, dtype=np.float64) / d) for d in (ROPE, HD)]).astype(np.float32),
        "ln": np.stack([np.stack([a["ln_in_g"], a["ln_in_b"]])] + [
            np.stack([a[f"ln{i}_g"][l], a[f"ln{i}_b"][l]]) for l in range(L) for i in (1, 2)]),
        "front": front,
        "lat_g": np.concatenate([a["mla_q_norm"], a["mla_kv_norm"]], axis=1).reshape(L, 8, P).transpose(0, 2, 1),
        "cmp_pe": np.stack([odd_even(a["nsa_cmp_k_pe"], 1)[..., 0], odd_even(a["nsa_cmp_v_pe"], 1)[..., 0]], axis=2),
        "cmp_w1": np.stack([odd_even(a["nsa_cmp_k_w1"], P), odd_even(a["nsa_cmp_v_w1"], P)], axis=2),
        "cmp_w2": np.stack([a["nsa_cmp_k_w2"], a["nsa_cmp_v_w2"]], axis=2),
        "sub_keys": a["peer_sub_keys"].transpose(0, 2, 4, 1, 3).reshape(L, P, HEADS, NKEYS),
        "peer_u": a["peer_u"].reshape(L, P, NKEYS, DK, P).transpose(0, 2, 4, 3, 1).reshape(L, NKEYS, P, 1024),
        "peer_v": a["peer_v"].reshape(L, P, NKEYS, D).transpose(0, 2, 1, 3),
    }
    got["positions"] = got["positions"].astype(np.int32)
    return {k: np.ascontiguousarray(v) for k, v in got.items()}


def kernel(**inputs):
    import concourse.bacc as bacc
    from concourse.bass_utils import run_bass_kernel_spmd

    arrays = lay_out({k: np.asarray(v) for k, v in inputs.items()})
    nc = bacc.Bacc("TRN2", target_bir_lowering=False, num_devices=1)
    t = {k: nc.dram_tensor(f"in_{k}", v.shape, mybir.dt.from_np(v.dtype), kind="ExternalInput").ap()
         for k, v in arrays.items()}
    out = nc.dram_tensor("out_0", (P, TT, D), F32, kind="ExternalOutput").ap()
    build(nc, t, out)
    r = run_bass_kernel_spmd(nc, [{f"in_{k}": v for k, v in arrays.items()}], core_ids=[0])
    return r.results[0]["out_0"].transpose(1, 0, 2).reshape(1, SEQ, D)
```

```python
from contextlib import ExitStack

import numpy as np

import concourse.bass as bass
from concourse import mybir

F32 = mybir.dt.float32
F32R = mybir.dt.float32r
I32 = mybir.dt.int32
U32 = mybir.dt.uint32
BF16 = mybir.dt.bfloat16
ALU = mybir.AluOpType
ACT = mybir.ActivationFunctionType
AX = mybir.AxisListType

P = 128
SEQ, D, DEPTH = 256, 1024, 2
TT = SEQ // P
DK = D // P
HEADS = 8
NOPE, ROPE, VDIM = 64, 32, 64
QKD = NOPE + ROPE
Q_RANK, KV_RANK = 768, 256
HD = 64
GROUPS = 2
CMP_BLOCK, CMP_STRIDE = 32, 16
NCMP = (SEQ - CMP_BLOCK) // CMP_STRIDE + 1
NKEYS, TOPK = 128, 16
ALPHA = (2 * DEPTH) ** 0.25
LN_EPS, RMS_EPS, NEG = 1e-5, 1e-6, -1e30
MLA_SCALE, NSA_SCALE = QKD ** -0.5, HD ** -0.5
LOWEST = -3.0e38
TWO_PI = 2 * np.pi
PI_A = 6.28125
PI_B = np.round((TWO_PI - PI_A) * 2.0 ** 20) / 2.0 ** 20
PI_C = float(np.float32(TWO_PI - PI_A - PI_B))
ROUND = 12582912.0

C_KR = Q_RANK + KV_RANK
C_NQ = C_KR + ROPE
C_KV = C_NQ + HEADS * HD
C_NG = C_KV + 6 * GROUPS * HD
C_MG = C_NG + 3 * HEADS
GW = GROUPS * HD
COLS_A = [(C_NQ, 512), (C_KV, GW), (C_KV + 2 * GW, GW), (C_KV + 4 * GW, GW), (C_KV + 5 * GW, GW)]
ROT = HEADS + 3 * GROUPS
COLS_B = [(C_KV + GW, GW), (C_KV + 3 * GW, GW), (C_KR, ROPE), (C_NG, 3 * HEADS)]
WB = 2 * GW + ROPE + 3 * HEADS

SLOTS = 4
N_LAT, N_UQ, N_UKV, N_B, N_A, N_MG, N_BR, N_OUT, N_PQ = 8, 6, 2, 4, 8, 16, 8, 8, 8
MG_EARLY = 2
T_LAT = 0
T_UQ = T_LAT + N_LAT
T_B = T_UQ + N_UQ
T_UKV = T_B + N_B
T_MG = T_UKV + N_UKV
T_A = T_MG + MG_EARLY
T_MG2 = T_A + N_A
T_BR = T_MG2 + N_MG - MG_EARLY
MG_TILE = [T_MG + c for c in range(MG_EARLY)] + [T_MG2 + c for c in range(N_MG - MG_EARLY)]
T_OUT = T_BR + N_BR
T_PQ = T_OUT + N_OUT
FRONT = T_PQ + N_PQ
T_U = FRONT
T_V = T_U + NKEYS
NT = T_V + NKEYS
TURNS = NT // SLOTS
AHEAD = 3
assert NT % SLOTS == 0 and FRONT % SLOTS == 0

A_LAT, A_RMS, A_B, A_HID, A_KCVC, A_CS, A_ATT, A_BR, A_PQ, A_SCR, A_U, A_G = (
    0, 8, 10, 17, 19, 20, 24, 40, 48, 56, 64, 192)
ATT_ORDER = "F0 F1 O0 F2 O1 F3 O2 F4 F5 O3 F6 F7 O4 O5 O6 O7".split()
O_USE = [A_ATT + ATT_ORDER.index(f"O{k}") for k in range(8)]
MG_USE = [12, 13, 14, 15, 16, 18, 22, 23] + [A_ATT + ATT_ORDER.index(f"F{k}") for k in range(8)]
NACC = 256
R_RMS, R_HID, R_KCVC, R_CS, R_O, R_SCR, R_G = 0, 2, 3, 4, 6, 14, 22
NREADY = R_G + SEQ // 4
NG = SEQ // 4
HOTS = 4
X_XT, X_Q, X_K, X_NQ, X_KT, X_CD, X_PC, X_AT, X_XT2, X_PK = 0, 4, 8, 12, 16, 18, 20, 24, 42, 46
NTR = 48
W_UQ, W_UKV, W_A, W_OUT, W_V = range(5)
NWIDE = 5
R_LAT, R_LN1, R_LN2 = TT, TT + 1, 2 * TT + 1
OPEN = 1
UNITS = [("mla", 0), ("mla", 1), ("sel", 0), ("win", 0), ("sel", 1), ("win", 1)]
NU = len(UNITS) * TT
O_OF = [0, 1, 2, 2, 3, 3]


def unit(u):
    tt, i = divmod(u, len(UNITS))
    kind, hg = UNITS[i]
    tr = [X_AT + u] if tt == 0 else [X_AT + 6 + 2 * (u - 6), X_AT + 7 + 2 * (u - 6)]
    return kind, hg, tt, tt * 4 + O_OF[i], tr


class Steps:

    def __init__(self, eng, sem, base, per_pass, apart=None):
        self.eng, self.sem, self.base, self.per_pass, self.n = eng, sem, base, per_pass, 0
        self.apart = apart

    def link(self, ins):
        ins.then_inc(self.sem, 1)
        self.n += 1
        self.eng.wait_ge(self.sem, self.base + self.n)
        if self.apart is not None:
            self.eng.sem_inc(self.apart, 1)

    def mark(self, ins):
        ins.then_inc(self.sem, 1)
        self.n += 1

    def settle(self):
        self.eng.wait_ge(self.sem, self.base + self.n)
        if self.apart is not None:
            self.eng.sem_inc(self.apart, 1)

    def end(self):
        assert self.n == self.per_pass, (self.n, self.per_pass)


def build(nc, t, out):
    with ExitStack() as ctx:
        def sem(name):
            return ctx.enter_context(nc.semaphore(name))

        base = 16512

        def at(name, shape, dt, offset):
            return nc.alloc_sbuf_tensor_at(name, shape, dt, offset=base + offset)

        K = 1024
        big = at("big", [P, NKEYS, SEQ], F32, 0)
        cq_hi = at("cq_hi", [P, 8, SEQ], F32R, 0)
        cq_lo = at("cq_lo", [P, 8, SEQ], F32R, 8 * K)
        oT_hi = at("oT_hi", [P, 2, 4, SEQ], F32R, 0)
        oT_lo = at("oT_lo", [P, 2, 4, SEQ], F32R, 8 * K)
        pqT = at("pqT", [P, HEADS, SEQ], F32, 0)
        q_tok = at("q_tok", [P, TT, HEADS, QKD], F32, 16 * K)
        k_tok = at("k_tok", [P, TT, HEADS, QKD], F32, 22 * K)
        v_mla = at("v_mla", [P, TT, HEADS, VDIM], F32, 28 * K)
        keys = at("keys", [P, HEADS, NKEYS], F32, 24 * K)
        qT = at("qT", [P, HEADS, SEQ], F32, 32 * K)
        kT = at("kT", [P, HEADS, SEQ], F32, 40 * K)
        ln_par = at("ln_par", [P, 2, D], F32, 40 * K)
        rot = at("rot", [P, TT, ROT, HD], F32, 48 * K)
        mix = at("mix", [P, 2, 2, 512], F32, 48 * K)
        v_win = at("v_win", [P, TT, GW], F32, 55 * K)
        v_sel = at("v_sel", [P, TT, GW], F32, 56 * K)
        cmp_tok = at("cmp_tok", [P, TT, 2, GROUPS, 2, HD], F32, 57 * K)
        rope_a = at("rope_a", [P, ROT * HD], F32, 61 * K)
        rope_b = at("rope_b", [P, ROT * HD], F32, 61 * K + 3584)
        nqT = at("nqT", [HD, HEADS, SEQ], F32, 68 * K)
        nkT = at("nkT", [HD, 4, SEQ], F32, 76 * K)
        cmpT = at("cmpT", [P, 4, SEQ], F32, 80 * K)
        blk = at("blk", [P, 2, 16, GROUPS * NCMP], F32, 84 * K)
        w1 = at("w1", [P, 2, 16, P], F32, 0)
        gates = at("gates", [P, 16, SEQ], F32, 88 * K)
        sq = at("sq", [P, 8, SEQ], F32, 104 * K)
        sc = at("sc", [P, 2, 4, SEQ], F32, 104 * K)
        pT = at("pT", [P, 2, 2, 512], F32, 112 * K)
        pcT = at("pcT", [16, HEADS, SEQ], F32, 120 * K)
        S0 = NKEYS - 16
        o = 128 * K
        xs = at("xs", [P, TT, D], F32, o)
        xT_hi = at("xT_hi", [P, DK, SEQ], F32R, o + 8 * K)
        xT_lo = at("xT_lo", [P, DK, SEQ], F32R, o + 16 * K)
        hot_i = at("hot_i", [P, HOTS, 4, P], F32, o + 8 * K)
        hot_j = at("hot_j", [P, HOTS, 4, P], F32, o + 16 * K)
        w_hi = at("w_hi", [P, SLOTS, SEQ], F32R, o + 16 * K)
        w_lo = at("w_lo", [P, SLOTS, SEQ], F32R, o + 20 * K)
        raw = at("raw", [P, SLOTS, 1024], F32, o + 24 * K)
        lo = at("lo", [P, SLOTS, 1024], F32R, o + 24 * K)
        hi = at("hi", [P, SLOTS, 1024], F32R, o + 40 * K)
        o += 56 * K
        where = [o]

        def small(name, shape, dt=F32):
            size = int(np.prod(shape[1:])) * (2 if dt == BF16 else 4)
            got = at(name, shape, dt, where[0])
            where[0] += (size + 31) // 32 * 32
            assert base + where[0] <= 229344
            return got

        ident = small("ident", [P, P])
        iota = small("iota", [P, P])
        causal = small("causal", [P, P])
        ident_r = small("ident_r", [P, P], F32R)
        causal_r = small("causal_r", [P, P], F32R)
        cmask = small("cmask", [P, TT, NCMP])
        cmask01 = small("cmask01", [P, TT, NCMP])
        cos_m = small("cos_m", [P, TT, ROPE])
        sin_m = small("sin_m", [P, TT, ROPE])
        cos_n = small("cos_n", [P, TT, HD])
        sin_n = small("sin_n", [P, TT, HD])
        ones = small("ones", [P, 2])
        neg_half = small("neg_half", [P, 4])
        picks = small("picks", [P, 3, TT, P])
        ident_b = small("ident_b", [P, P], BF16)
        minus_iota = small("minus_iota", [P, P], BF16)
        ones_b = small("ones_b", [P, P], BF16)
        places_b = small("places_b", [P, TT, P], BF16)
        picksT = small("picksT", [P, 3, SEQ])
        r_s = small("r_s", [P, 2, NKEYS])
        r_s2 = small("r_s2", [P, 2, NKEYS])
        r_v = small("r_v", [P, 2, TOPK])
        r_i = small("r_i", [P, 2, TOPK], U32)
        r_if = small("r_if", [P, 2, TOPK])
        r_c = small("r_c", [P, TOPK * TOPK])
        r_c2 = small("r_c2", [P, TOPK * TOPK])
        r_best = small("r_best", [P, TOPK])
        r_pos = small("r_pos", [P, TOPK], U32)
        r_ab = small("r_ab", [P, 2, TOPK], U32)
        r_abf = small("r_abf", [P, 2, TOPK])
        r_eq = small("r_eq", [P, 2, TOPK, TOPK])
        gsum = small("gsum", [P, TT * HEADS])
        stats = small("stats", [P, TT, 2, 6])
        mv = small("mv", [P, TT, 2])
        var = small("var", [P, 4])
        rstd = small("rstd", [P, 4])
        ngate = small("ngate", [P, TT, 3 * HEADS])
        kr = small("kr", [P, TT, ROPE])
        negmax = small("negmax", [P, 2, 4])
        sums = small("sums", [P, 2, 4])
        recip = small("recip", [P, 2, 4])
        cs = small("cs", [P, TT, HEADS, 16])
        cst = small("cst", [P, TT, 3, HEADS])
        lat_g = small("lat_g", [P, 8])
        pe = small("pe", [P, 2, 16])
        w2 = small("w2", [P, 2, HD])
        hid = small("hid", [P, 2, GROUPS * NCMP])
        kc = small("kc", [HD, GROUPS * NCMP])
        vc = small("vc", [16, GROUPS, HD])
        pos_i = small("pos_i", [P, TT], I32)
        pos_f = small("pos_f", [P, TT])
        freq = small("freq", [P, 48])
        ang = at("ang", [P, 4, TT, 48], F32, 0)
        warm = small("warm", [P, 2])

        acc = ctx.enter_context(nc.psum_tensor("acc", [P, 2, 512], F32))
        tr = ctx.enter_context(nc.psum_tensor("tr", [P, 2, 512], F32))
        wide = ctx.enter_context(nc.psum_tensor("wide", [P, TT, 1024], F32))

        loaded = [sem(f"loaded{s}") for s in range(SLOTS)]
        hi_done = sem("hi_done")
        lo_done = sem("lo_done")
        slot_free = [sem(f"slot_free{s}") for s in range(SLOTS)]
        acc_ready = sem("acc_ready")
        acc_read = [sem("acc_read0"), sem("acc_read1")]
        tr_ready = sem("tr_ready")
        tr_read = [sem("tr_read0"), sem("tr_read1")]
        wide_ready = sem("wide_ready")
        wide_read = [sem("wide_read0"), sem("wide_read1")]
        pos_loaded = sem("pos_loaded")
        x_loaded = [sem("x_loaded0"), sem("x_loaded1")]
        masks_ready = sem("masks_ready")
        consts_ready = sem("consts_ready")
        tables_step = sem("tables_step")
        angles_ready = sem("angles_ready")
        sines_ready = sem("sines_ready")
        small_loaded = sem("small_loaded")
        keys_loaded = sem("keys_loaded")
        w1_loaded = sem("w1_loaded")
        half_ready = sem("half_ready")
        qk_ready = sem("qk_ready")
        gates_ready = sem("gates_ready")
        ln_loaded = sem("ln_loaded")
        x_ready = sem("x_ready")
        tr_hi = sem("tr_hi")
        var_ready = sem("var_ready")
        rstd_ready = sem("rstd_ready")
        sq_done = sem("sq_done")
        lat_hi = sem("lat_hi")
        mix_sum = sem("mix_sum")
        o_hi = sem("o_hi")
        mix_hi = sem("mix_hi")
        ngate_ready = sem("ngate_ready")
        tok_ready = sem("tok_ready")
        blk_ready = sem("blk_ready")
        cmp_shifted = sem("cmp_shifted")
        cmp_exp = sem("cmp_exp")
        cmp_ready = sem("cmp_ready")
        max_ready = sem("max_ready")
        exp_ready = sem("exp_ready")
        p_ready = sem("p_ready")
        mixed_ready = sem("mixed_ready")
        best_ready = sem("best_ready")
        gate_exp = sem("gate_exp")
        picks_ready = sem("picks_ready")
        distance_done = sem("distance_done")
        apart_j_ready = sem("apart_j_ready")
        whole_ready = sem("whole_ready")
        hot_i_ready = sem("hot_i_ready")
        hot_i_odd = sem("hot_i_odd")
        hot_j_ready = sem("hot_j_ready")
        w_hi_done = sem("w_hi_done")
        w_lo_done = sem("w_lo_done")
        dve_step = sem("dve_step")
        route_step = sem("route_step")
        ln_step = sem("ln_step")
        pool_step = sem("pool_step")
        warm_step = sem("warm_step")
        stored = sem("stored")
        apart = sem("apart")

        block = ctx.enter_context(nc.Block())

        @block.sync
        def _(sp):
            for free in slot_free:
                sp.sem_inc(free, OPEN)
            sp.dma_start(pos_i[:], t["positions"]).then_inc(pos_loaded, 16)
            sp.dma_start(freq[:], t["freq"].partition_broadcast(P)).then_inc(pos_loaded, 16)
            for tt in range(TT):
                sp.dma_start(xs[:, tt], t["x"][:, tt]).then_inc(x_loaded[tt], 16)

            def load(l, src, first, turns):
                with sp.Fori(0, turns) as q:
                    for s in range(SLOTS):
                        turn = l * TURNS + (q + first // SLOTS)
                        sp.wait_ge(slot_free[s], OPEN + turn)
                        sp.dma_start(raw[:, s], src[l, q * SLOTS + s]).then_inc(loaded[s], 16)

            with sp.Fori(0, DEPTH) as l:
                load(l, t["front"], 0, FRONT // SLOTS)
                load(l, t["peer_u"], T_U, NKEYS // SLOTS)
                load(l, t["peer_v"], T_V, NKEYS // SLOTS)
            sp.wait_ge(x_ready, TT * (1 + 2 * DEPTH))
            sp.dma_start(out, xs[:]).then_inc(stored, 16)
            sp.wait_ge(stored, 16)

        @block.gpsimd
        def _(pool):
            pst = Steps(pool, pool_step, 0, 10)

            def ln_load(i):
                for r in range(2):
                    pool.dma_start(ln_par[:, r], t["ln"][i, r].partition_broadcast(P)).then_inc(ln_loaded, 16)

            ln_load(0)
            pst.link(nc.gpsimd.memset(ident[:], 0.0))
            pst.link(nc.gpsimd.affine_select(ident[:], ident[:], [[-1, P]], ALU.not_equal, 1.0, 0, 1))
            pst.link(nc.gpsimd.iota(iota[:], [[1, P]], 0, 0, allow_small_or_imprecise_dtypes=True))
            pst.link(nc.gpsimd.memset(causal[:], 0.0))
            pst.link(nc.gpsimd.affine_select(causal[:], causal[:], [[-1, P]], ALU.is_ge, NEG, 0, 1))
            pst.link(nc.gpsimd.memset(cmask[:], 0.0))
            pst.link(nc.gpsimd.memset(cmask01[:], 1.0))
            pat = [[P, TT], [-CMP_STRIDE, NCMP]]
            pst.link(nc.gpsimd.affine_select(cmask[:], cmask[:], pat, ALU.is_ge, NEG, 1 - CMP_BLOCK, 1))
            pst.link(nc.gpsimd.affine_select(cmask01[:], cmask01[:], pat, ALU.is_ge, 0.0, 1 - CMP_BLOCK, 1))
            nc.gpsimd.memset(ones[:], 1.0)
            pst.link(nc.gpsimd.memset(neg_half[:], -0.5))
            pst.end()
            nc.gpsimd.memset(warm[:], 0.0).then_inc(consts_ready, 1)

            def rsqrt(n, a, b):
                pool.wait_ge(var_ready, n + 1)
                nc.gpsimd.tensor_tensor(rstd[:, a:b], var[:, a:b], neg_half[:, a:b], ALU.pow).then_inc(rstd_ready, 1)

            for tt in range(TT):
                rsqrt(tt, tt, tt + 1)
            with pool.Fori(0, DEPTH) as l:
                pool.wait_ge(slot_free[SLOTS - 1], OPEN + l * TURNS)
                pool.dma_start(lat_g[:], t["lat_g"][l]).then_inc(small_loaded, 16)
                pool.dma_start(pe[:], t["cmp_pe"][l]).then_inc(small_loaded, 16)
                pool.dma_start(w2[:], t["cmp_w2"][l]).then_inc(small_loaded, 16)
                rsqrt(5 * l + R_LAT, 0, 2 * TT)
                pool.wait_ge(slot_free[(T_MG - 1) % SLOTS], OPEN + l * TURNS + (T_MG - 1) // SLOTS + 1)
                pool.dma_start(w1[:], t["cmp_w1"][l]).then_inc(w1_loaded, 16)
                pool.wait_ge(tr_ready, l * NTR + X_NQ)
                pool.dma_start(keys[:], t["sub_keys"][l]).then_inc(keys_loaded, 16)
                pool.wait_ge(acc_ready, l * NREADY + R_SCR)
                for r in range(2):
                    pool.dma_start(ln_par[:, r], t["ln"][l * 2 + 1, r].partition_broadcast(P)).then_inc(ln_loaded, 16)
                for tt in range(TT):
                    rsqrt(5 * l + R_LN1 + tt, tt, tt + 1)
                pool.wait_ge(w_lo_done, l * NKEYS + 48)
                for r in range(2):
                    pool.dma_start(ln_par[:, r], t["ln"][l * 2 + 2, r].partition_broadcast(P)).then_inc(ln_loaded, 16)
                for tt in range(TT):
                    rsqrt(5 * l + R_LN2 + tt, tt, tt + 1)

        @block.scalar
        def _(act):
            def split_hi(l, q, s):
                act.wait_ge(loaded[s], (l * TURNS + q + 1) * 16)
                nc.scalar.activation(hi[:, s], raw[:, s], ACT.Identity).then_inc(hi_done, 1)

            def tile_step(l, n):
                split_hi(l, (n + AHEAD) // SLOTS, (n + AHEAD) % SLOTS)

            def tile_used(l, q, s):
                act.wait_ge(slot_free[s], OPEN + l * TURNS + q + 1)

            def tr_copy(l, i, dst, src):
                act.wait_ge(tr_ready, l * NTR + i + 1)
                nc.scalar.activation(dst, src, ACT.Identity).then_inc(tr_read[i % 2], 1)

            def warm_up(func, n):
                nc.scalar.activation(warm[:, 1:2], warm[:, 0:1], func).then_inc(warm_step, 1)
                act.wait_ge(warm_step, n)

            act.wait_ge(consts_ready, 1)
            nc.scalar.activation(ident_r[:], ident[:], ACT.Identity).then_inc(masks_ready, 1)
            nc.scalar.activation(causal_r[:], causal[:], ACT.Identity).then_inc(masks_ready, 1)
            act.wait_ge(angles_ready, 1)
            nc.scalar.activation(ang[:, 2], ang[:, 0], ACT.Sin).then_inc(sines_ready, 1)
            nc.scalar.activation(ang[:, 3], ang[:, 1], ACT.Sin).then_inc(sines_ready, 1)

            with act.Fori(0, DEPTH) as l:
                warm_up(ACT.Gelu, l * 2 + 1)
                for n in range(AHEAD):
                    split_hi(l, 0, n)

                def transposed_hi(first, hi_first, dst):
                    for g in range(4):
                        act.wait_ge(tr_ready, l * NTR + first + g + 1)
                        nc.scalar.activation(dst(g), tr[:, (first + g) % 2].rearrange("p (c t) -> p c t", c=4),
                                             ACT.Identity).then_inc(tr_hi, 1)

                def xT_part(g):
                    tt, cg = divmod(g, 2)
                    return xT_hi[:, 4 * cg:4 * cg + 4, tt * P:(tt + 1) * P]

                transposed_hi(X_XT, 0, xT_part)
                for c in range(N_LAT):
                    tile_used(l, (T_LAT + c) // SLOTS, (T_LAT + c) % SLOTS)
                    nc.scalar.activation(sq[:, c], acc[:, c % 2, :SEQ], ACT.Square).then_inc(sq_done, 1)
                    if c == 0:
                        act.wait_ge(small_loaded, l * 48 + 48)
                    nc.scalar.activation(cq_hi[:, c], acc[:, c % 2, :SEQ], ACT.Identity,
                                         scale=lat_g[:, c:c + 1]).then_inc(lat_hi, 1)
                    tile_step(l, T_LAT + c)
                for n in range(T_UQ, T_UKV):
                    tile_step(l, n)
                n = T_UKV - 1
                tile_used(l, n // SLOTS, n % SLOTS)
                for tt in range(TT):
                    nc.scalar.activation(ngate[:, tt], acc[:, tt, 2 * GW + ROPE:WB], ACT.Sigmoid).then_inc(ngate_ready, 1)
                for n in range(T_UKV, T_MG):
                    tile_step(l, n)

                def gate_copy(c, split=True):
                    n, use = MG_TILE[c], MG_USE[c]
                    tile_used(l, n // SLOTS, n % SLOTS)
                    nc.scalar.activation(gates[:, c], acc[:, use % 2, :SEQ], ACT.Identity).then_inc(acc_read[use % 2], 1)
                    if split:
                        tile_step(l, n)

                for c in range(MG_EARLY):
                    gate_copy(c)
                for n in range(T_A, T_MG2):
                    tile_step(l, n)
                for c in range(MG_EARLY, 4):
                    gate_copy(c)

                def heads_copy(i, part, width, bank, scale=1.0):
                    act.wait_ge(tr_ready, l * NTR + i + 1)
                    nc.scalar.activation(part, tr[:width, bank].rearrange("p (h t) -> p h t", h=4), ACT.Identity,
                                         scale=scale).then_inc(tr_read[bank], 1)

                for first, dst in ((X_Q, qT), (X_K, kT)):
                    for g in range(4):
                        tt, hg = divmod(g, 2)
                        heads_copy(first + g, dst[:QKD, 4 * hg:4 * hg + 4, tt * P:(tt + 1) * P], QKD, g % 2)
                for g in range(0, 4, 2):
                    tt, hg = divmod(g, 2)
                    heads_copy(X_NQ + g, nqT[:, 4 * hg:4 * hg + 4, tt * P:(tt + 1) * P], HD, 0, NSA_SCALE)
                heads_copy(X_KT, nkT[:, :, 0:P], HD, 0)
                heads_copy(X_CD, cmpT[:, :, 0:P], P, 0)
                gate_copy(4)
                act.wait_ge(acc_ready, l * NREADY + R_HID + 1)
                nc.scalar.activation(hid[:], acc[:, A_HID % 2, :2 * GROUPS * NCMP].rearrange("p (c n) -> p c n", c=2),
                                     ACT.Gelu).then_inc(acc_read[A_HID % 2], 1)
                gate_copy(5)
                for tt in range(TT):
                    act.wait_ge(cmp_shifted, l * TT + tt + 1)
                    nc.scalar.activation(cs[:, tt, :, :NCMP], cs[:, tt, :, :NCMP], ACT.Exp).then_inc(cmp_exp, 1)
                gate_copy(6)
                gate_copy(7)
                for tt in range(TT):
                    i = X_PC + 2 * tt
                    tr_copy(l, i, pcT[:NCMP, 0:4, tt * P:(tt + 1) * P],
                            tr[:NCMP, 0].rearrange("p (h t) -> p h t", h=4))

                def copy_o(oi):
                    act.wait_ge(acc_ready, l * NREADY + R_O + oi + 1)
                    tt, i = divmod(oi, 4)
                    bank = O_USE[oi] % 2
                    nc.scalar.activation(oT_hi[:, i // 2, 2 * (i % 2):2 * (i % 2) + 2, tt * P:(tt + 1) * P],
                                         acc[:, bank, :256].rearrange("p (c t) -> p c t", c=2), ACT.Identity).then_inc(o_hi, 1)

                def copy_pT(u):
                    for kb, i in enumerate(unit(u)[4]):
                        if i % 2 == 0:
                            tr_copy(l, i, pT[:, u % 2, kb], tr[:, 0])

                def exp_scores(u):
                    tt = unit(u)[2]
                    if u >= 2:
                        act.wait_ge(tr_ready, l * NTR + unit(u - 2)[4][-1] + 1)
                    act.wait_ge(max_ready, l * NU + u + 1)
                    for h in range(4):
                        ins = nc.scalar.activation(sc[:, u % 2, h, :(tt + 1) * P],
                                                   wide[:, u % 2, 256 * h:256 * h + (tt + 1) * P],
                                                   ACT.Exp, bias=negmax[:, u % 2, h:h + 1],
                                                   accum_out=sums[:, u % 2, h:h + 1])
                    ins.then_inc(exp_ready, 1)

                exp_scores(0)
                for u in range(NU + 1):
                    if u + 1 < NU:
                        exp_scores(u + 1)
                    if u + 8 < N_MG:
                        gate_copy(u + 8, False)
                    if u < NU:
                        copy_pT(u)
                    if u + 8 < N_MG:
                        tile_step(l, MG_TILE[u + 8])
                    if u >= 1 and (u == NU or unit(u - 1)[3] != unit(u)[3]):
                        copy_o(unit(u - 1)[3])
                for b in range(2):
                    act.wait_ge(acc_read[b], OPEN + l * (NACC // 2) + A_BR // 2)
                g2 = gates[:].rearrange("p (b c) t -> p b c t", b=2)
                for q in range(4):
                    nc.scalar.activation(g2[:, :, 2 * q:2 * q + 2], g2[:, :, 2 * q:2 * q + 2],
                                         ACT.Sigmoid).then_inc(gates_ready, 1)
                for q in range(4):
                    for e in range(2):
                        tile_step(l, T_BR + 2 * q + e)
                    act.wait_ge(mix_sum, l * 4 + q + 1)
                    nc.scalar.activation(xT_hi[:, 2 * q:2 * q + 2], mix[:, q % 2, 0].rearrange("p (f t) -> p f t", f=2),
                                         ACT.Identity).then_inc(mix_hi, 1)
                for n in range(T_OUT, T_PQ):
                    tile_step(l, n)
                transposed_hi(X_XT2, 4, xT_part)
                warm_up(ACT.Gelu, l * 2 + 2)
                with act.Fori(0, N_PQ // SLOTS) as i:
                    for e in range(SLOTS):
                        tile_used(l, (i + (T_PQ + e) // SLOTS), (T_PQ + e) % SLOTS)
                        nc.scalar.activation(pqT[:, i * SLOTS + e], acc[:, e % 2, :SEQ],
                                             ACT.Identity).then_inc(acc_read[e % 2], 1)
                        split_hi(l, (i + (T_PQ + e + AHEAD) // SLOTS), (T_PQ + e + AHEAD) % SLOTS)
                for i in range(8):
                    c, p = divmod(i, 2)
                    act.wait_ge(acc_ready, l * NREADY + R_SCR + i + 1)
                    nc.scalar.activation(big[:, S0 + 4 * c:S0 + 4 * c + 4, p * P:(p + 1) * P],
                                         acc[:, p].rearrange("p (u n) -> p u n", u=4),
                                         ACT.Identity).then_inc(acc_read[p], 1)
                def gelu_tile(i, e):
                    n = T_U + e
                    tile_used(l, (i * 2 + n // SLOTS), n % SLOTS)
                    nc.scalar.activation(big[:, i * 8 + e], acc[:, e % 2, :SEQ], ACT.Gelu).then_inc(acc_read[e % 2], 1)

                def after_gelu(i, e):
                    n = T_U + e + AHEAD
                    split_hi(l, (i * 2 + n // SLOTS), n % SLOTS)

                with act.Fori(0, NKEYS // 8 - 1) as i:
                    for e in range(8):
                        gelu_tile(i, e)
                        after_gelu(i, e)
                for e in range(8):
                    gelu_tile(NKEYS // 8 - 1, e)
                    if e < 7:
                        after_gelu(NKEYS // 8 - 1, e)
                act.wait_ge(best_ready, l + 1)
                nc.scalar.activation(picks[:, 2], picks[:, 2], ACT.Exp).then_inc(gate_exp, 1)
                after_gelu(NKEYS // 8 - 1, 7)

                def distances(i, e):
                    act.wait_ge(acc_ready, l * NREADY + (R_G + 1 - HOTS) + (i * HOTS + e))
                    for r in range(4):
                        tok = i * (4 * HOTS) + (4 * e + r)
                        ins = nc.scalar.activation(hot_i[:, e % HOTS, r], iota[:], ACT.Abs,
                                                   bias=picksT[:, 0, bass.ds(tok, 1)], scale=-1.0)
                    ins.then_inc(distance_done, 1)

                def one_hot(i, e):
                    if e % 2 == 1:
                        return
                    act.wait_ge(distance_done, l * NG + (i * HOTS + (e + 1)))
                    nc.scalar.activation(hot_i[:, e], hot_i[:, e], ACT.Relu, bias=ones[:, 0:1],
                                         scale=-1.0).then_inc(hot_i_ready, 1)

                act.wait_ge(tr_read[X_PK % 2], OPEN + l * (NTR // 2) + NTR // 2)
                distances(0, 0)
                with act.Fori(0, NG // HOTS - 1) as i:
                    for e in range(HOTS):
                        distances(i, e + 1)
                        one_hot(i, e)
                for e in range(HOTS):
                    if e + 1 < HOTS:
                        distances(NG // HOTS - 1, e + 1)
                    one_hot(NG // HOTS - 1, e)

                def split_w_hi(j, s):
                    nc.scalar.activation(w_hi[:, s], big[:, j], ACT.Identity).then_inc(w_hi_done, 1)

                for b in range(2):
                    act.wait_ge(acc_read[b], OPEN + l * (NACC // 2) + NACC // 2)
                for j in range(AHEAD):
                    split_w_hi(j, j)
                with act.Fori(0, NKEYS // SLOTS - 1) as i:
                    for e in range(SLOTS):
                        n = T_V + e + AHEAD
                        split_hi(l, (i + n // SLOTS), n % SLOTS)
                        split_w_hi(i * SLOTS + (e + AHEAD), n % SLOTS)
                split_hi(l, TURNS - 1, SLOTS - 1)
                split_w_hi(NKEYS - 1, SLOTS - 1)

        @block.vector
        def _(dve):
            def split_lo(l, q, s):
                dve.wait_ge(hi_done, l * NT + q * SLOTS + s + 1)
                nc.vector.tensor_tensor(lo[:, s], raw[:, s], hi[:, s].bitcast(F32), ALU.subtract).then_inc(lo_done, 1)

            def tile_step(l, n):
                split_lo(l, (n + AHEAD) // SLOTS, (n + AHEAD) % SLOTS)

            def tile_used(l, q, s):
                dve.wait_ge(slot_free[s], OPEN + l * TURNS + q + 1)

            def tr_copy(l, i, dst, src):
                dve.wait_ge(tr_ready, l * NTR + i + 1)
                nc.vector.tensor_copy(dst, src).then_inc(tr_read[i % 2], 1)

            def statistics(tt, chain):
                for c in range(2):
                    chain.link(nc.vector.bn_stats(stats[:, tt, c], xs[:, tt, 512 * c:512 * c + 512]))
                dve.sem_inc(apart, 1)
                chain.link(nc.vector.bn_aggr(mv[:, tt], stats[:, tt].rearrange("p c s -> p (c s)")))

            def normalise(tt, nth, loads, chain, meanwhile=None):
                nc.vector.tensor_scalar(var[:, tt:tt + 1], mv[:, tt, 1:2], LN_EPS, None, ALU.add).then_inc(var_ready, 1)
                dve.wait_ge(ln_loaded, loads)
                chain.link(nc.vector.scalar_tensor_tensor(out=xs[:, tt], in0=xs[:, tt], scalar=mv[:, tt, 0:1],
                                                          in1=ln_par[:, 0], op0=ALU.subtract, op1=ALU.mult))
                if meanwhile is not None:
                    meanwhile()
                dve.wait_ge(rstd_ready, nth + 1)
                nc.vector.scalar_tensor_tensor(out=xs[:, tt], in0=xs[:, tt], scalar=rstd[:, tt:tt + 1],
                                               in1=ln_par[:, 1], op0=ALU.mult, op1=ALU.add).then_inc(x_ready, 1)

            dve.sem_inc(mixed_ready, OPEN)

            tab = Steps(dve, tables_step, 0, 19)
            dve.wait_ge(pos_loaded, 32)
            tab.link(nc.vector.tensor_copy(pos_f[:], pos_i[:]))
            for tt in range(TT):
                tab.link(nc.vector.tensor_scalar(ang[:, 0, tt], freq[:], pos_f[:, tt:tt + 1], None, ALU.mult))
            tab.link(nc.vector.tensor_scalar(ang[:, 1], ang[:, 0], 1.0 / TWO_PI, None, ALU.mult))
            tab.link(nc.vector.tensor_scalar(ang[:, 1], ang[:, 1], ROUND, None, ALU.add))
            tab.link(nc.vector.tensor_scalar(ang[:, 1], ang[:, 1], ROUND, None, ALU.subtract))
            for part in (PI_A, PI_B, PI_C):
                tab.link(nc.vector.scalar_tensor_tensor(out=ang[:, 0], in0=ang[:, 1], scalar=-part, in1=ang[:, 0],
                                                        op0=ALU.mult, op1=ALU.add))
            tab.link(nc.vector.tensor_scalar(ang[:, 0], ang[:, 0], float(np.float32(np.pi)),
                                             -float(np.float32(np.pi)), ALU.min, ALU.max))
            tab.link(nc.vector.scalar_tensor_tensor(out=ang[:, 1], in0=ang[:, 0], scalar=-1.0, in1=ang[:, 0],
                                                    op0=ALU.mult, op1=ALU.max))
            nc.vector.tensor_scalar(ang[:, 1], ang[:, 1], -1.0, float(np.pi / 2), ALU.mult, ALU.add).then_inc(angles_ready, 1)
            chain = Steps(dve, ln_step, 0, TT * 4)
            for tt in range(TT):
                dve.wait_ge(x_loaded[tt], 16)
                statistics(tt, chain)
                normalise(tt, tt, 32, chain)
            chain.end()
            dve.wait_ge(sines_ready, 2)
            R2, H2 = ROPE // 2, HD // 2
            tab.link(nc.vector.tensor_copy(cos_m[:, :, :R2], ang[:, 3, :, :R2]))
            tab.link(nc.vector.tensor_copy(cos_m[:, :, R2:], ang[:, 3, :, :R2]))
            tab.link(nc.vector.tensor_copy(sin_m[:, :, R2:], ang[:, 2, :, :R2]))
            tab.link(nc.vector.tensor_scalar(sin_m[:, :, :R2], ang[:, 2, :, :R2], -1.0, None, ALU.mult))
            tab.link(nc.vector.tensor_copy(cos_n[:, :, :H2], ang[:, 3, :, R2:]))
            tab.link(nc.vector.tensor_copy(cos_n[:, :, H2:], ang[:, 3, :, R2:]))
            tab.link(nc.vector.tensor_copy(sin_n[:, :, H2:], ang[:, 2, :, R2:]))
            tab.link(nc.vector.tensor_scalar(sin_n[:, :, :H2], ang[:, 2, :, R2:], -1.0, None, ALU.mult))
            tab.end()
            dve.wait_ge(consts_ready, 1)
            nc.vector.tensor_copy(ident_b[:], ident[:]).then_inc(whole_ready, 1)
            nc.vector.tensor_scalar(minus_iota[:], iota[:], -1.0, None, ALU.mult).then_inc(whole_ready, 1)
            nc.vector.tensor_scalar(ones_b[:], iota[:], 0.0, 1.0, ALU.mult, ALU.add).then_inc(whole_ready, 1)

            with dve.Fori(0, DEPTH) as l:
                st = Steps(dve, dve_step, l * DVE_STEPS, DVE_STEPS)
                split_lo(l, 0, 0)

                def transposed_lo(first, hi_first, dst_hi, dst_lo):
                    for g in range(4):
                        dve.wait_ge(tr_hi, l * 8 + hi_first + g + 1)
                        nc.vector.tensor_tensor(dst_lo(g), tr[:, (first + g) % 2].rearrange("p (c t) -> p c t", c=4),
                                                dst_hi(g).bitcast(F32), ALU.subtract).then_inc(tr_read[(first + g) % 2], 1)

                def x_part(part):
                    def f(g):
                        tt, cg = divmod(g, 2)
                        return part[:, 4 * cg:4 * cg + 4, tt * P:(tt + 1) * P]
                    return f

                def rotate(dst, src, cos, sin, heads, width, tmp_a, tmp_b, release=None):
                    h = width // 2
                    a = tmp_a[:, :heads * width].rearrange("p (h d) -> p h d", d=width)
                    b = tmp_b[:, :heads * width].rearrange("p (h d) -> p h d", d=width)
                    full = [P, heads, width]
                    half = [P, heads, h]
                    st.link(nc.vector.tensor_tensor(a, src, cos.unsqueeze(1).broadcast_to(full), ALU.mult))
                    st.link(nc.vector.tensor_tensor(b[:, :, :h], src[:, :, h:], sin[:, :h].unsqueeze(1).broadcast_to(half), ALU.mult))
                    st.link(nc.vector.tensor_tensor(b[:, :, h:], src[:, :, :h], sin[:, h:].unsqueeze(1).broadcast_to(half), ALU.mult))
                    if release is not None:
                        release()
                    return nc.vector.tensor_tensor(dst, a, b, ALU.add)

                transposed_lo(X_XT, 0, x_part(xT_hi), x_part(xT_lo))
                split_lo(l, 0, 1)
                split_lo(l, 0, 2)
                dve.wait_ge(small_loaded, l * 48 + 48)
                for c in range(N_LAT):
                    dve.wait_ge(lat_hi, l * N_LAT + c + 1)
                    nc.vector.scalar_tensor_tensor(out=cq_lo[:, c], in0=acc[:, c % 2, :SEQ], scalar=lat_g[:, c:c + 1],
                                                   in1=cq_hi[:, c].bitcast(F32), op0=ALU.mult,
                                                   op1=ALU.subtract).then_inc(acc_read[c % 2], 1)
                    tile_step(l, T_LAT + c)
                dve.wait_ge(acc_ready, l * NREADY + R_RMS + 1)
                nc.vector.tensor_scalar(var[:, 0:TT], acc[:, 0, 0:TT], 1.0 / Q_RANK, RMS_EPS, ALU.mult,
                                        ALU.add).then_inc(acc_read[0], 1)
                dve.wait_ge(acc_ready, l * NREADY + R_RMS + 2)
                st.link(nc.vector.tensor_scalar(var[:, TT:2 * TT], acc[:, 1, 0:TT], 1.0 / KV_RANK, RMS_EPS, ALU.mult, ALU.add))
                nc.vector.tensor_copy(gsum[:, 0:TT], acc[:, 1, 0:TT]).then_inc(acc_read[1], 1)
                nc.vector.tensor_copy(gsum[:, TT:2 * TT], var[:, 0:TT]).then_inc(var_ready, 1)
                for n in range(T_UQ, T_B):
                    tile_step(l, n)
                dve.wait_ge(rstd_ready, 5 * l + R_LAT + 1)
                n = T_B - 1
                tile_used(l, n // SLOTS, n % SLOTS)
                for tt in range(TT):
                    nc.vector.tensor_scalar(q_tok[:, tt].rearrange("p (a h) d -> p a (h d)", a=2),
                                            wide[:, tt].rearrange("p (a c) -> p a c", a=2)[:, :, :384],
                                            rstd[:, tt:tt + 1], MLA_SCALE, ALU.mult, ALU.mult).then_inc(wide_read[tt], 1)
                    tile_step(l, T_B + tt)
                for tt in range(TT):
                    tile_step(l, T_B + 2 + tt)
                n = T_UKV - 1
                tile_used(l, n // SLOTS, n % SLOTS)
                for tt in range(TT):
                    dve.wait_ge(ngate_ready, l * TT + tt + 1)
                    pair = acc[:, tt, :GW].rearrange("p (g d) -> p g d", g=GROUPS)
                    nc.vector.tensor_copy(cmp_tok[:, tt, 1], pair.unsqueeze(2).broadcast_to([P, GROUPS, 2, HD]))
                    nc.vector.tensor_copy(v_sel[:, tt], acc[:, tt, GW:2 * GW])
                    nc.vector.tensor_copy(kr[:, tt], acc[:, tt, 2 * GW:2 * GW + ROPE]).then_inc(acc_read[tt], 1)
                    tile_step(l, T_UKV + tt)
                n = T_MG - 1
                tile_used(l, n // SLOTS, n % SLOTS)
                for tt in range(TT):
                    kv = wide[:, tt].rearrange("p (h d) -> p h d", d=NOPE + VDIM)
                    nc.vector.tensor_scalar(k_tok[:, tt, :, :NOPE], kv[:, :, :NOPE], rstd[:, TT + tt:TT + tt + 1], None, ALU.mult)
                    nc.vector.tensor_scalar(v_mla[:, tt], kv[:, :, NOPE:], rstd[:, TT + tt:TT + tt + 1], None,
                                            ALU.mult).then_inc(wide_read[tt], 1)
                    tile_step(l, T_MG + tt)
                for tt in range(TT):
                    dve.wait_ge(wide_read[tt], OPEN + l * NWIDE + W_UQ + 1)
                    part = q_tok[:, tt, :, NOPE:]
                    st.link(rotate(part, part, cos_m[:, tt], sin_m[:, tt], HEADS, ROPE, rope_a, rope_b))
                    tile_step(l, T_A + 2 * tt)
                    dve.wait_ge(acc_read[tt], OPEN + l * (NACC // 2) + (A_B + tt) // 2 + 1)
                    st.link(rotate(kr[:, tt:tt + 1], kr[:, tt:tt + 1], cos_m[:, tt], sin_m[:, tt], 1, ROPE, rope_a, rope_b))
                    nc.vector.tensor_copy(k_tok[:, tt, :, NOPE:], kr[:, tt:tt + 1].broadcast_to(
                        [P, HEADS, ROPE])).then_inc(qk_ready, 1)
                    tile_step(l, T_A + 2 * tt + 1)
                for n in range(T_A + 4, T_MG2):
                    tile_step(l, n)
                n = T_MG2 - 1
                tile_used(l, n // SLOTS, n % SLOTS)
                for tt in range(TT):
                    def release():
                        nc.vector.tensor_copy(v_win[:, tt], wide[:, tt, ROT * HD:]).then_inc(wide_read[tt], 1)

                    st.link(rotate(rot[:, tt], wide[:, tt, :ROT * HD].rearrange("p (h d) -> p h d", d=HD),
                                   cos_n[:, tt], sin_n[:, tt], ROT, HD, rope_a, rope_b, release))
                    nc.vector.tensor_copy(cmp_tok[:, tt, 0], rot[:, tt, HEADS:HEADS + GROUPS].unsqueeze(2).broadcast_to(
                        [P, GROUPS, 2, HD])).then_inc(tok_ready, 1)
                for c in range(MG_EARLY, 4):
                    tile_step(l, MG_TILE[c])
                for g in range(1, 4, 2):
                    tt, hg = divmod(g, 2)
                    dve.wait_ge(tr_ready, l * NTR + X_NQ + g + 1)
                    nc.vector.tensor_scalar(nqT[:, 4 * hg:4 * hg + 4, tt * P:(tt + 1) * P],
                                            tr[:HD, 1].rearrange("p (h t) -> p h t", h=4), NSA_SCALE, None,
                                            ALU.mult).then_inc(tr_read[1], 1)
                tr_copy(l, X_KT + 1, nkT[:, :, P:], tr[:HD, 1].rearrange("p (h t) -> p h t", h=4))
                tr_copy(l, X_CD + 1, cmpT[:, :, P:], tr[:, 1].rearrange("p (h t) -> p h t", h=4))
                for b in range(2):
                    dve.wait_ge(tr_read[b], OPEN + l * (NTR // 2) + (X_CD + 1) // 2 + 1)
                for c in range(2):
                    for par in range(2):
                        rows = slice(par * HD, par * HD + HD)
                        for g in range(GROUPS):
                            src = bass.AP(cmpT[rows, 2 * c + g].tensor, cmpT[rows, 2 * c + g].offset + par,
                                          [cmpT[rows, 2 * c + g].ap[0], [2, 16], [CMP_STRIDE, NCMP]])
                            ins = nc.vector.tensor_tensor(
                                blk[rows, c, :, g * NCMP:(g + 1) * NCMP], src,
                                pe[rows, c].unsqueeze(2).broadcast_to([HD, 16, NCMP]), ALU.add)
                            ins.then_inc(blk_ready, 1)
                tile_step(l, MG_TILE[4])
                dve.wait_ge(acc_ready, l * NREADY + R_KCVC + 1)
                b = A_KCVC % 2
                st.link(nc.vector.tensor_copy(kc[:], acc[:HD, b, 0:GROUPS * NCMP]))
                nc.vector.tensor_copy(vc[:NCMP], acc[:NCMP, b, 64:64 + GROUPS * HD].rearrange(
                    "p (g d) -> p g d", g=GROUPS)).then_inc(acc_read[b], 1)
                tile_step(l, MG_TILE[5])
                m3 = [P, HEADS, NCMP]
                for tt in range(TT):
                    b = (A_CS + tt) % 2
                    dve.wait_ge(acc_ready, l * NREADY + R_CS + tt + 1)
                    e = cs[:, tt, :, :NCMP]
                    nc.vector.tensor_tensor(
                        e, acc[:, b, :HEADS * 16].rearrange("p (h n) -> p h n", n=16)[:, :, :NCMP],
                        cmask[:, tt].unsqueeze(1).broadcast_to(m3), ALU.add).then_inc(acc_read[b], 1)
                    dve.wait_ge(acc_read[b], OPEN + l * (NACC // 2) + (A_CS + tt) // 2 + 1)
                    st.link(nc.vector.tensor_reduce(cst[:, tt, 0], e, AX.X, ALU.max))
                    nc.vector.tensor_tensor(e, e, cst[:, tt, 0].unsqueeze(2).broadcast_to(m3),
                                            ALU.subtract).then_inc(cmp_shifted, 1)
                tile_step(l, MG_TILE[6])
                for tt in range(TT):
                    e = cs[:, tt, :, :NCMP]
                    dve.wait_ge(cmp_exp, l * TT + tt + 1)
                    st.link(nc.vector.tensor_reduce(cst[:, tt, 1], e, AX.X, ALU.add))
                    st.link(nc.vector.reciprocal(cst[:, tt, 2], cst[:, tt, 1]))
                    g0 = ngate[:, tt].rearrange("p (h b) -> p h b", b=3)[:, :, 0]
                    st.link(nc.vector.tensor_tensor(cst[:, tt, 2], cst[:, tt, 2], g0, ALU.mult))
                    st.link(nc.vector.tensor_tensor(e, e, cmask01[:, tt].unsqueeze(1).broadcast_to(m3), ALU.mult))
                    nc.vector.tensor_tensor(e, e, cst[:, tt, 2].unsqueeze(2).broadcast_to(m3),
                                            ALU.mult).then_inc(cmp_ready, 1)
                tile_step(l, MG_TILE[7])
                for tt in range(TT):
                    tr_copy(l, X_PC + 2 * tt + 1, pcT[:NCMP, 4:8, tt * P:(tt + 1) * P],
                            tr[:NCMP, 1].rearrange("p (h t) -> p h t", h=4))

                def largest(u):
                    keys_n = (unit(u)[2] + 1) * P
                    dve.wait_ge(wide_ready, l * NU + u + 1)
                    nc.vector.tensor_reduce(negmax[:, u % 2], wide[:, u % 2].rearrange("p (h k) -> p h k", h=4)[:, :, :keys_n],
                                            AX.X, ALU.max, negate=True).then_inc(max_ready, 1)

                def weights_out(u):
                    kind, hg, tt, oi, trs = unit(u)
                    dve.wait_ge(exp_ready, l * NU + u + 1)
                    st.link(nc.vector.reciprocal(recip[:, u % 2], sums[:, u % 2]))
                    if kind != "mla":
                        g = ngate[:, tt].rearrange("p (h b) -> p h b", b=3)[:, 4 * hg:4 * hg + 4, 1 if kind == "sel" else 2]
                        st.link(nc.vector.tensor_tensor(recip[:, u % 2], recip[:, u % 2], g, ALU.mult))
                    for h in range(4):
                        s = sc[:, u % 2, h, :(tt + 1) * P]
                        ins = nc.vector.tensor_scalar(s, s, recip[:, u % 2, h:h + 1], None, ALU.mult)
                    ins.then_inc(p_ready, 1)

                def copy_pT(u):
                    for kb, i in enumerate(unit(u)[4]):
                        if i % 2 == 1:
                            tr_copy(l, i, pT[:, u % 2, kb], tr[:, 1])

                def output_lo(oi):
                    tt, i = divmod(oi, 4)
                    bank = O_USE[oi] % 2
                    dve.wait_ge(o_hi, l * 8 + oi + 1)
                    part = (slice(None), i // 2, slice(2 * (i % 2), 2 * (i % 2) + 2), slice(tt * P, (tt + 1) * P))
                    nc.vector.tensor_tensor(oT_lo[part], acc[:, bank, :256].rearrange("p (c t) -> p c t", c=2),
                                            oT_hi[part].bitcast(F32), ALU.subtract).then_inc(acc_read[bank], 1)

                largest(0)
                weights_out(0)
                for u in range(NU):
                    if u + 1 < NU:
                        largest(u + 1)
                    if u + 1 < NU:
                        weights_out(u + 1)
                    copy_pT(u)
                    if u + 8 < N_MG:
                        tile_step(l, MG_TILE[u + 8])
                    if u >= 1 and unit(u - 1)[3] != unit(u)[3]:
                        output_lo(unit(u - 1)[3])
                output_lo(7)
                def mixed_lo(q):
                    dve.wait_ge(mix_hi, l * 4 + q + 1)
                    nc.vector.tensor_tensor(xT_lo[:, 2 * q:2 * q + 2], mix[:, q % 2, 0].rearrange("p (f t) -> p f t", f=2),
                                            xT_hi[:, 2 * q:2 * q + 2].bitcast(F32), ALU.subtract).then_inc(mixed_ready, 1)

                for q in range(4):
                    for e in range(2):
                        n = T_BR + 2 * q + e
                        tile_used(l, n // SLOTS, n % SLOTS)
                        dve.wait_ge(gates_ready, l * 4 + q + 1)
                        if q >= 2:
                            dve.wait_ge(mixed_ready, OPEN + l * 4 + q - 1)
                        nc.vector.tensor_tensor(mix[:, q % 2, e].rearrange("p (f t) -> p f t", f=2),
                                                acc[:, e].rearrange("p (f t) -> p f t", f=2),
                                                gates[:, 8 * e + 2 * q:8 * e + 2 * q + 2], ALU.mult).then_inc(acc_read[e], 1)
                        tile_step(l, n)
                        if e == 0 and q > 0:
                            mixed_lo(q - 1)
                    for e in range(2):
                        dve.wait_ge(acc_read[e], OPEN + l * (NACC // 2) + A_BR // 2 + q + 1)
                    nc.vector.tensor_tensor(mix[:, q % 2, 0], mix[:, q % 2, 0], mix[:, q % 2, 1], ALU.add).then_inc(mix_sum, 1)
                tile_step(l, T_OUT)
                mixed_lo(3)
                for n in range(T_OUT + 1, T_PQ - AHEAD):
                    tile_step(l, n)

                def add_and_norm(nth, last_tile, use, request, loads, meanwhile=None):
                    for tt in range(TT):
                        if tt == 0:
                            dve.wait_ge(half_ready, l * 2 + nth + 1)
                        else:
                            tile_used(l, last_tile // SLOTS, last_tile % SLOTS)
                        nc.vector.scalar_tensor_tensor(out=xs[:, tt], in0=xs[:, tt], scalar=ALPHA, in1=wide[:, tt],
                                                       op0=ALU.mult, op1=ALU.add).then_inc(wide_read[tt], 1)
                        dve.wait_ge(wide_read[tt], OPEN + l * NWIDE + use + 1)
                        statistics(tt, st)
                        normalise(tt, 5 * l + request + tt, loads, st, meanwhile if tt == TT - 1 else None)

                add_and_norm(0, T_PQ - 1, W_OUT, R_LN1, l * 64 + 64, lambda: tile_step(l, T_PQ - AHEAD))
                transposed_lo(X_XT2, 4, x_part(xT_hi), x_part(xT_lo))
                for n in range(T_PQ - AHEAD + 1, T_PQ):
                    tile_step(l, n)
                with dve.Fori(0, N_PQ // SLOTS) as i:
                    for e in range(SLOTS):
                        split_lo(l, (i + (T_PQ + e + AHEAD) // SLOTS), (T_PQ + e + AHEAD) % SLOTS)
                for b in range(2):
                    dve.wait_ge(acc_read[b], OPEN + l * (NACC // 2) + A_U // 2)
                dve.sem_inc(apart, 1)

                def route(i, splits):
                    rt = Steps(dve, route_step, (l * 16 + i) * ROUTE_STEPS, ROUTE_STEPS, apart)

                    kk = [P, TOPK, TOPK]
                    k2 = [P, 2, TOPK, TOPK]
                    unit_places = picks[:, 0:2].rearrange("p a t (h k) -> p a (t h) k", k=TOPK)[:, :, i]
                    unit_gates = picks[:, 2].rearrange("p t (h k) -> p (t h) k", k=TOPK)[:, i]
                    stages = [
                        [lambda: nc.vector.tensor_copy(r_s[:].rearrange("p a n -> p (a n)"), big[:, i + S0])],
                        [lambda p=p: nc.vector.max(r_v[:, p, 0:8], r_s[:, p]) for p in range(2)],
                        [lambda p=p: nc.vector.match_replace(r_s2[:, p], r_v[:, p, 0:8], r_s[:, p], LOWEST) for p in range(2)]
                        + [lambda p=p: nc.vector.max_index(r_i[:, p, 0:8], r_v[:, p, 0:8], r_s[:, p]) for p in range(2)],
                        [lambda p=p: nc.vector.max(r_v[:, p, 8:16], r_s2[:, p]) for p in range(2)],
                        [lambda: nc.vector.tensor_tensor(
                            r_c[:].rearrange("p (a b) -> p a b", a=TOPK), r_v[:, 0].unsqueeze(2).broadcast_to(kk),
                            r_v[:, 1].unsqueeze(1).broadcast_to(kk), ALU.add)]
                        + [lambda p=p: nc.vector.max_index(r_i[:, p, 8:16], r_v[:, p, 8:16], r_s2[:, p]) for p in range(2)],
                        [lambda: nc.vector.max(r_best[:, 0:8], r_c[:]), lambda: nc.vector.tensor_copy(r_if[:], r_i[:])],
                        [lambda: nc.vector.match_replace(r_c2[:], r_best[:, 0:8], r_c[:], LOWEST),
                         lambda: nc.vector.max_index(r_pos[:, 0:8], r_best[:, 0:8], r_c[:])],
                        [lambda: nc.vector.max(r_best[:, 8:16], r_c2[:])],
                        [lambda: nc.vector.max_index(r_pos[:, 8:16], r_best[:, 8:16], r_c2[:]),
                         lambda: nc.vector.tensor_scalar(unit_gates, r_best[:], r_best[:, 0:1], None, ALU.subtract)],
                        [lambda: nc.vector.tensor_scalar(r_ab[:, 0], r_pos[:], 4, None, ALU.logical_shift_right),
                         lambda: nc.vector.tensor_scalar(r_ab[:, 1], r_pos[:], 15, None, ALU.bitwise_and)],
                        [lambda: nc.vector.tensor_copy(r_abf[:], r_ab[:])],
                        [lambda: nc.vector.tensor_tensor(
                            r_eq[:], r_abf[:].unsqueeze(3).broadcast_to(k2),
                            iota[:, :TOPK].unsqueeze(1).unsqueeze(1).broadcast_to(k2), ALU.is_equal)],
                        [lambda: nc.vector.tensor_tensor(
                            r_eq[:], r_eq[:], r_if[:].unsqueeze(2).broadcast_to(k2), ALU.mult)],
                        [lambda: nc.vector.tensor_reduce(unit_places, r_eq[:], AX.X, ALU.add)],
                    ]
                    assert sum(map(len, stages)) == ROUTE_STEPS
                    split_after = [round((len(stages) - 1) * (e + 0.5) / 8) for e in range(8)]
                    for g, stage in enumerate(stages):
                        for ins in stage:
                            rt.mark(ins())
                        for e in range(splits):
                            if split_after[e] == g:
                                after_route(i, e)
                        rt.settle()
                    rt.end()

                def after_route(i, e):
                    n = T_U + e + AHEAD
                    split_lo(l, (i * 2 + n // SLOTS), n % SLOTS)

                with dve.Fori(0, NKEYS // 8 - 1) as i:
                    route(i, 8)
                route(NKEYS // 8 - 1, 8 - AHEAD)

                nc.vector.tensor_copy(gsum[:, 0:1], gsum[:, 0:1]).then_inc(best_ready, 1)
                nc.vector.tensor_copy(places_b[:], picks[:, 1]).then_inc(whole_ready, 1)
                tr_copy(l, X_PK, picksT[:, 0:2], tr[:, X_PK % 2].rearrange("p (k t) -> p k t", k=2))
                after_route(NKEYS // 8 - 1, 5)
                dve.wait_ge(gate_exp, l + 1)
                g = picks[:, 2].rearrange("p t (h k) -> p (t h) k", k=TOPK)
                st.link(nc.vector.tensor_reduce(gsum[:], g, AX.X, ALU.add))
                st.link(nc.vector.reciprocal(gsum[:], gsum[:]))
                nc.vector.tensor_tensor(g, g, gsum[:].unsqueeze(2).broadcast_to([P, TT * HEADS, TOPK]),
                                        ALU.mult).then_inc(picks_ready, 1)
                after_route(NKEYS // 8 - 1, 6)
                tr_copy(l, X_PK + 1, picksT[:, 2], tr[:, (X_PK + 1) % 2, :SEQ])
                for b in range(2):
                    dve.wait_ge(tr_read[b], OPEN + l * (NTR // 2) + NTR // 2)
                dve.sem_inc(apart, 1)

                def gated_rows(i, e):
                    dve.wait_ge(acc_ready, l * NREADY + (R_G + 1 - HOTS) + (i * HOTS + e))
                    dve.wait_ge(apart_j_ready, l * NG + (i * HOTS + (e + 1)))
                    nc.vector.scalar_tensor_tensor(
                        out=hot_j[:, e % HOTS], in0=wide[:, e % HOTS // 2, 512 * (e % 2):512 * (e % 2) + 512].rearrange("p (t j) -> p t j", t=4),
                        scalar=0.0, in1=picksT[:, 2, bass.ds(i * (4 * HOTS) + 4 * e, 4)].unsqueeze(2).broadcast_to([P, 4, P]),
                        op0=ALU.is_equal, op1=ALU.mult).then_inc(hot_j_ready, 1)

                def one_hot(i, e):
                    dve.wait_ge(distance_done, l * NG + (i * HOTS + (e + 1)))
                    nc.vector.tensor_scalar(hot_i[:, e], hot_i[:, e], 0.0, None, ALU.is_equal).then_inc(hot_i_odd, 1)

                def gate_gelu(i, e):
                    dve.wait_ge(acc_ready, l * NREADY + R_G + 1 + (i * HOTS + e))
                    part = big[:, :, bass.ds(i * (4 * HOTS) + 4 * e, 4)].rearrange("p j t -> p t j")
                    nc.vector.tensor_tensor(part, acc[:, e % 2].rearrange("p (t j) -> p t j", t=4), part,
                                            ALU.mult).then_inc(acc_read[e % 2], 1)

                gated_rows(0, 0)
                after_route(NKEYS // 8 - 1, 7)
                gated_rows(0, 1)
                with dve.Fori(0, NG // HOTS - 1) as i:
                    for e in range(HOTS):
                        gated_rows(i, e + 2)
                        if e % 2 == 0:
                            one_hot(i, e + 1)
                        gate_gelu(i, e)
                for e in range(HOTS):
                    if e + 2 < HOTS:
                        gated_rows(NG // HOTS - 1, e + 2)
                    if e % 2 == 0:
                        one_hot(NG // HOTS - 1, e + 1)
                    gate_gelu(NG // HOTS - 1, e)

                def split_w_lo(nth, j, s):
                    dve.wait_ge(w_hi_done, l * NKEYS + nth + 1)
                    nc.vector.tensor_tensor(w_lo[:, s], big[:, j], w_hi[:, s].bitcast(F32), ALU.subtract).then_inc(w_lo_done, 1)

                for b in range(2):
                    dve.wait_ge(acc_read[b], OPEN + l * (NACC // 2) + NACC // 2)
                for j in range(AHEAD):
                    split_w_lo(j, j, j)
                with dve.Fori(0, NKEYS // SLOTS - 1) as i:
                    for e in range(SLOTS):
                        n = T_V + e + AHEAD
                        split_lo(l, (i + n // SLOTS), n % SLOTS)
                        j = i * SLOTS + (e + AHEAD)
                        split_w_lo(j, j, n % SLOTS)
                split_lo(l, TURNS - 1, SLOTS - 1)
                split_w_lo(NKEYS - 1, NKEYS - 1, SLOTS - 1)
                add_and_norm(1, NT - 1, W_V, R_LN2, l * 64 + 96)
                st.end()

        @block.tensor
        def _(pe_):
            mm = nc.tensor.matmul

            def tile_ready(l, q, s):
                pe_.wait_ge(lo_done, l * NT + q * SLOTS + s + 1)

            def acc_free(l, use):
                pe_.wait_ge(acc_read[use % 2], OPEN + l * (NACC // 2) + use // 2)

            def tr_free(l, use):
                pe_.wait_ge(tr_read[use % 2], OPEN + l * (NTR // 2) + use // 2)

            def wide_free(l, use):
                for tt in range(TT):
                    pe_.wait_ge(wide_read[tt], OPEN + l * NWIDE + use)

            def columns_tile(s, xh, xl, bank):
                for k in range(DK):
                    c = slice(k * P, (k + 1) * P)
                    dst = acc[:, bank, :SEQ]
                    mm(dst, lo[:, s, c], xh[:, k], start=k == 0, stop=False)
                    mm(dst, hi[:, s, c], xl[:, k], start=False, stop=False)
                    ins = mm(dst, hi[:, s, c], xh[:, k], start=False, stop=k == DK - 1)
                ins.then_inc(slot_free[s], 1)

            def rows_tile(s, ah, al, first, last, width, offsets, tts=range(TT)):
                for tt in tts:
                    tok = slice(tt * P, (tt + 1) * P)
                    for k, (a, w) in enumerate(((al, hi), (ah, lo), (ah, hi))):
                        for h, off in enumerate(offsets):
                            ins = mm(wide[:, tt, 512 * h:512 * h + width], a[:, tok], w[:, s, off:off + width],
                                     start=first and k == 0, stop=last and k == 2)
                if TT - 1 in tts:
                    ins.then_inc(slot_free[s], 1)
                elif last:
                    ins.then_inc(half_ready, 1)

            for free in (*acc_read, *tr_read, *wide_read):
                pe_.sem_inc(free, OPEN)
            pe_.wait_ge(consts_ready, 1)
            pe_.wait_ge(masks_ready, 2)
            with pe_.Fori(0, DEPTH) as l:
                def transpose_x(first, nth):
                    for g in range(4):
                        tt, cg = divmod(g, 2)
                        pe_.wait_ge(x_ready, nth + tt + 1)
                        tr_free(l, first + g)
                        for c in range(4):
                            ins = nc.tensor.transpose(tr[:, (first + g) % 2, c * P:(c + 1) * P],
                                                      xs[:, tt, (4 * cg + c) * P:(4 * cg + c + 1) * P], ident[:])
                        ins.then_inc(tr_ready, 1)

                def xT_written(first):
                    for b in range(2):
                        pe_.wait_ge(tr_read[b], OPEN + l * (NTR // 2) + first // 2 + 2)

                transpose_x(X_XT, l * 4)
                xT_written(X_XT)
                for c in range(N_LAT):
                    n = T_LAT + c
                    acc_free(l, A_LAT + c)
                    tile_ready(l, n // SLOTS, n % SLOTS)
                    columns_tile(n % SLOTS, xT_hi, xT_lo, c % 2)
                pe_.wait_ge(sq_done, l * N_LAT + N_LAT)
                for b, chunks in enumerate((range(0, 6), range(6, 8))):
                    acc_free(l, A_RMS + b)
                    for tt in range(TT):
                        for c in chunks:
                            ins = mm(acc[:, b, tt:tt + 1], sq[:, c, tt * P:(tt + 1) * P], ones[:, 0:1],
                                     start=c == chunks[0], stop=c == chunks[-1])
                    ins.then_inc(acc_ready, 1)
                def latent_ready(c):
                    pe_.wait_ge(acc_read[c % 2], OPEN + l * (NACC // 2) + (A_LAT + c) // 2 + 1)

                wide_free(l, W_UQ)
                for c in range(N_UQ):
                    n = T_UQ + c
                    latent_ready(c)
                    tile_ready(l, n // SLOTS, n % SLOTS)
                    rows_tile(n % SLOTS, cq_hi[:, c], cq_lo[:, c], c == 0, c == N_UQ - 1, 384, (0, 384))
                for b in range(2):
                    acc_free(l, A_B + b)
                for q in range(N_B):
                    n = T_B + q
                    tile_ready(l, n // SLOTS, n % SLOTS)
                    s = n % SLOTS
                    for kk in range(2):
                        k = 2 * q + kk
                        c = slice(kk * WB, (kk + 1) * WB)
                        for tt in range(TT):
                            tok = slice(tt * P, (tt + 1) * P)
                            dst = acc[:, tt, :WB]
                            mm(dst, xT_lo[:, k, tok], hi[:, s, c], start=k == 0, stop=False)
                            mm(dst, xT_hi[:, k, tok], lo[:, s, c], start=False, stop=False)
                            ins = mm(dst, xT_hi[:, k, tok], hi[:, s, c], start=False, stop=k == DK - 1)
                    ins.then_inc(slot_free[s], 1)
                wide_free(l, W_UKV)
                for c in range(N_UKV):
                    n = T_UKV + c
                    latent_ready(N_UQ + c)
                    tile_ready(l, n // SLOTS, n % SLOTS)
                    rows_tile(n % SLOTS, cq_hi[:, 6 + c], cq_lo[:, 6 + c], c == 0, c == 1, 512, (0, 512))

                def gate_tile(c):
                    n = MG_TILE[c]
                    acc_free(l, MG_USE[c])
                    tile_ready(l, n // SLOTS, n % SLOTS)
                    columns_tile(n % SLOTS, xT_hi, xT_lo, MG_USE[c] % 2)

                for c in range(MG_EARLY):
                    gate_tile(c)
                wide_free(l, W_A)
                for k in range(N_A):
                    n = T_A + k
                    tile_ready(l, n // SLOTS, n % SLOTS)
                    rows_tile(n % SLOTS, xT_hi[:, k], xT_lo[:, k], k == 0, k == N_A - 1, 512, (0, 512))

                def transpose_heads(use, sources, rows):
                    tr_free(l, use)
                    pe_.sem_inc(apart, 1)
                    for j, src in enumerate(sources):
                        ins = nc.tensor.transpose(tr[:rows, use % 2, j * P:(j + 1) * P], src, ident[:])
                    ins.then_inc(tr_ready, 1)

                for c in range(MG_EARLY, 4):
                    gate_tile(c)
                pe_.wait_ge(qk_ready, l * TT + TT)
                for use, src in ((X_Q, q_tok), (X_K, k_tok)):
                    for g in range(4):
                        tt, hg = divmod(g, 2)
                        transpose_heads(use + g, [src[:, tt, 4 * hg + j] for j in range(4)], QKD)
                pe_.wait_ge(tok_ready, l * TT + TT)
                for g in range(4):
                    tt, hg = divmod(g, 2)
                    transpose_heads(X_NQ + g, [rot[:, tt, 4 * hg + j] for j in range(4)], HD)
                for tt in range(TT):
                    transpose_heads(X_KT + tt, [rot[:, tt, HEADS + GROUPS + j] for j in range(4)], HD)
                for tt in range(TT):
                    transpose_heads(X_CD + tt, [cmp_tok[:, tt, c, g].rearrange("p a d -> p (a d)")
                                                for c in range(2) for g in range(GROUPS)], P)
                gate_tile(4)
                pe_.wait_ge(w1_loaded, l * 16 + 16)
                pe_.wait_ge(blk_ready, l * 8 + 8)
                acc_free(l, A_HID)
                nb = GROUPS * NCMP
                for c in range(2):
                    for r in range(16):
                        ins = mm(acc[:, A_HID % 2, c * nb:(c + 1) * nb], w1[:, c, r], blk[:, c, r], start=r == 0, stop=r == 15)
                ins.then_inc(acc_ready, 1)
                gate_tile(5)
                pe_.wait_ge(acc_read[A_HID % 2], OPEN + l * (NACC // 2) + A_HID // 2 + 1)
                acc_free(l, A_KCVC)
                b = A_KCVC % 2
                mm(acc[:HD, b, 0:nb], w2[:, 0], hid[:, 0], start=True, stop=True)
                for g in range(GROUPS):
                    ins = mm(acc[:NCMP, b, 64 + g * HD:64 + (g + 1) * HD], hid[:, 1, g * NCMP:(g + 1) * NCMP], w2[:, 1],
                             start=True, stop=True)
                ins.then_inc(acc_ready, 1)
                pe_.wait_ge(acc_read[b], OPEN + l * (NACC // 2) + A_KCVC // 2 + 1)
                for tt in range(TT):
                    acc_free(l, A_CS + tt)
                    for h in range(HEADS):
                        g = h // 4
                        ins = mm(acc[:, (A_CS + tt) % 2, h * 16:h * 16 + NCMP], nqT[:, h, tt * P:(tt + 1) * P],
                                 kc[:, g * NCMP:(g + 1) * NCMP], start=True, stop=True)
                    ins.then_inc(acc_ready, 1)
                gate_tile(6)
                gate_tile(7)
                for tt in range(TT):
                    pe_.wait_ge(cmp_ready, l * TT + tt + 1)
                    for hg in range(2):
                        transpose_heads(X_PC + 2 * tt + hg, [cs[:, tt, 4 * hg + j, :NCMP] for j in range(4)], NCMP)

                def scores(u):
                    kind, hg, tt, oi, trs = unit(u)
                    keys_n = (tt + 1) * P
                    if u < 2:
                        pe_.wait_ge(wide_read[u], OPEN + l * NWIDE + W_OUT)
                    else:
                        pe_.wait_ge(exp_ready, l * NU + u - 1)
                    tok = slice(tt * P, (tt + 1) * P)
                    banks = wide[:, u % 2].rearrange("p (b h k) -> p b h k", b=2, h=2)
                    for b in range(2):
                        for h in range(2):
                            if kind == "mla":
                                q, k = qT[:QKD, 4 * hg + 2 * b + h, tok], kT[:QKD, 4 * hg + 2 * b + h, :keys_n]
                            else:
                                q = nqT[:, 4 * hg + 2 * b + h, tok]
                                k = nkT[:, (0 if kind == "sel" else GROUPS) + hg, :keys_n]
                            mm(banks[:, b, h, :keys_n], q, k, start=h == 0, stop=False, skip_group_check=True)
                        ins = mm(banks[:, b, :, keys_n - P:keys_n], ident_r[:], causal_r[:].unsqueeze(1).broadcast_to([P, 2, P]),
                                 start=False, stop=True, skip_group_check=True)
                    ins.then_inc(wide_ready, 1)

                def transpose_p(u):
                    kind, hg, tt, oi, trs = unit(u)
                    pe_.wait_ge(p_ready, l * NU + u + 1)
                    for kb, use in enumerate(trs):
                        transpose_heads(use, [sc[:, u % 2, h, kb * P:(kb + 1) * P] for h in range(4)], P)

                def outputs(u):
                    kind, hg, tt, oi, trs = unit(u)
                    bank = O_USE[oi] % 2
                    first = kind != "win"
                    if first:
                        acc_free(l, O_USE[oi])
                    def out(h):
                        return acc[(h % 2) * HD:(h % 2) * HD + HD, bank, (h // 2) * P:(h // 2 + 1) * P]

                    def pairs(x):
                        return [x[:, par::2] for par in range(2)]

                    both = [acc[par * HD:(par + 1) * HD, bank, :256].rearrange("p (c t) -> p c t", c=2) for par in range(2)]
                    if kind == "sel":
                        if hg == 0:
                            for b in range(2):
                                pe_.wait_ge(tr_read[b], OPEN + l * (NTR // 2) + X_PC // 2 + tt + 1)
                        for dst, p in zip(both, pairs(pcT[:NCMP, 4 * hg:4 * hg + 4, tt * P:(tt + 1) * P])):
                            mm(dst, vc[:NCMP, hg], p, start=True, stop=False, skip_group_check=True)
                        first = False
                    for kb, use in enumerate(trs):
                        pe_.wait_ge(tr_read[use % 2], OPEN + l * (NTR // 2) + use // 2 + 1)
                    for kb in range(tt + 1):
                        last = kind != "sel" and kb == tt
                        pt = pT[:, u % 2, kb].rearrange("p (h t) -> p h t", h=4)
                        if kind == "mla":
                            for h in range(4):
                                ins = mm(out(h), v_mla[:, kb, 4 * hg + h], pt[:, h], start=kb == 0 and h < 2, stop=last,
                                         skip_group_check=True)
                        else:
                            v = (v_sel if kind == "sel" else v_win)[:, kb, hg * HD:(hg + 1) * HD]
                            for dst, p in zip(both, pairs(pt)):
                                ins = mm(dst, v, p, start=False, stop=last, skip_group_check=True)
                    if kind != "sel":
                        ins.then_inc(acc_ready, 1)

                scores(0)
                for u in range(NU):
                    if u + 1 < NU:
                        scores(u + 1)
                    if u + 8 < N_MG:
                        gate_tile(u + 8)
                    transpose_p(u)
                    if u >= 1:
                        outputs(u - 1)
                outputs(NU - 1)
                for b in range(2):
                    pe_.wait_ge(acc_read[b], OPEN + l * (NACC // 2) + A_BR // 2)
                for c in range(N_BR):
                    n = T_BR + c
                    s = n % SLOTS
                    acc_free(l, A_BR + c)
                    tile_ready(l, n // SLOTS, s)
                    for f in range(2):
                        for k in range(4):
                            w = slice(k * 256 + f * P, k * 256 + f * P + P)
                            dst = acc[:, c % 2, f * SEQ:(f + 1) * SEQ]
                            mm(dst, lo[:, s, w], oT_hi[:, c % 2, k], start=k == 0, stop=False)
                            mm(dst, hi[:, s, w], oT_lo[:, c % 2, k], start=False, stop=False)
                            ins = mm(dst, hi[:, s, w], oT_hi[:, c % 2, k], start=False, stop=k == 3)
                    ins.then_inc(slot_free[s], 1)
                wide_free(l, W_OUT)
                for k in range(N_OUT - SLOTS):
                    n = T_OUT + k
                    pe_.wait_ge(mixed_ready, OPEN + l * 4 + k // 2 + 1)
                    tile_ready(l, n // SLOTS, n % SLOTS)
                    rows_tile(n % SLOTS, xT_hi[:, k], xT_lo[:, k], k == 0, False, 512, (0, 512))
                for tt in range(TT):
                    for k in range(N_OUT - SLOTS, N_OUT):
                        n = T_OUT + k
                        pe_.wait_ge(mixed_ready, OPEN + l * 4 + k // 2 + 1)
                        tile_ready(l, n // SLOTS, n % SLOTS)
                        rows_tile(n % SLOTS, xT_hi[:, k], xT_lo[:, k], False, k == N_OUT - 1, 512, (0, 512), (tt,))
                transpose_x(X_XT2, l * 4 + 2)
                xT_written(X_XT2)
                pe_.sem_inc(apart, 1)
                with pe_.Fori(0, N_PQ // SLOTS) as i:
                    for e in range(SLOTS):
                        s, q = (T_PQ + e) % SLOTS, (T_PQ + e) // SLOTS
                        pe_.wait_ge(acc_read[e % 2], OPEN + l * (NACC // 2) + (i * 2 + (A_PQ + e) // 2))
                        tile_ready(l, (i + q), s)
                        columns_tile(s, xT_hi, xT_lo, e % 2)
                pe_.wait_ge(keys_loaded, l * 16 + 16)
                for b in range(2):
                    pe_.wait_ge(acc_read[b], OPEN + l * (NACC // 2) + A_SCR // 2)
                for c in range(4):
                    for p in range(2):
                        acc_free(l, A_SCR + 2 * c + p)
                        rows = slice(p * HD, (p + 1) * HD)
                        for r in range(4):
                            tt, h = divmod(4 * c + r, HEADS)
                            ins = mm(acc[:, p, r * P:(r + 1) * P], pqT[rows, h, tt * P:(tt + 1) * P], keys[rows, h],
                                     start=True, stop=True)
                        ins.then_inc(acc_ready, 1)
                with pe_.Fori(0, NKEYS // 8) as i:
                    for e in range(8):
                        s, q = (T_U + e) % SLOTS, (T_U + e) // SLOTS
                        pe_.wait_ge(acc_read[e % 2], OPEN + l * (NACC // 2) + (i * 4 + (A_U + e) // 2))
                        tile_ready(l, (i * 2 + q), s)
                        columns_tile(s, xT_hi, xT_lo, e % 2)
                pe_.wait_ge(best_ready, l + 1)
                transpose_heads(X_PK, [picks[:, a, tt] for a in range(2) for tt in range(TT)], P)
                pe_.wait_ge(picks_ready, l + 1)
                transpose_heads(X_PK + 1, [picks[:, 2, tt] for tt in range(TT)], P)
                pe_.wait_ge(whole_ready, 3 + l + 1)
                for b in range(TT):
                    pe_.wait_ge(wide_read[b], OPEN + l * NWIDE + W_V)

                def apart_j(tt, i, e):
                    dst = wide[:, e // 2, 512 * (e % 2):512 * (e % 2) + 512].rearrange("p (t j) -> p t j", t=4)
                    mm(dst, places_b[:, tt], ident_b[:, bass.ds(i * (4 * HOTS) + 4 * e, 4)].unsqueeze(2).broadcast_to([P, 4, P]),
                       start=True, stop=False)
                    mm(dst, ones_b[0:1], minus_iota[0:1].unsqueeze(1).broadcast_to([1, 4, P]),
                       start=False, stop=True).then_inc(apart_j_ready, 1)

                def gates_of(i, e):
                    pe_.wait_ge(acc_read[e % 2], OPEN + l * (NACC // 2) + (i * 2 + (A_G + e) // 2))
                    if e % 2 == 0:
                        pe_.wait_ge(hot_i_ready, l * (NG // 2) + (i * 2 + (e // 2 + 1)))
                    else:
                        pe_.wait_ge(hot_i_odd, l * (NG // 2) + (i * 2 + (e // 2 + 1)))
                    pe_.wait_ge(hot_j_ready, l * NG + (i * HOTS + (e + 1)))
                    for r in range(4):
                        ins = mm(acc[:, e % 2, r * P:(r + 1) * P], hot_i[:, e, r], hot_j[:, e, r], start=True, stop=True)
                    ins.then_inc(acc_ready, 1)

                def step(i, nxt):
                    for e in range(HOTS):
                        gates_of(i, e)
                        if nxt is not None:
                            apart_j(*nxt, e)

                half = NG // HOTS // TT
                for e in range(HOTS):
                    apart_j(0, 0, e)
                with pe_.Fori(0, half - 1) as i:
                    step(i, (0, i + 1))
                step(half - 1, (1, 0))
                with pe_.Fori(half, 2 * half - 1) as i:
                    step(i, (1, i - (half - 1)))
                step(2 * half - 1, None)
                wide_free(l, W_V)
                pe_.sem_inc(apart, 1)

                def v_tile(i, e, first, last, tts=range(TT)):
                    s, q = (T_V + e) % SLOTS, (T_V + e) // SLOTS
                    pe_.wait_ge(w_lo_done, l * NKEYS + (i * SLOTS + (e + 1)))
                    tile_ready(l, (i + q), s)
                    rows_tile(s, w_hi[:, s], w_lo[:, s], first, last, 512, (0, 512), tts)

                for e in range(SLOTS):
                    v_tile(0, e, e == 0, False)
                with pe_.Fori(1, NKEYS // SLOTS - 1) as i:
                    for e in range(SLOTS):
                        v_tile(i, e, False, False)
                for tt in range(TT):
                    for e in range(SLOTS):
                        v_tile(NKEYS // SLOTS - 1, e, False, e == SLOTS - 1, (tt,))


DVE_STEPS = 74
ROUTE_STEPS = 25


def lay_out(a):
    L = DEPTH
    w_in = a["w_in"]

    def columns(w, first, width=P):
        part = w[:, first:first + width]
        return part.reshape(-1, P, width).transpose(1, 0, 2).reshape(P, -1)

    front = np.zeros((L, FRONT, P, 1024), np.float32)
    for l in range(L):
        w = w_in[l]
        wa = np.concatenate([w[:, c:c + n] for c, n in COLS_A], axis=1)
        wb = np.concatenate([w[:, c:c + n] for c, n in COLS_B], axis=1)
        for c in range(N_LAT):
            front[l, T_LAT + c] = columns(w, c * P)
        for c in range(N_UQ):
            front[l, T_UQ + c, :, :HEADS * QKD] = a["mla_w_uq"][l, c * P:(c + 1) * P]
        for c in range(N_UKV):
            front[l, T_UKV + c] = a["mla_w_ukv"][l, c * P:(c + 1) * P]
        for q in range(N_B):
            front[l, T_B + q, :, :2 * WB] = columns(wb[q * 2 * P:(q + 1) * 2 * P], 0, WB)
        for k in range(N_A):
            front[l, T_A + k] = wa[k * P:(k + 1) * P]
        for c in range(N_MG):
            front[l, MG_TILE[c]] = columns(w, C_MG + c * P)
        for q in range(4):
            front[l, T_BR + 2 * q] = columns(a["w_branch_mla"][l], q * 256, 256)
            front[l, T_BR + 2 * q + 1] = columns(a["w_branch_nsa"][l], q * 256, 256)
        for k in range(N_OUT):
            front[l, T_OUT + k] = a["w_out"][l, k * P:(k + 1) * P]
        for h in range(N_PQ):
            front[l, T_PQ + h] = columns(a["peer_w_query"][l], h * P)

    def odd_even(x, width):
        return x.reshape(L, 16, 2, HD, width).transpose(0, 2, 3, 1, 4).reshape(L, P, 16, width)

    got = {
        "x": a["x"].reshape(TT, P, D).transpose(1, 0, 2),
        "positions": a["positions"].reshape(TT, P).T,
        "freq": np.concatenate([10000.0 ** (-np.arange(0, d, 2, dtype=np.float64) / d) for d in (ROPE, HD)]).astype(np.float32),
        "ln": np.stack([np.stack([a["ln_in_g"], a["ln_in_b"]])] + [
            np.stack([a[f"ln{i}_g"][l], a[f"ln{i}_b"][l]]) for l in range(L) for i in (1, 2)]),
        "front": front,
        "lat_g": np.concatenate([a["mla_q_norm"], a["mla_kv_norm"]], axis=1).reshape(L, 8, P).transpose(0, 2, 1),
        "cmp_pe": np.stack([odd_even(a["nsa_cmp_k_pe"], 1)[..., 0], odd_even(a["nsa_cmp_v_pe"], 1)[..., 0]], axis=2),
        "cmp_w1": np.stack([odd_even(a["nsa_cmp_k_w1"], P), odd_even(a["nsa_cmp_v_w1"], P)], axis=2),
        "cmp_w2": np.stack([a["nsa_cmp_k_w2"], a["nsa_cmp_v_w2"]], axis=2),
        "sub_keys": a["peer_sub_keys"].transpose(0, 2, 4, 1, 3).reshape(L, P, HEADS, NKEYS),
        "peer_u": a["peer_u"].reshape(L, P, NKEYS, DK, P).transpose(0, 2, 4, 3, 1).reshape(L, NKEYS, P, 1024),
        "peer_v": a["peer_v"].reshape(L, P, NKEYS, D).transpose(0, 2, 1, 3),
    }
    got["positions"] = got["positions"].astype(np.int32)
    return {k: np.ascontiguousarray(v) for k, v in got.items()}


def kernel(**inputs):
    import concourse.bacc as bacc
    from concourse.bass_utils import run_bass_kernel_spmd

    arrays = lay_out({k: np.asarray(v) for k, v in inputs.items()})
    nc = bacc.Bacc("TRN2", target_bir_lowering=False, num_devices=1)
    t = {k: nc.dram_tensor(f"in_{k}", v.shape, mybir.dt.from_np(v.dtype), kind="ExternalInput").ap()
         for k, v in arrays.items()}
    out = nc.dram_tensor("out_0", (P, TT, D), F32, kind="ExternalOutput").ap()
    build(nc, t, out)
    r = run_bass_kernel_spmd(nc, [{f"in_{k}": v for k, v in arrays.items()}], core_ids=[0])
    return r.results[0]["out_0"].transpose(1, 0, 2).reshape(1, SEQ, D)
```
